# Optimizing a Trainium2 kernel written in Bass

```python
import math
import jax, jax.numpy as jnp
from jax import lax
import numpy as np

D_MODEL = 1024
BATCH = 1
SEQ = 256
DEPTH = 2

N_MIXERS = 2
N_DIFF = (DEPTH + 1) // 2
N_RET = DEPTH // 2

DA_HEADS = 8
DA_HEAD_DIM = 64
DA_V_DIM = 2 * DA_HEAD_DIM
Q_BLOCK = 128
RET_HEADS = 4
RET_DK = 256
RET_DV = 512
RET_CHUNK = 128
N_EXPERTS = 64
TOP_K = 8
N_GROUPS = 8
TOPK_GROUPS = 4
EXPERT_FF = 256
SHARED_FF = 256
ROUTED_SCALE = 2.5
DISPATCH_BLOCK = 128
EPS = 1e-6

kernel_name = "hybrid_diffattn_retnet_moe_adaln"

def rmsnorm(x, g):
    xf = x.astype(jnp.float32)
    y = xf * lax.rsqrt(jnp.mean(xf * xf, axis=-1, keepdims=True) + EPS)
    return (y * g.astype(jnp.float32)).astype(x.dtype)

def alibi_slopes(n_heads):
    return 2.0 ** (-8.0 * jnp.arange(1, n_heads + 1, dtype=jnp.float32) / n_heads)

def diff_attention(xn, w_in, w_out, lq1, lk1, lq2, lk2, subln_g, layer_idx):
    B, S, _ = xn.shape
    H, dh, dv = DA_HEADS, DA_HEAD_DIM, DA_V_DIM
    proj = xn @ w_in
    q, k, v = jnp.split(proj, [2 * H * dh, 4 * H * dh], axis=-1)
    q = q.reshape(B, S, 2 * H, dh).transpose(0, 2, 1, 3) * (dh ** -0.5)
    k = k.reshape(B, S, 2 * H, dh).transpose(0, 2, 1, 3)
    v = v.reshape(B, S, H, dv).transpose(0, 2, 1, 3)
    lam_init = 0.8 - 0.6 * math.exp(-0.3 * layer_idx)
    lam = (jnp.exp(jnp.sum(lq1.astype(jnp.float32) * lk1.astype(jnp.float32)))
           - jnp.exp(jnp.sum(lq2.astype(jnp.float32) * lk2.astype(jnp.float32))) + lam_init)
    slopes2 = jnp.repeat(alibi_slopes(H), 2)
    n_blk = S // Q_BLOCK
    q_blocks = q.reshape(B, 2 * H, n_blk, Q_BLOCK, dh).transpose(2, 0, 1, 3, 4)
    kpos = jnp.arange(S)

    def one_block(args):
        qb, b_idx = args
        qpos = b_idx * Q_BLOCK + jnp.arange(Q_BLOCK)
        dist = (qpos[:, None] - kpos[None, :]).astype(jnp.float32)
        s = jnp.einsum('bhqd,bhkd->bhqk', qb, k).astype(jnp.float32) - slopes2[:, None, None] * dist
        s = jnp.where(dist >= 0, s, -jnp.inf)
        p = jax.nn.softmax(s, axis=-1).reshape(B, H, 2, Q_BLOCK, S)
        a = p[:, :, 0] - lam * p[:, :, 1]
        return jnp.einsum('bhqk,bhkv->bhqv', a.astype(v.dtype), v)

    o = lax.map(one_block, (q_blocks, jnp.arange(n_blk)))
    o = o.transpose(1, 0, 3, 2, 4).reshape(B, S, H, dv)
    o = rmsnorm(o, subln_g) * (1.0 - lam_init)
    return o.reshape(B, S, H * dv) @ w_out

def retention(xn, w_in, w_out, gn_g):
    B, S, _ = xn.shape
    H, dk, dv, C = RET_HEADS, RET_DK, RET_DV, RET_CHUNK
    n_c = S // C
    proj = (xn @ w_in).astype(jnp.float32)
    q, k, v, g = jnp.split(proj, [H * dk, 2 * H * dk, 2 * H * dk + H * dv], axis=-1)
    q = q.reshape(B, n_c, C, H, dk).transpose(1, 0, 3, 2, 4)
    k = k.reshape(B, n_c, C, H, dk).transpose(1, 0, 3, 2, 4) * (dk ** -0.5)
    v = v.reshape(B, n_c, C, H, dv).transpose(1, 0, 3, 2, 4)
    log_g = jnp.log1p(-(2.0 ** (-5.0 - jnp.arange(H, dtype=jnp.float32))))
    idx = jnp.arange(C, dtype=jnp.float32)
    diff = idx[:, None] - idx[None, :]
    decay = jnp.where(diff >= 0, jnp.exp(log_g[:, None, None] * jnp.maximum(diff, 0.0)), 0.0)
    zeta = jnp.exp(log_g[:, None] * (C - 1 - idx))
    xi = jnp.exp(log_g[:, None] * (idx + 1))
    g_c = jnp.exp(log_g * C)

    def step(R, inp):
        qc, kc, vc = inp
        inner = jnp.einsum('bhid,bhjd->bhij', qc, kc) * decay
        o = (jnp.einsum('bhij,bhjv->bhiv', inner, vc)
             + jnp.einsum('bhid,bhdv->bhiv', qc, R) * xi[:, :, None])
        R = g_c[:, None, None] * R + jnp.einsum('bhjd,bhjv->bhdv', kc * zeta[:, :, None], vc)
        return R, o

    R0 = jnp.zeros((B, H, dk, dv), jnp.float32)
    _, o = lax.scan(step, R0, (q, k, v))
    o = o.transpose(1, 0, 3, 2, 4).reshape(B, S, H, dv)
    o = rmsnorm(o, gn_g.reshape(H, dv))
    y = jax.nn.silu(g) * o.reshape(B, S, H * dv)
    return y.astype(xn.dtype) @ w_out

def moe(xm, router_w, router_b, w1, w3, w2, s_w1, s_w3, s_w2):
    B, S, D = xm.shape
    T = B * S
    E, K, BLK = N_EXPERTS, TOP_K, DISPATCH_BLOCK
    xt = xm.reshape(T, D)
    scores = jax.nn.sigmoid((xt @ router_w).astype(jnp.float32))
    choice = scores + router_b.astype(jnp.float32)
    grp = choice.reshape(T, N_GROUPS, E // N_GROUPS)
    grp_score = lax.top_k(grp, 2)[0].sum(-1)
    _, grp_idx = lax.top_k(grp_score, TOPK_GROUPS)
    grp_mask = jax.nn.one_hot(grp_idx, N_GROUPS, dtype=jnp.float32).sum(1) > 0
    choice = jnp.where(jnp.repeat(grp_mask, E // N_GROUPS, axis=1), choice, -jnp.inf)
    _, top_idx = lax.top_k(choice, K)
    top_w = jnp.take_along_axis(scores, top_idx, axis=1)
    top_w = top_w / jnp.sum(top_w, axis=-1, keepdims=True) * ROUTED_SCALE

    A = T * K
    flat_e = top_idx.reshape(A).astype(jnp.int32)
    flat_tok = jnp.arange(A, dtype=jnp.int32) // K
    flat_w = top_w.reshape(A)
    order = jnp.argsort(flat_e)
    e_s, tok_s, w_s = flat_e[order], flat_tok[order], flat_w[order]
    counts = jnp.bincount(flat_e, length=E).astype(jnp.int32)
    starts = jnp.cumsum(counts) - counts
    pad_counts = (counts + BLK - 1) // BLK * BLK
    pad_ends = jnp.cumsum(pad_counts)
    pad_starts = pad_ends - pad_counts
    dest = pad_starts[e_s] + jnp.arange(A, dtype=jnp.int32) - starts[e_s]
    n_blocks = -(-A // BLK) + E
    P = n_blocks * BLK
    buf_tok = jnp.full((P,), T, jnp.int32).at[dest].set(tok_s)
    buf_w = jnp.zeros((P,), jnp.float32).at[dest].set(w_s)
    blk_e = jnp.minimum(jnp.searchsorted(pad_ends, jnp.arange(n_blocks, dtype=jnp.int32) * BLK,
                                         side='right'), E - 1)
    x_pad = jnp.concatenate([xt, jnp.zeros((1, D), xt.dtype)], axis=0)

    def blk_step(acc, inp):
        tok, wgt, e = inp
        xb = x_pad[tok]
        h = jax.nn.silu(xb @ w1[e]) * (xb @ w3[e])
        yb = (h @ w2[e]) * wgt[:, None].astype(xb.dtype)
        return acc.at[tok].add(yb), None

    acc0 = jnp.zeros((T + 1, D), xt.dtype)
    acc, _ = lax.scan(blk_step, acc0,
                      (buf_tok.reshape(n_blocks, BLK), buf_w.reshape(n_blocks, BLK), blk_e))
    shared = (jax.nn.silu(xt @ s_w1) * (xt @ s_w3)) @ s_w2
    return (acc[:T] + shared).reshape(B, S, D)

def setup_inputs(seed: int = 0) -> dict:
    key = jax.random.key(seed)
    ks = jax.random.split(key, 25)
    D, F, SF, E = D_MODEL, EXPERT_FF, SHARED_FF, N_EXPERTS
    nrm = lambda k, shape, s: jax.random.normal(k, shape, jnp.float32) * s
    gain = lambda k, shape: 1.0 + 0.02 * jax.random.normal(k, shape, jnp.float32)
    ret_in = 2 * RET_HEADS * RET_DK + 2 * RET_HEADS * RET_DV
    return {
        "x": nrm(ks[0], (BATCH, SEQ, D), 1.0),
        "c": nrm(ks[1], (BATCH, D), 1.0),
        "norm_mix": gain(ks[2], (DEPTH, D)),
        "norm_ffn": gain(ks[3], (DEPTH, D)),
        "ada_w": nrm(ks[4], (DEPTH, D, 6 * D), 0.5 * D ** -0.5),
        "ada_b": nrm(ks[5], (DEPTH, 6 * D), 0.02),
        "da_w_in": nrm(ks[6], (N_DIFF, D, 6 * DA_HEADS * DA_HEAD_DIM), D ** -0.5),
        "da_w_out": nrm(ks[7], (N_DIFF, DA_HEADS * DA_V_DIM, D), (DA_HEADS * DA_V_DIM) ** -0.5),
        "da_lq1": nrm(ks[8], (N_DIFF, DA_HEAD_DIM), 0.1),
        "da_lk1": nrm(ks[9], (N_DIFF, DA_HEAD_DIM), 0.1),
        "da_lq2": nrm(ks[10], (N_DIFF, DA_HEAD_DIM), 0.1),
        "da_lk2": nrm(ks[11], (N_DIFF, DA_HEAD_DIM), 0.1),
        "da_subln": gain(ks[12], (N_DIFF, DA_V_DIM)),
        "ret_w_in": nrm(ks[13], (N_RET, D, ret_in), D ** -0.5),
        "ret_w_out": nrm(ks[14], (N_RET, RET_HEADS * RET_DV, D), (RET_HEADS * RET_DV) ** -0.5),
        "ret_gn": gain(ks[15], (N_RET, RET_HEADS * RET_DV)),
        "router_w": nrm(ks[16], (DEPTH, D, E), D ** -0.5),
        "router_b": nrm(ks[17], (DEPTH, E), 0.01),
        "exp_w1": nrm(ks[18], (DEPTH, E, D, F), D ** -0.5),
        "exp_w3": nrm(ks[19], (DEPTH, E, D, F), D ** -0.5),
        "exp_w2": nrm(ks[20], (DEPTH, E, F, D), F ** -0.5),
        "sh_w1": nrm(ks[21], (DEPTH, D, SF), D ** -0.5),
        "sh_w3": nrm(ks[22], (DEPTH, D, SF), D ** -0.5),
        "sh_w2": nrm(ks[23], (DEPTH, SF, D), SF ** -0.5),
        "final_norm": gain(ks[24], (D,)),
    }

def reference(x, c, norm_mix, norm_ffn, ada_w, ada_b, da_w_in, da_w_out, da_lq1, da_lk1,
              da_lq2, da_lk2, da_subln, ret_w_in, ret_w_out, ret_gn, router_w, router_b,
              exp_w1, exp_w3, exp_w2, sh_w1, sh_w3, sh_w2, final_norm):
    for i in range(DEPTH):
        mod = jax.nn.silu(c) @ ada_w[i] + ada_b[i]
        sh_a, sc_a, g_a, sh_f, sc_f, g_f = jnp.split(mod[:, None, :], 6, axis=-1)
        h = rmsnorm(x, norm_mix[i]) * (1.0 + sc_a) + sh_a
        j = i // N_MIXERS
        if i % N_MIXERS == 0:
            y = diff_attention(h, da_w_in[j], da_w_out[j], da_lq1[j], da_lk1[j],
                               da_lq2[j], da_lk2[j], da_subln[j], i)
        else:
            y = retention(h, ret_w_in[j], ret_w_out[j], ret_gn[j])
        x = x + g_a * y
        h = rmsnorm(x, norm_ffn[i]) * (1.0 + sc_f) + sh_f
        x = x + g_f * moe(h, router_w[i], router_b[i], exp_w1[i], exp_w3[i], exp_w2[i],
                          sh_w1[i], sh_w3[i], sh_w2[i])
    return rmsnorm(x, final_norm)


_drawn_inputs = setup_inputs


def setup_inputs(seed=0):
    import zlib

    import numpy as np

    out = dict(_drawn_inputs(seed))
    spreads = {}
    factors = {'da_lk1': 4.382, 'da_lq2': 4.776, 'ret_gn': 6.727, 'final_norm': 2.847}
    for name, (base, spread) in spreads.items():
        noise = np.random.default_rng([zlib.crc32(name.encode()), seed]).standard_normal(out[name].shape)
        drawn = base * np.exp(spread * noise) if base else spread * noise
        out[name] = __import__('jax').numpy.asarray(drawn.astype(out[name].dtype))
    for name, factor in factors.items():
        out[name] = (out[name] * factor).astype(out[name].dtype)
    return out
```

```python
import math
from contextlib import ExitStack

import concourse.bass as bass
from concourse import mybir

F32 = mybir.dt.float32
BF16 = mybir.dt.bfloat16
I32 = mybir.dt.int32
ALU = mybir.AluOpType
ACT = mybir.ActivationFunctionType
AX_X = mybir.AxisListType.X

P = 128
EPS = 1e-6
RING = 12
TW = 2048
SLOTS = 64
DA_HEADS, DA_DH = 8, 64
RET_HEADS, RET_DK = 4, 256
GROUPS, TOPG, TOPK = 8, 4, 8
ROUTED_SCALE = 2.5
FAR = 1e30


def plan_stream():
    order = [("ada", 0, i) for i in range(24)]
    for s in range(6):
        order += [("mix_in", 0, 2 * s), ("mix_in", 0, 2 * s + 1)]
        order += [("ada", 1, 4 * s + q) for q in range(4)]
    order += [("mix_out", 0, i) for i in range(4)]
    order += [("shared", 0, i) for i in range(3)] + [("pad",)] * 2
    moe = {0: len(order)}
    order += [("expert", 0, i) for i in range(192)]
    order += [("mix_in", 1, i) for i in range(24)] + [("mix_out", 1, i) for i in range(8)]
    order += [("shared", 1, i) for i in range(3)] + [("pad",)]
    moe[1] = len(order)
    order += [("expert", 1, i) for i in range(192)]
    return order, moe


def trunk(nc, x, c, norm_mix, norm_ffn, ada_w, ada_b, da_w_in, da_w_out, da_lq1, da_lk1, da_lq2, da_lk2,
          da_subln, ret_w_in, ret_w_out, ret_gn, router_w, router_b, exp_w1, exp_w3, exp_w2,
          sh_w1, sh_w3, sh_w2, final_norm, out):
    _, T, D = x.shape
    TC, KD = T // P, D // P
    E = router_w.shape[2]
    PAIRS = E // 2
    NH = D // 512
    LAM_INIT = 0.8 - 0.6 * math.exp(-0.3 * 0)
    DEPTH = 2
    DA_ITEMS = 2 * DA_HEADS

    order, MOE0 = plan_stream()
    where = {key: n for n, key in enumerate(order) if key[0] != "pad"}
    loads = [sum(1 for m in range(n % RING, n + 1, RING) if order[m][0] != "pad") for n in range(len(order))]
    assert all(MOE0[l] % 3 == 0 for l in range(DEPTH))

    with ExitStack() as ctx:
        def sb(name, shape, dt=F32):
            return ctx.enter_context(nc.sbuf_tensor(name, shape, dt))

        def sem(name):
            return ctx.enter_context(nc.semaphore(name))

        ring = sb("ring", [P, RING * TW])
        X = sb("X", [P, TC, D])
        HH = sb("HH", [P, 2 * TC * D])
        h = HH[:, 0:TC * D].rearrange("p (c d) -> p c d", c=TC)
        hT = HH[:, TC * D:].rearrange("p (k t) -> p k t", k=KD)
        mods = sb("mods", [P, 6, D])
        arena = sb("arena", [P, 12288])

        ident = sb("ident", [P, P])
        upper = sb("upper", [P, P], BF16)
        ones = sb("ones", [P, P], BF16)
        ident16 = sb("ident16", [P, P], BF16)
        dist = sb("dist", [P, T])
        slot_no = sb("slot_no", [P, SLOTS])
        pass_base = sb("pass_base", [P, 4, 4])
        before = sb("before", [P, GROUPS, GROUPS])
        cT = sb("cT", [P, KD])
        cs = sb("cs", [P, KD])
        cb = sb("cb", [P, KD, 32])
        lsum = sb("lsum", [P, 2])
        lexp = sb("lexp", [P, 2])
        nlam = sb("nlam", [P, 1])
        subg = sb("subg", [P, 1])
        subs = sb("subs", [P, 1])
        gn = sb("gn", [P, 16])
        rw = sb("rw", [P, DEPTH, KD, E])
        rb = sb("rb", [P, DEPTH, E])
        soft = sb("soft", [P, 3, 2 * DA_HEADS, 2])
        decay = sb("decay", [P, RET_HEADS, T])
        ret_s = sb("ret_s", [P, T + P])
        ss = sb("ss", [P, 16])
        rs = sb("rs", [P, 16])

        banks = [ctx.enter_context(nc.psum_tensor(f"bank{i}", [P, 512], F32)) for i in range(8)]
        mod_dram = nc.dram_tensor("mod_dram", [DEPTH, 6, D], F32, kind="Internal").ap()

        mrow = arena[:, 6144:7680].rearrange("p (s n) -> p s n", s=6)
        brow = arena[:, 7680:9216].rearrange("p (s n) -> p s n", s=6)
        nrow = arena[:, 9216:9728].rearrange("p (i n) -> p i n", i=2)
        lvec = arena[:, 9728:9984].rearrange("p (i n) -> p i n", i=4)
        lprod = arena[:, 9984:10112].rearrange("p (i n) -> p i n", i=2)
        qT = arena[:, 0:2048].rearrange("p (k t) -> p k t", k=8)
        kT = arena[:, 2048:4096].rearrange("p (k t) -> p k t", k=8)
        da_v = arena[:, 4096:6144].rearrange("p (c d) -> p c d", c=TC)
        da_o = arena[:, 6144:8192].rearrange("p (c h d) -> p c h d", c=TC, h=DA_HEADS)
        da_oT = arena[:, 8192:10240].rearrange("p (h t) -> p h t", h=DA_HEADS)
        da_s = arena[:, 10240:11264].rearrange("p (b m k) -> p b m k", b=2, m=2)
        da_a = arena[:, 11264:11776].rearrange("p (b k) -> p b k", b=2)
        da_aT = arena[:, 11776:12288].rearrange("p (b k q) -> p b k q", b=2, k=2)
        ret_v = arena[:, 4096:8192].rearrange("p (c d) -> p c d", c=TC)
        ret_sg = arena[:, 8192:12288].rearrange("p (c t) -> p c t", c=16)
        ret_yT = arena[:, 0:4096].rearrange("p (c t) -> p c t", c=16)
        ret_o = HH[:, :].rearrange("p (c h d) -> p c h d", c=TC, h=RET_HEADS)
        da_sq = arena[:, 0:2048].rearrange("p (c h d) -> p c h d", c=TC, h=DA_HEADS)
        ret_junk = cb.rearrange("p k m -> p (k m)").bitcast(BF16)
        parts = arena[:, 0:3072].bitcast(BF16).rearrange("p (c r d) -> p c r d", c=TC, r=3)
        xg = arena[:, 3072:4096].rearrange("p (k n) -> p k n", k=KD)
        y = arena[:, 4096:5632].bitcast(BF16).rearrange("p (r d) -> p r d", r=3)
        S = arena[:, 5632:5760].bitcast(BF16)
        sg = arena[:, 5760:6272]
        eh = arena[:, 6272:6528].rearrange("p (b n) -> p b n", b=2)
        ehT = arena[:, 6528:6784].rearrange("p (b n) -> p b n", b=2)
        y_rest = arena[:, 8736:9760].rearrange("p (f n) -> p f n", f=NH)
        Pg = arena[:, 9760:9888].bitcast(BF16).rearrange("p (c n) -> p c n", c=TC)
        wparts = arena[:, 9888:10080].bitcast(BF16).rearrange("p (c e r) -> p c e r", c=TC, r=3)
        wrest = arena[:, 10080:10208].rearrange("p (c e) -> p c e", c=TC)
        w_slot = arena[:, 10208:10209]
        shT = arena[:, 6784:7296].rearrange("p (b t) -> p b t", b=2)
        score = arena[:, 7296:7424].rearrange("p (c e) -> p c e", c=TC)
        choice = arena[:, 7424:7552].rearrange("p (c e) -> p c e", c=TC)
        masked = arena[:, 7552:7680].rearrange("p (c e) -> p c e", c=TC)
        chosen = arena[:, 7680:7808].rearrange("p (c e) -> p c e", c=TC)
        top = arena[:, 7808:7936].rearrange("p (g m) -> p g m", m=8)
        gs = arena[:, 7936:7952].rearrange("p (c g) -> p c g", c=TC)
        cmp1 = arena[:, 7952:8080].rearrange("p (c g m) -> p c g m", c=TC, g=GROUPS)
        cmp2 = arena[:, 8080:8208].rearrange("p (c g m) -> p c g m", c=TC, g=GROUPS)
        grank = arena[:, 8208:8224].rearrange("p (c g) -> p c g", c=TC)
        top8 = arena[:, 8224:8240].rearrange("p (c m) -> p c m", c=TC)
        wsum = arena[:, 8240:8242]
        winv = arena[:, 8242:8244]
        mb = arena[:, 8244:8308].bitcast(BF16).rearrange("p (c e) -> p c e", c=TC)
        rank = arena[:, 8308:8436].rearrange("p (e c) -> p e c", c=TC)
        weight = arena[:, 8436:8564].rearrange("p (c e) -> p c e", c=TC)
        cnt = arena[0:1, 8564:8628]
        cmax = arena[0:1, 8628:8660]
        npf = arena[0:1, 8660:8692]
        npass = arena[0:1, 8692:8724].bitcast(I32)
        rk = arena[:, 8724:8728]

        landed = [sem(f"landed{i}") for i in range(RING)]
        tiles_used = sem("tiles_used")
        c_in, consts_in, x_in, rows_in = sem("c_in"), sem("consts_in"), sem("x_in"), [sem("rows_in0"), sem("rows_in1")]
        pool_consts, pool_step = sem("pool_consts"), sem("pool_step")
        rows_zero = sem("rows_zero")
        c_silu, cb_ready = sem("c_silu"), sem("cb_ready")
        ada_done = [sem(f"ada_done{l}") for l in range(DEPTH)]
        rows_ready = [sem(f"rows_ready{l}") for l in range(DEPTH)]
        rows_stored = sem("rows_stored")
        mix_mods, moe_mods, last_gain = sem("mix_mods"), sem("moe_mods"), sem("last_gain")
        sumsq, meansq, root, h_ready, h_turned, hT_ready = (
            sem(n) for n in ("sumsq", "meansq", "root", "h_ready", "h_turned", "hT_ready"))
        proj_done, proj_out = sem("proj_done"), sem("proj_out")
        scored, s_ready, exp_done, a_ready, a_turned, aT_ready, pv_done, o_ready = (
            sem(n) for n in ("scored", "s_ready", "exp_done", "a_ready", "a_turned", "aT_ready", "pv_done", "o_ready"))
        o_meansq, o_root, o_normed, o_turned, oT_ready = (
            sem(n) for n in ("o_meansq", "o_root", "o_normed", "o_turned", "oT_ready"))
        o_sumsq = sem("o_sumsq")
        lam_sums, lam_exp = sem("lam_sums"), sem("lam_exp")
        decay_arg, decay_exp, decay_ready = sem("decay_arg"), sem("decay_exp"), sem("decay_ready")
        out_done, x_new = sem("out_done"), sem("x_new")
        part_hi, rest_ready, part_mid, parts_ready = (sem(n) for n in ("part_hi", "rest_ready", "part_mid", "parts_ready"))
        logits_done, scores_ready, chosen_ready, ranks_done, route_ready = (
            sem(n) for n in ("logits_done", "scores_ready", "chosen_ready", "ranks_done", "route_ready"))
        sh_up, sh_silu, sh_ready, sh_down = (sem(n) for n in ("sh_up", "sh_silu", "sh_ready", "sh_down"))
        U = [{n: sem(f"{n}{l}") for n in (
            "cols_ready", "onehot_ready", "gathered", "xg_lo", "xg_hi", "S_turned", "w_ready", "up_done", "silu_done",
            "eh_ready", "eh_turned", "ehT_ready", "combined", "S_ready", "down0", "down1", "y_hi", "bank0_read",
            "bank1_read", "y_mid", "y_ready")}
            for l in range(DEPTH)]
        routed_done = sem("routed_done")
        dve_step = sem("dve_step")
        written = sem("written")

        def tile_src(key):
            kind, l, i = key
            if kind == "ada":
                s, q = i // 4, i % 4
                return ada_w[l].rearrange("(p k) n -> p k n", k=KD)[:, :, s * D + q * 256:s * D + q * 256 + 256]
            if kind == "mix_in":
                w = (da_w_in if l == 0 else ret_w_in)[0]
                return w.rearrange("(p k) n -> p k n", k=KD)[:, :, i * 256:(i + 1) * 256]
            if kind == "mix_out":
                w = (da_w_out if l == 0 else ret_w_out)[0]
                return w[i * 256:(i + 1) * 256, :].rearrange("(b p) n -> p b n", p=P)
            w = (sh_w1, sh_w3, sh_w2)[i][l]
            return w.rearrange("(p k) n -> p k n", k=KD) if i < 2 else w.rearrange("(p b) n -> p b n", b=2)

        def slot(n):
            return ring[:, (n % RING) * TW:(n % RING + 1) * TW]

        def tile_in(n):
            return slot(n).rearrange("p (k n) -> p k n", k=KD)

        def tile_out(n):
            return slot(n).rearrange("p (b n) -> p b n", b=2)

        def arrived(eng, n):
            eng.wait_ge(landed[n % RING], 16 * loads[n])

        block = ctx.enter_context(nc.Block())

        @block.sync
        def _(sp):
            def one(n):
                if n >= RING:
                    sp.wait_ge(tiles_used, n - RING + 1)
                sp.dma_start(tile_in(n) if order[n][0] != "mix_out" and order[n][0:3:2] != ("shared", 2) else tile_out(n),
                             tile_src(order[n])).then_inc(landed[n % RING], 16)

            at = 0
            for l in range(DEPTH):
                for n in range(at, MOE0[l]):
                    if order[n][0] != "pad":
                        one(n)
                with sp.Fori(0, PAIRS // 2) as it:
                    for t in range(RING):
                        n = MOE0[l] + t
                        e = it * 4 + t // 3
                        sp.wait_ge(tiles_used, it * RING + (n - RING + 1))
                        w = (exp_w1, exp_w3, exp_w2)[t % 3][l][bass.ds(e, 1), :, :]
                        if t % 3 < 2:
                            sp.dma_start(tile_in(n), w.rearrange("o (p k) n -> p (o k) n", k=KD)).then_inc(landed[n % RING], 16)
                        else:
                            sp.dma_start(tile_out(n), w.rearrange("o (p b) n -> p (o b) n", b=2)).then_inc(landed[n % RING], 16)
                at = MOE0[l] + 3 * E

        @block.gpsimd
        def _(pool):
            steps = [0]

            def step(ins):
                ins.then_inc(pool_step, 1)
                steps[0] += 1
                pool.wait_ge(pool_step, steps[0])

            nc.gpsimd.memset(brow[:, :, :], 0.0).then_inc(rows_zero, 1)
            nc.gpsimd.memset(nrow[:, :, :], 0.0).then_inc(rows_zero, 1)
            step(nc.gpsimd.memset(ident[:, :], 0.0))
            step(nc.gpsimd.affine_select(out=ident[:, :], in_=ident[:, :], compare_op=ALU.not_equal, fill=1.0, base=0,
                                         pattern=[[-1, P]], channel_multiplier=1))
            step(nc.gpsimd.memset(upper[:, :], 1.0))
            step(nc.gpsimd.affine_select(out=upper[:, :], in_=upper[:, :], compare_op=ALU.is_gt, fill=0.0, base=0,
                                         pattern=[[1, P]], channel_multiplier=-1))
            nc.gpsimd.memset(ones[:, :], 1.0)
            nc.gpsimd.tensor_copy(ident16[:, :], ident[:, :])
            step(nc.gpsimd.iota(dist[:, :], pattern=[[-1, T]], base=T - P, channel_multiplier=1,
                                allow_small_or_imprecise_dtypes=True))
            step(nc.gpsimd.affine_select(out=dist[:, :], in_=dist[:, :], compare_op=ALU.is_ge, fill=FAR, base=T - P,
                                         pattern=[[-1, T]], channel_multiplier=1))
            nc.gpsimd.iota(slot_no[:, :], pattern=[[1, SLOTS]], base=0, channel_multiplier=0,
                           allow_small_or_imprecise_dtypes=True)
            nc.gpsimd.iota(pass_base[:, :, :], pattern=[[-SLOTS, 4], [0, 4]], base=0, channel_multiplier=0,
                           allow_small_or_imprecise_dtypes=True)
            step(nc.gpsimd.memset(before[:, :, :], 1.0))
            step(nc.gpsimd.affine_select(out=before[:, :, :], in_=before[:, :, :], compare_op=ALU.is_gt, fill=0.0, base=0,
                                         pattern=[[1, GROUPS], [-1, GROUPS]], channel_multiplier=0))
            nc.gpsimd.memset(ret_s[:, :], 0.0).then_inc(pool_consts, 1)

            def store_rows(l):
                pool.wait_ge(rows_ready[l], 1)
                for q in range(4):
                    pool.dma_start(mod_dram[l].rearrange("s (q n) -> q s n", q=4)[q:q + 1],
                                   mrow[32 * q:32 * q + 1, :, :]).then_inc(rows_stored, 16)
                pool.wait_ge(rows_stored, 64 * (l + 1))

            def spread(l, first, done):
                for s in range(first, first + 3):
                    pool.dma_start(mods[:, s, :], mod_dram[l, s:s + 1, :].broadcast_to([P, D])).then_inc(done, 16)

            for hd in range(RET_HEADS):
                nc.gpsimd.iota(decay[:, hd, :], pattern=[[1, T]], base=0, channel_multiplier=-1,
                               allow_small_or_imprecise_dtypes=True).then_inc(decay_arg, 1)
            store_rows(0)
            spread(0, 0, mix_mods)
            spread(0, 3, moe_mods)
            pool.wait_ge(decay_exp, RET_HEADS)
            for hd in range(RET_HEADS):
                ins = nc.gpsimd.affine_select(out=decay[:, hd, :], in_=decay[:, hd, :], compare_op=ALU.is_ge, fill=0.0,
                                              base=0, pattern=[[1, T]], channel_multiplier=-1)
            ins.then_inc(decay_ready, 1)
            store_rows(1)
            pool.wait_ge(x_new, 1)
            spread(1, 0, mix_mods)

            for l in range(DEPTH):
                u = U[l]
                pool.wait_ge(route_ready, l + 1)
                unit = pool.alloc_register(f"pool_unit{l}")
                pool.reg_mov(unit, 0)
                with pool.Fori(0, PAIRS) as q:
                    n = pool.value_load(npass[0:1, bass.ds(q, 1)], min_val=1, max_val=4)
                    with pool.Fori(0, n) as i:
                        g = pool.snap(unit, min_val=0, max_val=127)
                        pool.wait_ge(u["S_turned"], g + 1)
                        nc.gpsimd.tensor_tensor(rk, rank.rearrange("p e c -> p (e c)")[:, bass.ds(q * 4, 4)],
                                                pass_base.rearrange("p a b -> p (a b)")[:, bass.ds(i * 4, 4)], ALU.add
                                                ).then_inc(u["cols_ready"], 1)
                        pool.wait_ge(u["cols_ready"], g + 1)
                        pool.reg_add(unit, unit, 1)
                        for j in range(2):
                            for tc in range(TC):
                                m = TC * j + tc
                                ins = nc.gpsimd.tensor_scalar(Pg[:, tc, SLOTS * j:SLOTS * (j + 1)], slot_no[:, :],
                                                              rk[:, m:m + 1], None, ALU.is_equal)
                        ins.then_inc(u["onehot_ready"], 1)
                if l == 0:
                    pool.wait_ge(x_new, 2)
                    spread(1, 3, moe_mods)
                    pool.wait_ge(x_new, 3)
                    pool.dma_start(mods[:, 0, :], final_norm.rearrange("(a d) -> a d", a=1).broadcast_to([P, D])
                                   ).then_inc(last_gain, 16)

        @block.scalar
        def _(act):
            act.dma_start(cT[:, :], c.rearrange("o (p k) -> p (o k)", k=KD)).then_inc(c_in, 16)
            act.dma_start(X[:, :, :], x[0].rearrange("(c p) d -> p c d", p=P)).then_inc(x_in, 16)
            for i, v in enumerate((da_lq1, da_lk1, da_lq2, da_lk2)):
                act.dma_start(lvec[:, i, :], v.broadcast_to([P, DA_DH])).then_inc(consts_in, 16)
            act.dma_start(subg[:, :], da_subln.rearrange("a p -> p a"), allow_slow_non_contiguous=True).then_inc(consts_in, 16)
            act.dma_start(gn[:, :], ret_gn.rearrange("a (c p) -> p (a c)", p=P), allow_slow_non_contiguous=True).then_inc(consts_in, 16)
            for l in range(DEPTH):
                act.dma_start(rw[:, l, :, :], router_w[l].rearrange("(p k) e -> p k e", k=KD)).then_inc(consts_in, 16)
                act.dma_start(rb[:, l, :], router_b[l:l + 1, :].broadcast_to([P, E])).then_inc(consts_in, 16)

            def load_rows(l):
                for q in range(4):
                    act.dma_start(brow[32 * q:32 * q + 1, :, :],
                                  ada_b[l:l + 1].rearrange("a (s q n) -> q a s n", s=6, q=4)[q]).then_inc(rows_in[l], 16)
                    for i, g in enumerate((norm_mix, norm_ffn)):
                        act.dma_start(nrow[32 * q:32 * q + 1, i, :], g[l:l + 1, 256 * q:256 * (q + 1)]).then_inc(rows_in[l], 16)

            act.wait_ge(rows_zero, 2)
            load_rows(0)

            act.wait_ge(c_in, 16)
            nc.scalar.activation(cs[:, :], cT[:, :], ACT.Silu).then_inc(c_silu, 1)

            def release(k):
                act.sem_inc(tiles_used, k)

            for s in range(6):
                act.wait_ge(ada_done[0], s + 1)
                release(4)
            act.wait_ge(rows_ready[0], 1)
            load_rows(1)

            for hd in range(RET_HEADS):
                log_g = math.log1p(-(2.0 ** (-5.0 - hd)))
                act.wait_ge(decay_arg, hd + 1)
                nc.scalar.activation(decay[:, hd, :], decay[:, hd, :], ACT.Exp, scale=log_g).then_inc(decay_exp, 1)
            act.wait_ge(lam_sums, 1)
            nc.scalar.activation(lexp[:, :], lsum[:, :], ACT.Exp).then_inc(lam_exp, 1)

            norms = [0]

            def norm_stats():
                n = norms[0]
                for tc in range(TC):
                    if n == 0:
                        act.wait_ge(x_in, 16)
                    nc.scalar.activation(h[:, tc, :], X[:, tc, :], ACT.Square, accum_out=ss[:, tc:tc + 1]
                                         ).then_inc(sumsq, 1)
                act.wait_ge(meansq, n + 1)
                nc.scalar.activation(rs[:, 0:TC], ss[:, 0:TC], ACT.Sqrt).then_inc(root, 1)
                norms[0] += 1

            def evict_hT():
                n = norms[0] - 1
                for m in range(4):
                    act.wait_ge(h_turned, 4 * n + m + 1)
                    nc.scalar.copy(hT[:, 2 * m:2 * m + 2, :], banks[m][:, :].rearrange("p (k t) -> p k t", k=2)
                                   ).then_inc(hT_ready, 1)

            proj = [0]

            def evict_proj(dst, func=None):
                act.wait_ge(proj_done, proj[0] + 1)
                src = banks[3 + proj[0] % 4][:, :].rearrange("p (m t) -> p m t", m=2)
                if func is None:
                    nc.scalar.copy(dst, src).then_inc(proj_out, 1)
                else:
                    nc.scalar.activation(dst, src, func).then_inc(proj_out, 1)
                proj[0] += 1
                release(1)

            def mixer_out(l, tiles):
                for i in range(tiles):
                    act.wait_ge(out_done, (0 if l == 0 else 4) + i + 1)
                    release(1)

            def moe(l):
                norm_stats()
                evict_hT()
                nc.scalar.copy(parts[:, :, 0, :], h).then_inc(part_hi, 1)
                act.wait_ge(rest_ready, l + 1)
                nc.scalar.copy(parts[:, :, 1, :], h).then_inc(part_mid, 1)
                act.wait_ge(logits_done, l + 1)
                nc.scalar.activation(score, banks[2][:, 0:TC * E].rearrange("p (c e) -> p c e", c=TC), ACT.Sigmoid
                                     ).then_inc(scores_ready, 1)
                act.wait_ge(sh_up, l + 1)
                nc.scalar.activation(sg, banks[0][:, :], ACT.Silu).then_inc(sh_silu, 1)
                release(2)
                act.wait_ge(sh_down, l + 1)
                release(MOE0[l] - where["shared", l, 2])
                act.wait_ge(route_ready, l + 1)
                u = U[l]
                unit = act.alloc_register(f"act_unit{l}")
                act.reg_mov(unit, 0)
                with act.Fori(0, PAIRS) as q:
                    n = act.value_load(npass[0:1, bass.ds(q, 1)], min_val=1, max_val=4)
                    with act.Fori(0, n) as i:
                        g = act.snap(unit, min_val=0, max_val=127)
                        act.wait_ge(u["gathered"], g * 2 + 1)
                        nc.scalar.copy(xg[:, 0:4, :], banks[2][:, :].rearrange("p (k n) -> p k n", k=4)).then_inc(u["xg_lo"], 1)
                        act.wait_ge(u["up_done"], g + 1)
                        nc.scalar.activation(sg[:, 0:256], banks[1][:, 0:256], ACT.Silu).then_inc(u["silu_done"], 1)
                        act.wait_ge(u["eh_turned"], g + 1)
                        nc.scalar.copy(ehT, banks[2][:, 0:256].rearrange("p (b n) -> p b n", b=2)).then_inc(u["ehT_ready"], 1)
                        for hf in range(NH):
                            act.wait_ge(u[f"down{hf}"], g + 1)
                            nc.scalar.copy(y[:, 0, 512 * hf:512 * hf + 512], banks[hf][:, :]).then_inc(u["y_hi"], 1)
                        for hf in range(NH):
                            act.wait_ge(u[f"bank{hf}_read"], g + 2)
                            nc.scalar.copy(y[:, 1, 512 * hf:512 * hf + 512], y_rest[:, hf, :]).then_inc(u["y_mid"], 1)
                        act.reg_add(unit, unit, 1)

            def evict_aT(n):
                act.wait_ge(a_turned, n + 1)
                W = P * (1 + n % 2)
                nc.scalar.copy(da_aT[:, n % 2, 0:1 + n % 2, :], banks[5 + n % 2][:, 0:W].rearrange("p (b q) -> p b q", q=P)
                               ).then_inc(aT_ready, 1)

            norm_stats()
            evict_hT()
            for s in range(6):
                for i in (2 * s, 2 * s + 1):
                    if i < 4:
                        evict_proj(qT[:, 2 * i:2 * i + 2, :])
                    elif i < 8:
                        evict_proj(kT[:, 2 * (i - 4):2 * (i - 4) + 2, :])
                    else:
                        evict_proj(da_v[:, :, 256 * (i - 8):256 * (i - 7)])
                act.wait_ge(ada_done[1], s + 1)
                release(4)
            for n in range(2 * DA_HEADS):
                W = P * (1 + n % 2)
                act.wait_ge(s_ready, n + 1)
                for m in range(2):
                    nc.scalar.activation(da_s[:, n % 2, m, 0:W], da_s[:, n % 2, m, 0:W], ACT.Exp, scale=0.125,
                                         bias=soft[:, 0, n, m:m + 1], accum_out=soft[:, 1, n, m:m + 1]).then_inc(exp_done, 1)
                if n >= 1:
                    evict_aT(n - 1)
            evict_aT(2 * DA_HEADS - 1)
            act.wait_ge(o_meansq, 1)
            nc.scalar.activation(rs[:, :], ss[:, :], ACT.Sqrt).then_inc(o_root, 1)
            for m in range(4):
                act.wait_ge(o_turned, m + 1)
                nc.scalar.activation(da_oT[:, 2 * m:2 * m + 2, :], banks[m][:, :].rearrange("p (k t) -> p k t", k=2),
                                     ACT.Copy, scale=subs[:, 0:1]).then_inc(oT_ready, 1)
            mixer_out(0, 4)
            act.wait_ge(x_new, 1)
            moe(0)
            act.wait_ge(x_new, 2)

            norm_stats()
            evict_hT()
            for i in range(24):
                if i < 4:
                    evict_proj(qT[:, 2 * i:2 * i + 2, :])
                elif i < 8:
                    evict_proj(kT[:, 2 * (i - 4):2 * (i - 4) + 2, :])
                elif i < 16:
                    evict_proj(ret_v[:, :, 256 * (i - 8):256 * (i - 7)])
                else:
                    evict_proj(ret_sg[:, 2 * (i - 16):2 * (i - 16) + 2, :], ACT.Silu)
            for n in range(2 * RET_HEADS):
                hd, qb = n // 2, n % 2
                act.wait_ge(pv_done, DA_ITEMS + n + 1)
                if n >= 1:
                    act.wait_ge(o_sumsq, n)
                nc.scalar.activation(ret_junk, banks[5 + n % 2][:, :], ACT.Square, accum_out=ss[:, n:n + 1]
                                     ).then_inc(o_sumsq, 1)
                nc.scalar.copy(ret_o[:, qb, hd, :], banks[5 + n % 2][:, :]).then_inc(o_ready, 1)
            act.wait_ge(o_meansq, 2)
            nc.scalar.activation(rs[:, 0:8], ss[:, 0:8], ACT.Sqrt).then_inc(o_root, 1)
            mixer_out(1, 8)
            act.wait_ge(x_new, 3)
            moe(1)
            act.wait_ge(x_new, 4)
            norm_stats()
            for tc in range(TC):
                act.wait_ge(h_ready, 2 * 4 + tc + 1)
                act.dma_start(out[0, P * tc:P * (tc + 1), :], h[:, tc, :]).then_inc(written, 16)
            act.wait_ge(written, 16 * TC)

        @block.tensor
        def _(pe):
            def ada(l, s):
                tiles = [where["ada", l, 4 * s + q] for q in range(4)]
                for n in tiles:
                    arrived(pe, n)
                for k in range(KD):
                    for q in range(4):
                        ins = nc.tensor.matmul(banks[s // 2][32 * q:32 * q + 32, 256 * (s % 2):256 * (s % 2) + 256],
                                               cb[:, k, :], tile_in(tiles[q])[:, k, :], start=(k == 0), stop=(k == KD - 1))
                ins.then_inc(ada_done[l], 1)

            norms = [0]

            def turn_h():
                pe.wait_ge(h_ready, TC * (norms[0] + 1))
                for m in range(4):
                    for kk in range(2):
                        for tc in range(TC):
                            ins = nc.tensor.transpose(
                                banks[m][:, T * kk + P * tc:T * kk + P * tc + P],
                                h[:, tc, :].rearrange("t (p k) -> t k p", k=KD)[:, 2 * m + kk, :], ident[:, :])
                    ins.then_inc(h_turned, 1)
                norms[0] += 1
                pe.wait_ge(hT_ready, 4 * norms[0])

            proj = [0]

            def project(l, i, token_major):
                n = where["mix_in", l, i]
                arrived(pe, n)
                if proj[0] >= 4:
                    pe.wait_ge(proj_out, proj[0] - 3)
                bank, w = banks[3 + proj[0] % 4], tile_in(n)
                for m in range(2):
                    for k in range(KD):
                        tokens, columns = hT[:, k, P * m:P * m + P], w[:, k, P * m:P * m + P]
                        a, b = (tokens, w[:, k, :]) if token_major else (columns, hT[:, k, :])
                        ins = nc.tensor.matmul(bank[:, 256 * m:256 * m + 256], a, b, start=(k == 0), stop=(k == KD - 1))
                ins.then_inc(proj_done, 1)
                proj[0] += 1

            def mix_out(l, tiles, src):
                for i in range(tiles):
                    arrived(pe, where["mix_out", l, i])
                    w = tile_out(where["mix_out", l, i])
                    if l == 1:
                        pe.wait_ge(oT_ready, 4 + 2 * (i + 1))
                    for b in range(2):
                        for tc in range(TC):
                            for hf in range(NH):
                                ins = nc.tensor.matmul(banks[4 + NH * tc + hf][:, :], src[:, 2 * i + b, P * tc:P * tc + P],
                                                       w[:, b, 512 * hf:512 * hf + 512], start=(i == 0 and b == 0),
                                                       stop=(i == tiles - 1 and b == 1), skip_group_check=True)
                    ins.then_inc(out_done, 1)

            def moe(l):
                turn_h()
                for tc in range(TC):
                    for k in range(KD):
                        ins = nc.tensor.matmul(banks[2][:, E * tc:E * tc + E], hT[:, k, P * tc:P * tc + P], rw[:, l, k, :],
                                               start=(k == 0), stop=(k == KD - 1))
                ins.then_inc(logits_done, 1)
                for i in range(2):
                    arrived(pe, where["shared", l, i])
                    w = tile_in(where["shared", l, i]).rearrange("p k (m b) -> p k b m", b=2)
                    for b in range(2):
                        for k in range(KD):
                            ins = nc.tensor.matmul(banks[i][:, 256 * b:256 * b + 256], w[:, k, b, :], hT[:, k, :],
                                                   start=(k == 0), stop=(k == KD - 1))
                ins.then_inc(sh_up, 1)
                pe.wait_ge(chosen_ready, l + 1)
                nc.tensor.matmul(banks[3][:, 0:E], upper[:, :], mb[:, 0, :], start=True, stop=True)
                nc.tensor.matmul(banks[3][:, E:2 * E], ones[:, :], mb[:, 0, :], start=True, stop=False)
                nc.tensor.matmul(banks[3][:, E:2 * E], upper[:, :], mb[:, 1, :], start=False, stop=True)
                nc.tensor.matmul(banks[3][0:1, 2 * E:3 * E], ones[:, 0:1], mb[:, 0, :], start=True, stop=False)
                nc.tensor.matmul(banks[3][0:1, 2 * E:3 * E], ones[:, 0:1], mb[:, 1, :], start=False, stop=True
                                 ).then_inc(ranks_done, 1)
                pe.wait_ge(sh_ready, l + 1)
                arrived(pe, where["shared", l, 2])
                w = tile_out(where["shared", l, 2])
                for tc in range(TC):
                    for hf in range(NH):
                        for b in range(2):
                            ins = nc.tensor.matmul(banks[4 + NH * tc + hf][:, :], shT[:, b, P * tc:P * tc + P],
                                                   w[:, b, 512 * hf:512 * hf + 512], start=(b == 0), stop=False,
                                                   skip_group_check=True)
                ins.then_inc(sh_down, 1)

                u = U[l]

                def combine(tc, last=False):
                    for hf in range(NH):
                        for r in range(3):
                            ins = nc.tensor.matmul(banks[4 + NH * tc + hf][:, :], S[:, P * tc:P * tc + P],
                                                   y[:, r, 512 * hf:512 * hf + 512], start=False, stop=(last and r == 2),
                                                   skip_group_check=True)
                    return ins

                pe.wait_ge(parts_ready, l + 1)
                pe.wait_ge(route_ready, l + 1)
                unit = pe.alloc_register(f"pe_unit{l}")
                pe.reg_mov(unit, 0)
                with pe.Fori(0, PAIRS // 2) as it:
                    for pair in range(2):
                        t0 = MOE0[l] + 6 * pair
                        s0 = [(t0 + 3 * j) % RING for j in range(2)]
                        w13 = [ring[:, s0[j] * TW:(s0[j] + 2) * TW].rearrange("p (w k n) -> p k w n", w=2, k=KD) for j in range(2)]
                        w2 = [tile_out(t0 + 3 * j + 2) for j in range(2)]

                        def arrived_now(t):
                            pe.wait_ge(landed[(t0 + t) % RING], it * 16 + 16 * loads[t0 + t])

                        n = pe.value_load(npass[0:1, bass.ds(it * 2 + pair, 1)], min_val=1, max_val=4)
                        with pe.Fori(0, n):
                            g = pe.snap(unit, min_val=0, max_val=127)
                            pe.wait_ge(u["onehot_ready"], g + 1)
                            for half in range(2):
                                if half == 1:
                                    pe.wait_ge(u["bank0_read"], g + 1)
                                for kk in range(4):
                                    for tc in range(TC):
                                        for r in range(3):
                                            ins = nc.tensor.matmul(
                                                banks[2 - 2 * half][:, P * kk:P * kk + P],
                                                parts[:, tc, r, :].rearrange("t (p k) -> t k p", k=KD)[:, 4 * half + kk, :],
                                                Pg[:, tc, :], start=(tc == 0 and r == 0), stop=(tc == TC - 1 and r == 2))
                                ins.then_inc(u["gathered"], 1)
                            pe.wait_ge(u["S_ready"], g + 1)
                            for tc in range(TC):
                                nc.tensor.matmul(banks[3][:, P * tc:P * tc + P], Pg[:, tc, :], ident16[:, :],
                                                 start=True, stop=True)
                            for tc in range(TC):
                                ins = nc.tensor.matmul(
                                    banks[3][:, T:T + 6], Pg[:, tc, :],
                                    wparts[:, tc].rearrange("p e r -> p (e r)")[:, bass.ds(it * 12 + 6 * pair, 6)],
                                    start=(tc == 0), stop=(tc == TC - 1))
                            ins.then_inc(u["S_turned"], 1)
                            pe.wait_ge(u["bank1_read"], g + 1)
                            for k in range(KD):
                                if k % 4 == 0:
                                    pe.wait_ge(u["xg_lo" if k == 0 else "xg_hi"], g + 1)
                                for j in range(2):
                                    if k == 0:
                                        arrived_now(3 * j)
                                        arrived_now(3 * j + 1)
                                    ins = nc.tensor.matmul(banks[1][SLOTS * j:SLOTS * (j + 1), :],
                                                           xg[:, k, SLOTS * j:SLOTS * (j + 1)], w13[j][:, k, :, :],
                                                           start=(k == 0), stop=(k == KD - 1))
                            ins.then_inc(u["up_done"], 1)
                            pe.wait_ge(u["y_ready"], g * 2 + 1)
                            combine(0)
                            pe.wait_ge(u["eh_ready"], g + 1)
                            for b in range(2):
                                ins = nc.tensor.transpose(banks[2][:, P * b:P * b + P], eh[:, b, :], ident[:, :])
                            ins.then_inc(u["eh_turned"], 1)
                            combine(1).then_inc(u["combined"], 1)
                            pe.wait_ge(u["ehT_ready"], g + 1)
                            for hf in range(NH):
                                for b in range(2):
                                    for j in range(2):
                                        if hf == 0 and b == 0:
                                            arrived_now(3 * j + 2)
                                        ins = nc.tensor.matmul(banks[hf][SLOTS * j:SLOTS * (j + 1), :],
                                                               ehT[:, b, SLOTS * j:SLOTS * (j + 1)],
                                                               w2[j][:, b, 512 * hf:512 * hf + 512], start=(b == 0), stop=(b == 1))
                                ins.then_inc(u["down0" if hf == 0 else "down1"], 1)
                            pe.reg_add(unit, unit, 1)
                total = pe.snap(unit, min_val=PAIRS, max_val=128)
                pe.wait_ge(u["S_ready"], total + 1)
                pe.wait_ge(u["y_ready"], total * 2 + 1)
                combine(0, last=True)
                combine(1, last=True).then_inc(routed_done, 1)

            pe.wait_ge(cb_ready, 1)
            for s in range(6):
                ada(0, s)
            pe.wait_ge(pool_consts, 1)
            turn_h()
            for s in range(6):
                project(0, 2 * s, token_major=(s >= 4))
                project(0, 2 * s + 1, token_major=(s >= 4))
                ada(1, s)
            pe.wait_ge(proj_out, 12)
            pe.wait_ge(rows_ready[1], 1)

            def scores(n):
                hd, qb = n // 2, n % 2
                if n >= 2:
                    pe.wait_ge(s_ready, n - 1)
                for m in range(2):
                    ins = nc.tensor.matmul(banks[1 + 2 * (n % 2) + m][:, 0:P * (1 + qb)],
                                           qT[64 * m:64 * m + 64, hd, P * qb:P * qb + P],
                                           kT[64 * m:64 * m + 64, hd, 0:P * (1 + qb)], start=True, stop=True)
                ins.then_inc(scored, 1)

            def turn_a(n):
                pe.wait_ge(a_ready, n + 1)
                if n >= 2:
                    pe.wait_ge(aT_ready, n - 1)
                for kb in range(1 + n % 2):
                    ins = nc.tensor.transpose(banks[5 + n % 2][:, P * kb:P * kb + P], da_a[:, n % 2, P * kb:P * kb + P], ident[:, :])
                ins.then_inc(a_turned, 1)

            def attend(n):
                hd, qb = n // 2, n % 2
                pe.wait_ge(aT_ready, n + 1)
                if n >= 2:
                    pe.wait_ge(o_ready, n - 1)
                for kb in range(1 + qb):
                    ins = nc.tensor.matmul(banks[7 * (n % 2)][:, 0:P], da_aT[:, n % 2, kb, :], da_v[:, kb, P * hd:P * hd + P],
                                           start=(kb == 0), stop=(kb == qb))
                ins.then_inc(pv_done, 1)

            scores(0)
            for n in range(DA_ITEMS):
                if n + 1 < DA_ITEMS:
                    scores(n + 1)
                turn_a(n)
                if n >= 1:
                    attend(n - 1)
            attend(DA_ITEMS - 1)
            pe.wait_ge(o_normed, 1)
            for m in range(4):
                for hh in range(2):
                    for tc in range(TC):
                        ins = nc.tensor.transpose(banks[m][:, T * hh + P * tc:T * hh + P * tc + P], da_o[:, tc, 2 * m + hh, :], ident[:, :])
                ins.then_inc(o_turned, 1)
            pe.wait_ge(oT_ready, 4)
            mix_out(0, 4, da_oT)
            moe(0)

            turn_h()
            for i in range(24):
                project(1, i, token_major=(8 <= i < 16))
            pe.wait_ge(proj_out, 36)

            def ret_scores(hd):
                if hd >= 2:
                    pe.wait_ge(s_ready, DA_ITEMS + hd - 1)
                bank = banks[hd % 2]
                for kk in range(2):
                    nc.tensor.matmul(bank[:, 0:T], kT[:, 2 * hd + kk, 0:P], qT[:, 2 * hd + kk, :], start=(kk == 0), stop=(kk == 1))
                for kk in range(2):
                    ins = nc.tensor.matmul(bank[:, T:T + P], kT[:, 2 * hd + kk, P:T], qT[:, 2 * hd + kk, P:T],
                                           start=(kk == 0), stop=(kk == 1))
                ins.then_inc(scored, 1)

            def ret_attend(hd):
                pe.wait_ge(s_ready, DA_ITEMS + hd + 1)
                v = [ret_v[:, jb, 512 * hd:512 * hd + 512] for jb in range(2)]
                if hd >= 1:
                    pe.wait_ge(o_ready, DA_ITEMS + 2 * hd - 1)
                nc.tensor.matmul(banks[5][:, :], ret_s[:, 0:P], v[0], start=True, stop=True).then_inc(pv_done, 1)
                if hd >= 1:
                    pe.wait_ge(o_ready, DA_ITEMS + 2 * hd)
                nc.tensor.matmul(banks[6][:, :], ret_s[:, P:T], v[0], start=True, stop=False)
                nc.tensor.matmul(banks[6][:, :], ret_s[:, T:T + P], v[1], start=False, stop=True).then_inc(pv_done, 1)

            ret_scores(0)
            for hd in range(RET_HEADS):
                if hd + 1 < RET_HEADS:
                    ret_scores(hd + 1)
                ret_attend(hd)
            pe.wait_ge(o_normed, 2)
            for ch in range(16):
                if ch >= 8:
                    pe.wait_ge(oT_ready, 4 + 2 * (ch // 2) - 6)
                for tc in range(TC):
                    ins = nc.tensor.transpose(banks[(ch // 2) % 4][:, T * (ch % 2) + P * tc:T * (ch % 2) + P * tc + P],
                                              ret_o[:, tc, ch // 4, P * (ch % 4):P * (ch % 4) + P], ident[:, :])
                if ch % 2:
                    ins.then_inc(o_turned, 1)
            mix_out(1, 8, ret_yT)
            moe(1)

        @block.vector
        def _(dve):
            steps = [0]

            def step(ins):
                ins.then_inc(dve_step, 1)
                steps[0] += 1
                dve.wait_ge(dve_step, steps[0])

            dve.wait_ge(c_silu, 1)
            nc.vector.tensor_copy(cb[:, :, :], cs[:, :].unsqueeze(2).to_broadcast([P, KD, 32])).then_inc(cb_ready, 1)
            dve.wait_ge(consts_in, 16 * 10)
            step(nc.vector.tensor_tensor(lprod, lvec[:, 0:4:2, :], lvec[:, 1:4:2, :], ALU.mult))
            nc.vector.tensor_reduce(lsum[:, :], lprod, AX_X, ALU.add).then_inc(lam_sums, 1)
            nc.vector.tensor_scalar(subs[:, :], subg[:, :], 1.0 - LAM_INIT, None, ALU.mult)

            def mod_rows(l):
                dve.wait_ge(rows_in[l], 16 * 12)
                dve.wait_ge(ada_done[l], 6)
                if l == 1:
                    dve.wait_ge(rows_stored, 64)
                for i in range(3):
                    ins = nc.vector.tensor_tensor(mrow[:, 2 * i:2 * i + 2, :], banks[i][:, :].rearrange("p (s n) -> p s n", s=2),
                                                  brow[:, 2 * i:2 * i + 2, :], ALU.add)
                step(ins)
                for i in range(2):
                    ins = nc.vector.scalar_tensor_tensor(out=mrow[:, 1 + 3 * i, :], in0=mrow[:, 1 + 3 * i, :], scalar=1.0,
                                                         in1=nrow[:, i, :], op0=ALU.add, op1=ALU.mult)
                ins.then_inc(rows_ready[l], 1)

            mod_rows(0)
            dve.wait_ge(lam_exp, 1)
            step(nc.vector.tensor_tensor(nlam[:, :], lexp[:, 1:2], lexp[:, 0:1], ALU.subtract))
            step(nc.vector.tensor_scalar(nlam[:, :], nlam[:, :], -LAM_INIT, None, ALU.add))

            norms = [0]

            def norm(first):
                n = norms[0]
                dve.wait_ge(sumsq, TC * (n + 1))
                nc.vector.tensor_scalar(ss[:, 0:TC], ss[:, 0:TC], 1.0 / D, EPS, ALU.mult, ALU.add).then_inc(meansq, 1)
                dve.wait_ge(root, n + 1)
                step(nc.vector.reciprocal(rs[:, 0:TC], rs[:, 0:TC]))
                if n == 4:
                    dve.wait_ge(last_gain, 16)
                else:
                    dve.wait_ge(mix_mods if first == 0 else moe_mods, 48 * (n // 2 + 1))
                gain = mods[:, 0 if n == 4 else first + 1, :]
                for tc in range(TC):
                    ins = nc.vector.scalar_tensor_tensor(out=h[:, tc, :], in0=X[:, tc, :], scalar=rs[:, tc:tc + 1],
                                                         in1=gain, op0=ALU.mult, op1=ALU.mult)
                    if n == 4:
                        ins.then_inc(h_ready, 1)
                if n < 4:
                    step(ins)
                    for tc in range(TC):
                        nc.vector.tensor_tensor(h[:, tc, :], h[:, tc, :], mods[:, first, :], ALU.add).then_inc(h_ready, 1)
                norms[0] += 1

            def update_x(gate):
                for tc in range(TC):
                    for hf in range(NH):
                        ins = nc.vector.tensor_tensor(h[:, tc, 512 * hf:512 * hf + 512], banks[4 + NH * tc + hf][:, :],
                                                      mods[:, gate, 512 * hf:512 * hf + 512], ALU.mult)
                step(ins)
                nc.vector.tensor_tensor(X[:, :, :], X[:, :, :], h, ALU.add).then_inc(x_new, 1)

            def moe(l):
                dve.wait_ge(x_new, 1 + 2 * l)
                norm(3)
                dve.wait_ge(h_turned, 4 * norms[0])
                dve.wait_ge(part_hi, l + 1)
                nc.vector.tensor_tensor(h, h, parts[:, :, 0, :], ALU.subtract).then_inc(rest_ready, 1)
                dve.wait_ge(rest_ready, l + 1)
                dve.wait_ge(part_mid, l + 1)
                nc.vector.tensor_tensor(parts[:, :, 2, :], h, parts[:, :, 1, :], ALU.subtract).then_inc(parts_ready, 1)
                dve.wait_ge(scores_ready, l + 1)
                step(nc.vector.tensor_tensor(choice, score, rb[:, l:l + 1, :].to_broadcast([P, TC, E]), ALU.add))
                for tc in range(TC):
                    for gr in range(GROUPS):
                        ins = nc.vector.max(top[:, tc * GROUPS + gr, :], choice[:, tc, 8 * gr:8 * gr + 8])
                step(ins)
                step(nc.vector.tensor_tensor(gs.rearrange("p c g -> p (c g)").unsqueeze(2), top[:, :, 0:1], top[:, :, 1:2], ALU.add))
                other = gs.unsqueeze(2).to_broadcast([P, TC, GROUPS, GROUPS])
                own = gs.unsqueeze(3).to_broadcast([P, TC, GROUPS, GROUPS])
                nc.vector.tensor_tensor(cmp1, other, own, ALU.is_gt)
                step(nc.vector.tensor_tensor(cmp2, other, own, ALU.is_equal))
                for tc in range(TC):
                    ins = nc.vector.tensor_tensor(cmp2[:, tc, :, :], cmp2[:, tc, :, :], before[:, :, :], ALU.mult)
                step(ins)
                step(nc.vector.tensor_tensor(cmp1, cmp1, cmp2, ALU.add))
                step(nc.vector.tensor_reduce(grank, cmp1, AX_X, ALU.add))
                step(nc.vector.tensor_scalar(grank, grank, TOPG - 0.5, -FAR, ALU.is_gt, ALU.mult))
                step(nc.vector.tensor_tensor(masked.rearrange("p c (g m) -> p (c g) m", m=8),
                                             choice.rearrange("p c (g m) -> p (c g) m", m=8),
                                             grank.rearrange("p c g -> p (c g)").unsqueeze(2).to_broadcast([P, TC * GROUPS, 8]),
                                             ALU.add))
                for tc in range(TC):
                    ins = nc.vector.max(top8[:, tc, :], masked[:, tc, :])
                step(ins)
                for tc in range(TC):
                    ins = nc.vector.match_replace(chosen[:, tc, :], top8[:, tc, :], masked[:, tc, :], -3e38)
                step(ins)
                step(nc.vector.tensor_tensor(chosen, chosen, masked, ALU.not_equal))
                nc.vector.tensor_copy(mb, chosen).then_inc(chosen_ready, 1)
                step(nc.vector.tensor_tensor(masked, score, chosen, ALU.mult))
                step(nc.vector.tensor_reduce(wsum, masked, AX_X, ALU.add))
                step(nc.vector.reciprocal(winv, wsum))
                for tc in range(TC):
                    ins = nc.vector.tensor_scalar(weight[:, tc, :], masked[:, tc, :], winv[:, tc:tc + 1], ROUTED_SCALE,
                                                  ALU.mult, ALU.mult)
                step(ins)
                step(nc.vector.tensor_copy(wparts[:, :, :, 0], weight))
                step(nc.vector.tensor_tensor(wrest, weight, wparts[:, :, :, 0], ALU.subtract))
                step(nc.vector.tensor_copy(wparts[:, :, :, 1], wrest))
                nc.vector.tensor_tensor(wparts[:, :, :, 2], wrest, wparts[:, :, :, 1], ALU.subtract)
                u = U[l]
                nc.vector.memset(S, 0.0).then_inc(u["S_ready"], 1)
                nc.vector.memset(y, 0.0).then_inc(u["y_ready"], 1)
                nc.vector.memset(w_slot, 0.0).then_inc(u["S_turned"], 1)
                nc.vector.memset(y_rest[:, 0, 0:1], 0.0).then_inc(u["bank0_read"], 1)
                nc.vector.memset(y_rest[:, 1, 0:1], 0.0).then_inc(u["bank1_read"], 1)
                dve.wait_ge(sh_silu, l + 1)
                nc.vector.tensor_tensor(shT, sg.rearrange("p (b t) -> p b t", b=2),
                                        banks[1][:, :].rearrange("p (b t) -> p b t", b=2), ALU.mult).then_inc(sh_ready, 1)
                dve.wait_ge(ranks_done, l + 1)
                nc.vector.scalar_tensor_tensor(out=choice, in0=banks[3][:, 0:TC * E].rearrange("p (c e) -> p c e", c=TC),
                                               scalar=1.0, in1=chosen, op0=ALU.add, op1=ALU.mult)
                step(nc.vector.tensor_copy(cnt, banks[3][0:1, 2 * E:3 * E]))
                nc.vector.tensor_scalar(rank.rearrange("p e c -> p c e"), choice, -1.0, None, ALU.add)
                pairs = cnt.rearrange("a (q j) -> a j q", j=2)
                step(nc.vector.tensor_tensor(cmax, pairs[:, 0, :], pairs[:, 1, :], ALU.max))
                step(nc.vector.tensor_scalar(npf, cmax, float(SLOTS), 1.0, ALU.is_gt, ALU.add))
                step(nc.vector.scalar_tensor_tensor(out=npf, in0=cmax, scalar=2.0 * SLOTS, in1=npf, op0=ALU.is_gt, op1=ALU.add))
                nc.vector.scalar_tensor_tensor(out=npass, in0=cmax, scalar=3.0 * SLOTS, in1=npf, op0=ALU.is_gt, op1=ALU.add
                                               ).then_inc(route_ready, 1)
                dve.wait_ge(route_ready, l + 1)
                unit = dve.alloc_register(f"dve_unit{l}")
                dve.reg_mov(unit, 0)
                with dve.Fori(0, PAIRS) as q:
                    n = dve.value_load(npass[0:1, bass.ds(q, 1)], min_val=1, max_val=4)
                    with dve.Fori(0, n):
                        g = dve.snap(unit, min_val=0, max_val=127)
                        dve.wait_ge(u["gathered"], g * 2 + 2)
                        nc.vector.tensor_copy(xg[:, 4:8, :], banks[0][:, :].rearrange("p (k n) -> p k n", k=4)
                                              ).then_inc(u["xg_hi"], 1)
                        dve.wait_ge(u["S_turned"], g + 2)
                        for j in range(2):
                            nc.vector.tensor_reduce(w_slot[SLOTS * j:SLOTS * (j + 1), :],
                                                    banks[3][SLOTS * j:SLOTS * (j + 1), T + 3 * j:T + 3 * j + 3], AX_X, ALU.add
                                                    ).then_inc(u["w_ready"], 1)
                        dve.wait_ge(u["w_ready"], g * 2 + 2)
                        dve.wait_ge(u["silu_done"], g + 1)
                        nc.vector.scalar_tensor_tensor(out=eh.rearrange("p b n -> p n b"),
                                                       in0=banks[1][:, 256:512].rearrange("p (n b) -> p n b", b=2),
                                                       scalar=w_slot, in1=sg[:, 0:256].rearrange("p (n b) -> p n b", b=2),
                                                       op0=ALU.mult, op1=ALU.mult).then_inc(u["eh_ready"], 1)
                        dve.wait_ge(u["combined"], g + 1)
                        nc.vector.tensor_copy(S, banks[3][:, 0:T]).then_inc(u["S_ready"], 1)
                        for hf in range(NH):
                            dve.wait_ge(u["y_hi"], g * 2 + hf + 1)
                            nc.vector.tensor_tensor(y_rest[:, hf, :], banks[hf][:, :], y[:, 0, 512 * hf:512 * hf + 512],
                                                    ALU.subtract).then_inc(u[f"bank{hf}_read"], 1)
                        for hf in range(NH):
                            dve.wait_ge(u["y_mid"], g * 2 + hf + 1)
                            nc.vector.tensor_tensor(y[:, 2, 512 * hf:512 * hf + 512], y_rest[:, hf, :],
                                                    y[:, 1, 512 * hf:512 * hf + 512], ALU.subtract).then_inc(u["y_ready"], 1)
                        dve.reg_add(unit, unit, 1)
                    dve.sem_inc(tiles_used, 6)
                dve.wait_ge(routed_done, l + 1)
                update_x(5)

            norm(0)
            mod_rows(1)

            def finish_a(n):
                W = P * (1 + n % 2)
                dve.wait_ge(exp_done, 2 * n + 2)
                step(nc.vector.reciprocal(soft[:, 2, n, :], soft[:, 1, n, :]))
                step(nc.vector.tensor_tensor(soft[:, 2, n, 1:2], soft[:, 2, n, 1:2], nlam[:, :], ALU.mult))
                if n >= 2:
                    dve.wait_ge(a_turned, n - 1)
                step(nc.vector.tensor_scalar(da_a[:, n % 2, 0:W], da_s[:, n % 2, 0, 0:W], soft[:, 2, n, 0:1], None, ALU.mult))
                nc.vector.scalar_tensor_tensor(out=da_a[:, n % 2, 0:W], in0=da_s[:, n % 2, 1, 0:W], scalar=soft[:, 2, n, 1:2],
                                               in1=da_a[:, n % 2, 0:W], op0=ALU.mult, op1=ALU.add).then_inc(a_ready, 1)

            def keep_o(n):
                dve.wait_ge(pv_done, n + 1)
                if n == 0:
                    dve.wait_ge(rows_stored, 128)
                nc.vector.tensor_copy(da_o[:, n % 2, n // 2, :], banks[7 * (n % 2)][:, 0:P]).then_inc(o_ready, 1)

            for n in range(DA_ITEMS):
                hd, qb = n // 2, n % 2
                W = P * (1 + qb)
                slope = 2.0 ** (-8.0 * (hd + 1) / DA_HEADS)
                sn = da_s[:, n % 2, :, 0:W]
                dve.wait_ge(scored, n + 1)
                if n >= 2:
                    dve.wait_ge(a_ready, n - 1)
                for m in range(2):
                    ins = nc.vector.scalar_tensor_tensor(out=sn[:, m, :], in0=dist[:, T - W:T], scalar=-8.0 * slope,
                                                         in1=banks[1 + 2 * (n % 2) + m][:, 0:W], op0=ALU.mult, op1=ALU.add)
                step(ins)
                step(nc.vector.tensor_reduce(soft[:, 0, n, :], sn, AX_X, ALU.max))
                nc.vector.tensor_scalar(soft[:, 0, n, :], soft[:, 0, n, :], -0.125, None, ALU.mult).then_inc(s_ready, 1)
                if n >= 1:
                    finish_a(n - 1)
                if n >= 3:
                    keep_o(n - 3)
            finish_a(DA_ITEMS - 1)
            for n in range(DA_ITEMS - 3, DA_ITEMS):
                keep_o(n)
            dve.wait_ge(o_ready, DA_ITEMS)
            for tc in range(TC):
                ins = nc.vector.tensor_tensor(da_sq[:, tc], da_o[:, tc], da_o[:, tc], ALU.mult)
            step(ins)
            step(nc.vector.tensor_reduce(ss[:, :], da_sq.rearrange("p c h d -> p (c h) d"), AX_X, ALU.add))
            nc.vector.tensor_scalar(ss[:, :], ss[:, :], 1.0 / P, EPS, ALU.mult, ALU.add).then_inc(o_meansq, 1)
            dve.wait_ge(o_root, 1)
            step(nc.vector.reciprocal(rs[:, :], rs[:, :]))
            o2 = da_o.rearrange("p c h d -> p (c h) d")
            nc.vector.tensor_tensor(o2, o2, rs[:, :].unsqueeze(2).to_broadcast([P, 2 * DA_HEADS, P]), ALU.mult
                                    ).then_inc(o_normed, 1)
            dve.wait_ge(out_done, 4)
            update_x(2)
            moe(0)

            dve.wait_ge(x_new, 2)
            norm(0)
            dve.wait_ge(decay_ready, 1)
            for hd in range(RET_HEADS):
                dve.wait_ge(scored, DA_ITEMS + hd + 1)
                if hd >= 1:
                    dve.wait_ge(pv_done, DA_ITEMS + 2 * hd)
                nc.vector.scalar_tensor_tensor(out=ret_s[:, 0:T], in0=banks[hd % 2][:, 0:T], scalar=RET_DK ** -0.5,
                                               in1=decay[:, hd, :], op0=ALU.mult, op1=ALU.mult)
                nc.vector.scalar_tensor_tensor(out=ret_s[:, T:T + P], in0=banks[hd % 2][:, T:T + P], scalar=RET_DK ** -0.5,
                                               in1=decay[:, hd, 0:P], op0=ALU.mult, op1=ALU.mult).then_inc(s_ready, 1)
            dve.wait_ge(o_sumsq, 2 * RET_HEADS)
            nc.vector.tensor_scalar(ss[:, 0:8], ss[:, 0:8], 1.0 / 512, EPS, ALU.mult, ALU.add).then_inc(o_meansq, 1)
            dve.wait_ge(o_root, 2)
            step(nc.vector.reciprocal(rs[:, 0:8], rs[:, 0:8]))
            dve.wait_ge(o_ready, DA_ITEMS + 2 * RET_HEADS)
            for n in range(2 * RET_HEADS):
                ins = nc.vector.tensor_scalar(ret_o[:, n % 2, n // 2, :], ret_o[:, n % 2, n // 2, :], rs[:, n:n + 1], None, ALU.mult)
            ins.then_inc(o_normed, 1)
            for ch in range(16):
                dve.wait_ge(o_turned, 4 + ch // 2 + 1)
                nc.vector.scalar_tensor_tensor(out=ret_yT[:, ch, :], in0=banks[(ch // 2) % 4][:, T * (ch % 2):T * (ch % 2) + T],
                                               scalar=gn[:, ch:ch + 1], in1=ret_sg[:, ch, :], op0=ALU.mult, op1=ALU.mult
                                               ).then_inc(oT_ready, 1)
            dve.wait_ge(out_done, 12)
            update_x(2)
            moe(1)
            dve.wait_ge(x_new, 4)
            norm(0)


_INS = ["x", "c", "norm_mix", "norm_ffn", "ada_w", "ada_b", "da_w_in", "da_w_out", "da_lq1", "da_lk1", "da_lq2",
        "da_lk2", "da_subln", "ret_w_in", "ret_w_out", "ret_gn", "router_w", "router_b", "exp_w1", "exp_w3",
        "exp_w2", "sh_w1", "sh_w3", "sh_w2", "final_norm"]
_OUTS = [((1, 256, 1024), "float32")]


def kernel(**inputs):
    import numpy as _np
    import concourse.bacc as _bacc
    from concourse import mybir as _mybir
    from concourse.bass_utils import run_bass_kernel_spmd as _run

    nc = _bacc.Bacc("TRN2", target_bir_lowering=False, num_devices=1)
    arrays, args = {}, []
    for name in _INS:
        a = _np.ascontiguousarray(inputs[name])
        arrays[f"in_{name}_dram"] = a
        args.append(nc.dram_tensor(f"in_{name}_dram", a.shape, _mybir.dt.from_np(a.dtype), kind="ExternalInput").ap())
    for i, (shape, dtype) in enumerate(_OUTS):
        dt = _mybir.dt.from_np(_np.dtype(dtype))
        args.append(nc.dram_tensor(f"out_{i}_dram", shape, dt, kind="ExternalOutput").ap())
    trunk(nc, *args)
    r = _run(nc, [arrays], core_ids=[0])
    got = tuple(r.results[0][f"out_{i}_dram"] for i in range(len(_OUTS)))
    return got[0]
```

```python
import math
from contextlib import ExitStack

import concourse.bass as bass
from concourse import mybir

F32 = mybir.dt.float32
BF16 = mybir.dt.bfloat16
I32 = mybir.dt.int32
ALU = mybir.AluOpType
ACT = mybir.ActivationFunctionType
AX_X = mybir.AxisListType.X

P = 128
EPS = 1e-6
RING = 12
TW = 2048
SLOTS = 64
DA_HEADS, DA_DH = 8, 64
RET_HEADS, RET_DK = 4, 256
GROUPS, TOPG, TOPK = 8, 4, 8
ROUTED_SCALE = 2.5
FAR = 1e30


LATER = [(1, s) for s in range(4)] + [(0, s) for s in range(2, 6)] + [(1, 4), (1, 5)]
AT_PROJ = [2, 5, 8, 11]
AT_ITEM = [1, 3, 6, 9, 11, 14]


def plan_stream():
    later = [[("ada", l, 4 * s + q) for q in range(4)] for l, s in LATER]
    order = [("ada", 0, i) for i in range(8)]
    for i in range(12):
        order.append(("mix_in", 0, i))
        if i in AT_PROJ:
            order += later[AT_PROJ.index(i)]
    order += sum(later[4:], [])
    order += [("mix_out", 0, i) for i in range(4)]
    order += [("shared", 0, i) for i in range(3)] + [("pad",)] * 2
    moe = {0: len(order)}
    order += [("expert", 0, i) for i in range(192)]
    order += [("mix_in", 1, i) for i in range(24)] + [("mix_out", 1, i) for i in range(8)]
    order += [("shared", 1, i) for i in range(3)] + [("pad",)]
    moe[1] = len(order)
    order += [("expert", 1, i) for i in range(192)]
    return order, moe


def trunk(nc, x, c, norm_mix, norm_ffn, ada_w, ada_b, da_w_in, da_w_out, da_lq1, da_lk1, da_lq2, da_lk2,
          da_subln, ret_w_in, ret_w_out, ret_gn, router_w, router_b, exp_w1, exp_w3, exp_w2,
          sh_w1, sh_w3, sh_w2, final_norm, out):
    _, T, D = x.shape
    TC, KD = T // P, D // P
    E = router_w.shape[2]
    PAIRS = E // 2
    NH = D // 512
    LAM_INIT = 0.8 - 0.6 * math.exp(-0.3 * 0)
    DEPTH = 2
    DA_ITEMS = 2 * DA_HEADS

    order, MOE0 = plan_stream()
    where = {key: n for n, key in enumerate(order) if key[0] != "pad"}
    loads = [sum(1 for m in range(n % RING, n + 1, RING) if order[m][0] != "pad") for n in range(len(order))]
    assert all(MOE0[l] % 3 == 0 for l in range(DEPTH))

    with ExitStack() as ctx:
        def sb(name, shape, dt=F32):
            return ctx.enter_context(nc.sbuf_tensor(name, shape, dt))

        def sem(name):
            return ctx.enter_context(nc.semaphore(name))

        ring = sb("ring", [P, RING * TW])
        X = sb("X", [P, TC, D])
        HH = sb("HH", [P, 2 * TC * D])
        h = HH[:, 0:TC * D].rearrange("p (c d) -> p c d", c=TC)
        hT = HH[:, TC * D:].rearrange("p (k t) -> p k t", k=KD)
        mods = sb("mods", [P, 6, D])
        arena = sb("arena", [P, 12288])

        ident = sb("ident", [P, P])
        upper = sb("upper", [P, P], BF16)
        ones = sb("ones", [P, P], BF16)
        ident16 = sb("ident16", [P, P], BF16)
        dist = sb("dist", [P, T])
        slot_no = sb("slot_no", [P, SLOTS])
        pass_base = sb("pass_base", [P, 4, 4])
        before = sb("before", [P, GROUPS, GROUPS])
        mod_T = sb("mod_T", [P, DEPTH, 6, KD])
        cT = sb("cT", [P, KD])
        cs = sb("cs", [P, KD])
        cb = sb("cb", [P, KD, 32])
        lsum = sb("lsum", [P, 2])
        lexp = sb("lexp", [P, 2])
        nlam = sb("nlam", [P, 1])
        subg = sb("subg", [P, 1])
        subs = sb("subs", [P, 1])
        gn = sb("gn", [P, 16])
        rw = sb("rw", [P, DEPTH, KD, E])
        rb = sb("rb", [P, DEPTH, E])
        soft = sb("soft", [P, 3, 2 * DA_HEADS, 2])
        decay = sb("decay", [P, RET_HEADS, T])
        ret_s = sb("ret_s", [P, T + P])
        ss = sb("ss", [P, 16])
        rs = sb("rs", [P, 16])

        banks = [ctx.enter_context(nc.psum_tensor(f"bank{i}", [P, 512], F32)) for i in range(8)]
        mod_dram = nc.dram_tensor("mod_dram", [DEPTH, 6, D], F32, kind="Internal").ap()

        mrow0 = arena[:, 6144:6656].rearrange("p (s n) -> p s n", s=2)
        brow0 = arena[:, 6912:7424].rearrange("p (s n) -> p s n", s=2)
        nrow0 = arena[:, 7424:7680].rearrange("p (s n) -> p s n", s=1)
        mrow = HH[:, 0:2560].rearrange("p (s n) -> p s n", s=10)
        browA = HH[:, 2560:3584].rearrange("p (s n) -> p s n", s=4)
        nrowA = HH[:, 3584:3840].rearrange("p (s n) -> p s n", s=1)
        browB = arena[:, 8192:9728].rearrange("p (s n) -> p s n", s=6)
        nrowB = arena[:, 9728:10240].rearrange("p (s n) -> p s n", s=2)
        lvec = arena[:, 11264:11520].rearrange("p (i n) -> p i n", i=4)
        lprod = arena[:, 11520:11648].rearrange("p (i n) -> p i n", i=2)
        qT = arena[:, 0:2048].rearrange("p (k t) -> p k t", k=8)
        kT = arena[:, 2048:4096].rearrange("p (k t) -> p k t", k=8)
        da_v = arena[:, 4096:6144].rearrange("p (c d) -> p c d", c=TC)
        da_o = arena[:, 6144:8192].rearrange("p (c h d) -> p c h d", c=TC, h=DA_HEADS)
        da_oT = arena[:, 0:2048].rearrange("p (h t) -> p h t", h=DA_HEADS)
        da_s = arena[:, 10240:11264].rearrange("p (b m k) -> p b m k", b=2, m=2)
        da_a = arena[:, 11264:11776].rearrange("p (b k) -> p b k", b=2)
        da_aT = arena[:, 11776:12288].rearrange("p (b k q) -> p b k q", b=2, k=2)
        ret_v = arena[:, 4096:8192].rearrange("p (c d) -> p c d", c=TC)
        ret_sg = arena[:, 8192:12288].rearrange("p (c t) -> p c t", c=16)
        ret_yT = arena[:, 0:4096].rearrange("p (c t) -> p c t", c=16)
        ret_o = HH[:, :].rearrange("p (c h d) -> p c h d", c=TC, h=RET_HEADS)
        da_sq = arena[:, 2048:4096].rearrange("p (c h d) -> p c h d", c=TC, h=DA_HEADS)
        ret_junk = cb.rearrange("p k m -> p (k m)").bitcast(BF16)
        parts = arena[:, 0:3072].bitcast(BF16).rearrange("p (c r d) -> p c r d", c=TC, r=3)
        xg = arena[:, 3072:4096].rearrange("p (k n) -> p k n", k=KD)
        y = arena[:, 4096:5632].bitcast(BF16).rearrange("p (r d) -> p r d", r=3)
        S = arena[:, 5632:5760].bitcast(BF16)
        sg = arena[:, 5760:6272]
        eh = arena[:, 6272:6528].rearrange("p (b n) -> p b n", b=2)
        ehT = arena[:, 6528:6784].rearrange("p (b n) -> p b n", b=2)
        y_rest = arena[:, 8736:9760].rearrange("p (f n) -> p f n", f=NH)
        Pg = arena[:, 9760:9888].bitcast(BF16).rearrange("p (c n) -> p c n", c=TC)
        wparts = arena[:, 9888:10080].bitcast(BF16).rearrange("p (c e r) -> p c e r", c=TC, r=3)
        wrest = arena[:, 10080:10208].rearrange("p (c e) -> p c e", c=TC)
        w_slot = arena[:, 10208:10209]
        shT = arena[:, 6784:7296].rearrange("p (b t) -> p b t", b=2)
        score = arena[:, 7296:7424].rearrange("p (c e) -> p c e", c=TC)
        choice = arena[:, 7424:7552].rearrange("p (c e) -> p c e", c=TC)
        masked = arena[:, 7552:7680].rearrange("p (c e) -> p c e", c=TC)
        chosen = arena[:, 7680:7808].rearrange("p (c e) -> p c e", c=TC)
        top = arena[:, 7808:7936].rearrange("p (g m) -> p g m", m=8)
        gs = arena[:, 7936:7952].rearrange("p (c g) -> p c g", c=TC)
        cmp1 = arena[:, 7952:8080].rearrange("p (c g m) -> p c g m", c=TC, g=GROUPS)
        cmp2 = arena[:, 8080:8208].rearrange("p (c g m) -> p c g m", c=TC, g=GROUPS)
        grank = arena[:, 8208:8224].rearrange("p (c g) -> p c g", c=TC)
        top8 = arena[:, 8224:8240].rearrange("p (c m) -> p c m", c=TC)
        wsum = arena[:, 8240:8242]
        winv = arena[:, 8242:8244]
        mb = arena[:, 8244:8308].bitcast(BF16).rearrange("p (c e) -> p c e", c=TC)
        rank = arena[:, 8308:8436].rearrange("p (e c) -> p e c", c=TC)
        weight = arena[:, 8436:8564].rearrange("p (c e) -> p c e", c=TC)
        cnt = arena[0:1, 8564:8628]
        cmax = arena[0:1, 8628:8660]
        npf = arena[0:1, 8660:8692]
        npass = arena[0:1, 8692:8724].bitcast(I32)
        rk = arena[:, 8724:8728]

        landed = [sem(f"landed{i}") for i in range(RING)]
        tiles_used = sem("tiles_used")
        c_in, consts_in, late_consts_in, x_in = sem("c_in"), sem("consts_in"), sem("late_consts_in"), sem("x_in")
        rows0_in, rowsA_in, rowsB_in = sem("rows0_in"), sem("rowsA_in"), sem("rowsB_in")
        pool_consts, pool_step = sem("pool_consts"), sem("pool_step")
        rows_zero = sem("rows_zero")
        c_silu, cb_ready = sem("c_silu"), sem("cb_ready")
        ada_done, bank_rows_read, rows_ready, row0_ready = (
            sem(n) for n in ("ada_done", "bank_rows_read", "rows_ready", "row0_ready"))
        mod_T_in = [sem(f"mod_T_in{n}") for n in range(4)]
        h_full = sem("h_full")
        rows0_turned, rows_stored = sem("rows0_turned"), sem("rows_stored")
        gate_and_moe_mods, last_gain = sem("gate_and_moe_mods"), sem("last_gain")
        sumsq, meansq, root, h_ready, h_turned, hT_act, hT_dve = (
            sem(n) for n in ("sumsq", "meansq", "root", "h_ready", "h_turned", "hT_act", "hT_dve"))
        proj_done, proj_out = sem("proj_done"), sem("proj_out")
        scored, s_ready, exp_done, a_ready, a_turned, aT_ready, pv_done, o_ready = (
            sem(n) for n in ("scored", "s_ready", "exp_done", "a_ready", "a_turned", "aT_ready", "pv_done", "o_ready"))
        o_meansq, o_root, o_normed, o_turned, oT_ready = (
            sem(n) for n in ("o_meansq", "o_root", "o_normed", "o_turned", "oT_ready"))
        o_sumsq = sem("o_sumsq")
        lam_sums, lam_exp = sem("lam_sums"), sem("lam_exp")
        decay_arg, decay_exp, decay_ready = sem("decay_arg"), sem("decay_exp"), sem("decay_ready")
        out_done, x_new = sem("out_done"), sem("x_new")
        part_hi, rest_ready, part_mid, parts_ready = (sem(n) for n in ("part_hi", "rest_ready", "part_mid", "parts_ready"))
        logits_done, scores_ready, chosen_ready, ranks_done, route_ready = (
            sem(n) for n in ("logits_done", "scores_ready", "chosen_ready", "ranks_done", "route_ready"))
        sh_up, sh_silu, sh_ready, sh_down = (sem(n) for n in ("sh_up", "sh_silu", "sh_ready", "sh_down"))
        U = [{n: sem(f"{n}{l}") for n in (
            "cols_ready", "onehot_ready", "gathered", "xg_lo", "xg_hi", "S_turned", "w_ready", "up_done", "silu_done",
            "eh_ready", "eh_turned", "ehT_ready", "combined", "S_ready", "down0", "down1", "y_hi", "bank0_read",
            "bank1_read", "y_mid", "y_ready")}
            for l in range(DEPTH)]
        routed_done = sem("routed_done")
        dve_step = sem("dve_step")
        written = sem("written")

        def tile_src(key):
            kind, l, i = key
            if kind == "ada":
                s, q = i // 4, i % 4
                return ada_w[l].rearrange("(p k) n -> p k n", k=KD)[:, :, s * D + q * 256:s * D + q * 256 + 256]
            if kind == "mix_in":
                w = (da_w_in if l == 0 else ret_w_in)[0]
                return w.rearrange("(p k) n -> p k n", k=KD)[:, :, i * 256:(i + 1) * 256]
            if kind == "mix_out":
                w = (da_w_out if l == 0 else ret_w_out)[0]
                return w[i * 256:(i + 1) * 256, :].rearrange("(b p) n -> p b n", p=P)
            w = (sh_w1, sh_w3, sh_w2)[i][l]
            return w.rearrange("(p k) n -> p k n", k=KD) if i < 2 else w.rearrange("(p b) n -> p b n", b=2)

        def slot(n):
            return ring[:, (n % RING) * TW:(n % RING + 1) * TW]

        def tile_in(n):
            return slot(n).rearrange("p (k n) -> p k n", k=KD)

        def tile_out(n):
            return slot(n).rearrange("p (b n) -> p b n", b=2)

        def arrived(eng, n):
            eng.wait_ge(landed[n % RING], 16 * loads[n])

        block = ctx.enter_context(nc.Block())

        @block.sync
        def _(sp):
            def one(n):
                if n >= RING:
                    sp.wait_ge(tiles_used, n - RING + 1)
                sp.dma_start(tile_in(n) if order[n][0] != "mix_out" and order[n][0:3:2] != ("shared", 2) else tile_out(n),
                             tile_src(order[n])).then_inc(landed[n % RING], 16)

            at = 0
            for l in range(DEPTH):
                for n in range(at, MOE0[l]):
                    if order[n][0] != "pad":
                        one(n)
                with sp.Fori(0, PAIRS // 2) as it:
                    for t in range(RING):
                        n = MOE0[l] + t
                        e = it * 4 + t // 3
                        sp.wait_ge(tiles_used, it * RING + (n - RING + 1))
                        w = (exp_w1, exp_w3, exp_w2)[t % 3][l][bass.ds(e, 1), :, :]
                        if t % 3 < 2:
                            sp.dma_start(tile_in(n), w.rearrange("o (p k) n -> p (o k) n", k=KD)).then_inc(landed[n % RING], 16)
                        else:
                            sp.dma_start(tile_out(n), w.rearrange("o (p b) n -> p (o b) n", b=2)).then_inc(landed[n % RING], 16)
                at = MOE0[l] + 3 * E

        @block.gpsimd
        def _(pool):
            steps = [0]

            def step(ins):
                ins.then_inc(pool_step, 1)
                steps[0] += 1
                pool.wait_ge(pool_step, steps[0])

            nc.gpsimd.memset(arena[:, 6912:7680], 0.0).then_inc(rows_zero, 1)
            nc.gpsimd.memset(arena[:, 8192:10240], 0.0).then_inc(rows_zero, 1)
            step(nc.gpsimd.memset(ident[:, :], 0.0))
            step(nc.gpsimd.affine_select(out=ident[:, :], in_=ident[:, :], compare_op=ALU.not_equal, fill=1.0, base=0,
                                         pattern=[[-1, P]], channel_multiplier=1))
            step(nc.gpsimd.memset(upper[:, :], 1.0))
            step(nc.gpsimd.affine_select(out=upper[:, :], in_=upper[:, :], compare_op=ALU.is_gt, fill=0.0, base=0,
                                         pattern=[[1, P]], channel_multiplier=-1))
            nc.gpsimd.memset(ones[:, :], 1.0)
            nc.gpsimd.tensor_copy(ident16[:, :], ident[:, :])
            step(nc.gpsimd.iota(dist[:, :], pattern=[[-1, T]], base=T - P, channel_multiplier=1,
                                allow_small_or_imprecise_dtypes=True))
            step(nc.gpsimd.affine_select(out=dist[:, :], in_=dist[:, :], compare_op=ALU.is_ge, fill=FAR, base=T - P,
                                         pattern=[[-1, T]], channel_multiplier=1))
            nc.gpsimd.iota(slot_no[:, :], pattern=[[1, SLOTS]], base=0, channel_multiplier=0,
                           allow_small_or_imprecise_dtypes=True)
            nc.gpsimd.iota(pass_base[:, :, :], pattern=[[-SLOTS, 4], [0, 4]], base=0, channel_multiplier=0,
                           allow_small_or_imprecise_dtypes=True)
            step(nc.gpsimd.memset(before[:, :, :], 1.0))
            step(nc.gpsimd.affine_select(out=before[:, :, :], in_=before[:, :, :], compare_op=ALU.is_gt, fill=0.0, base=0,
                                         pattern=[[1, GROUPS], [-1, GROUPS]], channel_multiplier=0))
            nc.gpsimd.memset(ret_s[:, :], 0.0).then_inc(pool_consts, 1)

            def store_rows(l, first, at, count):
                pool.wait_ge(rows_ready, at + count)
                for q in range(4):
                    pool.dma_start(mod_dram[l, first:first + count].rearrange("s (q n) -> q s n", q=4)[q:q + 1],
                                   mrow[32 * q:32 * q + 1, at:at + count, :]).then_inc(rows_stored, 16)

            def spread(l, first, count, done):
                for s in range(first, first + count):
                    pool.dma_start(mods[:, s, :], mod_dram[l, s:s + 1, :].broadcast_to([P, D])).then_inc(done, 16)

            def turn_mods(l, first):
                pool.dma_start(mod_T[:, l, first:first + 2, :],
                               mod_dram[l, first:first + 2].rearrange("s (p k) -> p s k", k=KD)
                               ).then_inc(mod_T_in[2 * l + first // 3], 16)

            for hd in range(RET_HEADS):
                nc.gpsimd.iota(decay[:, hd, :], pattern=[[1, T]], base=0, channel_multiplier=-1,
                               allow_small_or_imprecise_dtypes=True).then_inc(decay_arg, 1)
            pool.wait_ge(decay_exp, RET_HEADS)
            for hd in range(RET_HEADS):
                ins = nc.gpsimd.affine_select(out=decay[:, hd, :], in_=decay[:, hd, :], compare_op=ALU.is_ge, fill=0.0,
                                              base=0, pattern=[[1, T]], channel_multiplier=-1)
            ins.then_inc(decay_ready, 1)
            store_rows(1, 0, 0, 4)
            store_rows(0, 2, 4, 4)
            pool.wait_ge(rows_stored, 128)
            turn_mods(1, 0)
            turn_mods(0, 3)
            spread(0, 2, 4, gate_and_moe_mods)
            store_rows(1, 4, 8, 2)
            pool.wait_ge(rows_stored, 192)
            turn_mods(1, 3)
            pool.wait_ge(x_new, 2)
            spread(1, 2, 1, gate_and_moe_mods)

            for l in range(DEPTH):
                u = U[l]
                pool.wait_ge(route_ready, l + 1)
                unit = pool.alloc_register(f"pool_unit{l}")
                pool.reg_mov(unit, 0)
                with pool.Fori(0, PAIRS) as q:
                    n = pool.value_load(npass[0:1, bass.ds(q, 1)], min_val=1, max_val=4)
                    with pool.Fori(0, n) as i:
                        g = pool.snap(unit, min_val=0, max_val=127)
                        pool.wait_ge(u["S_turned"], g + 1)
                        nc.gpsimd.tensor_tensor(rk, rank.rearrange("p e c -> p (e c)")[:, bass.ds(q * 4, 4)],
                                                pass_base.rearrange("p a b -> p (a b)")[:, bass.ds(i * 4, 4)], ALU.add
                                                ).then_inc(u["cols_ready"], 1)
                        pool.wait_ge(u["cols_ready"], g + 1)
                        pool.reg_add(unit, unit, 1)
                        for j in range(2):
                            for tc in range(TC):
                                m = TC * j + tc
                                ins = nc.gpsimd.tensor_scalar(Pg[:, tc, SLOTS * j:SLOTS * (j + 1)], slot_no[:, :],
                                                              rk[:, m:m + 1], None, ALU.is_equal)
                        ins.then_inc(u["onehot_ready"], 1)
                if l == 0:
                    pool.wait_ge(x_new, 4)
                    spread(1, 3, 3, gate_and_moe_mods)
                    pool.dma_start(mods[:, 0, :], final_norm.rearrange("(a d) -> a d", a=1).broadcast_to([P, D])
                                   ).then_inc(last_gain, 16)

        @block.scalar
        def _(act):
            act.dma_start(cT[:, :], c.rearrange("o (p k) -> p (o k)", k=KD)).then_inc(c_in, 16)
            act.dma_start(X[:, :, :], x[0].rearrange("(c p) d -> p c d", p=P)).then_inc(x_in, 16)
            for i, v in enumerate((da_lq1, da_lk1, da_lq2, da_lk2)):
                act.dma_start(lvec[:, i, :], v.broadcast_to([P, DA_DH])).then_inc(consts_in, 16)
            act.dma_start(subg[:, :], da_subln.rearrange("a p -> p a"), allow_slow_non_contiguous=True).then_inc(consts_in, 16)
            act.wait_ge(rows_zero, 1)
            for q in range(4):
                act.dma_start(brow0[32 * q:32 * q + 1, :, :],
                              ada_b[0:1].rearrange("a (s q n) -> q a s n", s=6, q=4)[q, :, 0:2]).then_inc(rows0_in, 16)
                act.dma_start(nrow0[32 * q:32 * q + 1, 0, :], norm_mix[0:1, 256 * q:256 * (q + 1)]).then_inc(rows0_in, 16)

            act.wait_ge(c_in, 16)
            nc.scalar.activation(cs[:, :], cT[:, :], ACT.Silu).then_inc(c_silu, 1)

            def release(k):
                act.sem_inc(tiles_used, k)

            norms = [0]

            def norm_stats():
                n = norms[0]
                for tc in range(TC):
                    if n == 0:
                        act.wait_ge(x_in, 16)
                    else:
                        act.wait_ge(x_new, TC * (n - 1) + tc + 1)
                    nc.scalar.activation(h[:, tc, :], X[:, tc, :], ACT.Square, accum_out=ss[:, tc:tc + 1]
                                         ).then_inc(sumsq, 1)
                act.wait_ge(meansq, n + 1)
                nc.scalar.activation(rs[:, 0:TC], ss[:, 0:TC], ACT.Sqrt).then_inc(root, 1)
                norms[0] += 1

            def evict_hT():
                n = norms[0] - 1
                act.wait_ge(mod_T_in[n], 1 if n == 0 else 16)
                for m in (0, 2):
                    act.wait_ge(h_turned, 4 * n + m + 1)
                    for kk in range(2):
                        k = 2 * m + kk
                        ins = nc.scalar.activation(hT[:, k, :], banks[m][:, T * kk:T * kk + T], ACT.Identity,
                                                   scale=mod_T[:, n // 2, 3 * (n % 2) + 1, k:k + 1],
                                                   bias=mod_T[:, n // 2, 3 * (n % 2), k:k + 1])
                    ins.then_inc(hT_act, 1)

            norm_stats()
            for hd in range(RET_HEADS):
                log_g = math.log1p(-(2.0 ** (-5.0 - hd)))
                act.wait_ge(decay_arg, hd + 1)
                nc.scalar.activation(decay[:, hd, :], decay[:, hd, :], ACT.Exp, scale=log_g).then_inc(decay_exp, 1)
            act.wait_ge(lam_sums, 1)
            nc.scalar.activation(lexp[:, :], lsum[:, :], ACT.Exp).then_inc(lam_exp, 1)
            for s in range(2):
                act.wait_ge(ada_done, s + 1)
                release(4)
            act.dma_start(gn[:, :], ret_gn.rearrange("a (c p) -> p (a c)", p=P), allow_slow_non_contiguous=True
                          ).then_inc(late_consts_in, 16)
            for l in range(DEPTH):
                act.dma_start(rw[:, l, :, :], router_w[l].rearrange("(p k) e -> p k e", k=KD)).then_inc(late_consts_in, 16)
                act.dma_start(rb[:, l, :], router_b[l:l + 1, :].broadcast_to([P, E])).then_inc(late_consts_in, 16)
            act.wait_ge(rows_zero, 2)
            for q in range(4):
                act.dma_start(browB[32 * q:32 * q + 1, :, :],
                              ada_b[1:2].rearrange("a (s q n) -> q a s n", s=6, q=4)[q]).then_inc(rowsB_in, 16)
                for i, g in enumerate((norm_mix, norm_ffn)):
                    act.dma_start(nrowB[32 * q:32 * q + 1, i, :], g[1:2, 256 * q:256 * (q + 1)]).then_inc(rowsB_in, 16)
            proj = [0]

            def evict_proj(dst, func=None):
                act.wait_ge(proj_done, proj[0] + 1)
                src = banks[3 + proj[0] % 4][:, :].rearrange("p (m t) -> p m t", m=2)
                if func is None:
                    nc.scalar.copy(dst, src).then_inc(proj_out, 1)
                else:
                    nc.scalar.activation(dst, src, func).then_inc(proj_out, 1)
                proj[0] += 1
                release(1)

            def mixer_out(l, tiles):
                for i in range(tiles):
                    act.wait_ge(out_done, (0 if l == 0 else 4) + i + 1)
                    release(1)

            def moe(l):
                norm_stats()
                evict_hT()
                act.wait_ge(logits_done, l + 1)
                nc.scalar.activation(score, banks[2][:, 0:TC * E].rearrange("p (c e) -> p c e", c=TC), ACT.Sigmoid
                                     ).then_inc(scores_ready, 1)
                act.wait_ge(h_full, l + 1)
                nc.scalar.copy(parts[:, :, 0, :], h).then_inc(part_hi, 1)
                act.wait_ge(rest_ready, l + 1)
                nc.scalar.copy(parts[:, :, 1, :], h).then_inc(part_mid, 1)
                act.wait_ge(sh_up, l + 1)
                nc.scalar.activation(sg, banks[0][:, :], ACT.Silu).then_inc(sh_silu, 1)
                release(2)
                act.wait_ge(sh_down, l + 1)
                release(MOE0[l] - where["shared", l, 2])
                act.wait_ge(route_ready, l + 1)
                u = U[l]
                unit = act.alloc_register(f"act_unit{l}")
                act.reg_mov(unit, 0)
                with act.Fori(0, PAIRS) as q:
                    n = act.value_load(npass[0:1, bass.ds(q, 1)], min_val=1, max_val=4)
                    with act.Fori(0, n) as i:
                        g = act.snap(unit, min_val=0, max_val=127)
                        act.wait_ge(u["gathered"], g * 2 + 1)
                        nc.scalar.copy(xg[:, 0:4, :], banks[2][:, :].rearrange("p (k n) -> p k n", k=4)).then_inc(u["xg_lo"], 1)
                        act.wait_ge(u["up_done"], g + 1)
                        nc.scalar.activation(sg[:, 0:256], banks[1][:, 0:256], ACT.Silu).then_inc(u["silu_done"], 1)
                        act.wait_ge(u["eh_turned"], g + 1)
                        nc.scalar.copy(ehT, banks[2][:, 0:256].rearrange("p (b n) -> p b n", b=2)).then_inc(u["ehT_ready"], 1)
                        for hf in range(NH):
                            act.wait_ge(u[f"down{hf}"], g + 1)
                            nc.scalar.copy(y[:, 0, 512 * hf:512 * hf + 512], banks[hf][:, :]).then_inc(u["y_hi"], 1)
                        for hf in range(NH):
                            act.wait_ge(u[f"bank{hf}_read"], g + 2)
                            nc.scalar.copy(y[:, 1, 512 * hf:512 * hf + 512], y_rest[:, hf, :]).then_inc(u["y_mid"], 1)
                        act.reg_add(unit, unit, 1)

            def evict_aT(n):
                act.wait_ge(a_turned, n + 1)
                W = P * (1 + n % 2)
                nc.scalar.copy(da_aT[:, n % 2, 0:1 + n % 2, :], banks[5 + n % 2][:, 0:W].rearrange("p (b q) -> p b q", q=P)
                               ).then_inc(aT_ready, 1)

            evict_hT()
            for i in range(12):
                if i < 4:
                    evict_proj(qT[:, 2 * i:2 * i + 2, :])
                elif i < 8:
                    evict_proj(kT[:, 2 * (i - 4):2 * (i - 4) + 2, :])
                else:
                    evict_proj(da_v[:, :, 256 * (i - 8):256 * (i - 7)])
                if i in AT_PROJ:
                    act.wait_ge(ada_done, 2 + AT_PROJ.index(i) + 1)
                    release(4)
            for q in range(4):
                act.dma_start(browA[32 * q:32 * q + 1, :, :],
                              ada_b[0:1].rearrange("a (s q n) -> q a s n", s=6, q=4)[q, :, 2:6]).then_inc(rowsA_in, 16)
                act.dma_start(nrowA[32 * q:32 * q + 1, 0, :], norm_ffn[0:1, 256 * q:256 * (q + 1)]).then_inc(rowsA_in, 16)
            for n in range(2 * DA_HEADS):
                W = P * (1 + n % 2)
                if n >= 2 and n - 2 in AT_ITEM:
                    act.wait_ge(ada_done, 6 + AT_ITEM.index(n - 2) + 1)
                    release(4)
                act.wait_ge(s_ready, n + 1)
                for m in range(2):
                    nc.scalar.activation(da_s[:, n % 2, m, 0:W], da_s[:, n % 2, m, 0:W], ACT.Exp, scale=0.125,
                                         bias=soft[:, 0, n, m:m + 1], accum_out=soft[:, 1, n, m:m + 1]).then_inc(exp_done, 1)
                if n >= 1:
                    evict_aT(n - 1)
            evict_aT(2 * DA_HEADS - 1)
            for k, at in enumerate(AT_ITEM):
                if at >= DA_ITEMS - 2:
                    act.wait_ge(ada_done, 6 + k + 1)
                    release(4)
            act.wait_ge(o_meansq, 1)
            nc.scalar.activation(rs[:, :], ss[:, :], ACT.Sqrt).then_inc(o_root, 1)
            for m in range(4):
                act.wait_ge(o_turned, m + 1)
                nc.scalar.activation(da_oT[:, 2 * m:2 * m + 2, :], banks[m][:, :].rearrange("p (k t) -> p k t", k=2),
                                     ACT.Copy, scale=subs[:, 0:1]).then_inc(oT_ready, 1)
            mixer_out(0, 4)
            moe(0)

            norm_stats()
            evict_hT()
            for i in range(24):
                if i < 4:
                    evict_proj(qT[:, 2 * i:2 * i + 2, :])
                elif i < 8:
                    evict_proj(kT[:, 2 * (i - 4):2 * (i - 4) + 2, :])
                elif i < 16:
                    evict_proj(ret_v[:, :, 256 * (i - 8):256 * (i - 7)])
                else:
                    evict_proj(ret_sg[:, 2 * (i - 16):2 * (i - 16) + 2, :], ACT.Silu)
            for n in range(2 * RET_HEADS):
                hd, qb = n // 2, n % 2
                act.wait_ge(pv_done, DA_ITEMS + n + 1)
                if n >= 1:
                    act.wait_ge(o_sumsq, n)
                nc.scalar.activation(ret_junk, banks[5 + n % 2][:, :], ACT.Square, accum_out=ss[:, n:n + 1]
                                     ).then_inc(o_sumsq, 1)
                nc.scalar.copy(ret_o[:, qb, hd, :], banks[5 + n % 2][:, :]).then_inc(o_ready, 1)
            act.wait_ge(o_meansq, 2)
            nc.scalar.activation(rs[:, 0:8], ss[:, 0:8], ACT.Sqrt).then_inc(o_root, 1)
            mixer_out(1, 8)
            moe(1)
            norm_stats()
            for tc in range(TC):
                act.wait_ge(h_ready, 2 * 4 + tc + 1)
                act.dma_start(out[0, P * tc:P * (tc + 1), :], h[:, tc, :]).then_inc(written, 16)
            act.wait_ge(written, 16 * TC)

        @block.tensor
        def _(pe):
            def ada(l, s, bank):
                tiles = [where["ada", l, 4 * s + q] for q in range(4)]
                for n in tiles:
                    arrived(pe, n)
                for k in range(KD):
                    for q in range(4):
                        ins = nc.tensor.matmul(bank[32 * q:32 * q + 32, :],
                                               cb[:, k, :], tile_in(tiles[q])[:, k, :], start=(k == 0), stop=(k == KD - 1))
                ins.then_inc(ada_done, 1)

            norms = [0]

            def turn_h():
                pe.wait_ge(h_ready, TC * (norms[0] + 1))
                for m in range(4):
                    for kk in range(2):
                        for tc in range(TC):
                            ins = nc.tensor.transpose(
                                banks[m][:, T * kk + P * tc:T * kk + P * tc + P],
                                h[:, tc, :].rearrange("t (p k) -> t k p", k=KD)[:, 2 * m + kk, :], ident[:, :])
                    ins.then_inc(h_turned, 1)
                norms[0] += 1

            def hT_there():
                pe.wait_ge(hT_act, 2 * norms[0])
                pe.wait_ge(hT_dve, 2 * norms[0])

            proj = [0]

            def project(l, i, token_major):
                n = where["mix_in", l, i]
                arrived(pe, n)
                if proj[0] >= 4:
                    pe.wait_ge(proj_out, proj[0] - 3)
                bank, w = banks[3 + proj[0] % 4], tile_in(n)
                for m in range(2):
                    for k in range(KD):
                        tokens, columns = hT[:, k, P * m:P * m + P], w[:, k, P * m:P * m + P]
                        a, b = (tokens, w[:, k, :]) if token_major else (columns, hT[:, k, :])
                        ins = nc.tensor.matmul(bank[:, 256 * m:256 * m + 256], a, b, start=(k == 0), stop=(k == KD - 1))
                ins.then_inc(proj_done, 1)
                proj[0] += 1

            def mix_out(l, tiles, src):
                for i in range(tiles):
                    arrived(pe, where["mix_out", l, i])
                    w = tile_out(where["mix_out", l, i])
                    if l == 1:
                        pe.wait_ge(oT_ready, 4 + 2 * (i + 1))
                    for b in range(2):
                        for tc in range(TC):
                            for hf in range(NH):
                                ins = nc.tensor.matmul(banks[4 + NH * tc + hf][:, :], src[:, 2 * i + b, P * tc:P * tc + P],
                                                       w[:, b, 512 * hf:512 * hf + 512], start=(i == 0 and b == 0),
                                                       stop=(i == tiles - 1 and b == 1), skip_group_check=True)
                    ins.then_inc(out_done, 1)

            def moe(l):
                turn_h()
                hT_there()
                pe.wait_ge(late_consts_in, 16 * 5)
                for tc in range(TC):
                    for k in range(KD):
                        ins = nc.tensor.matmul(banks[2][:, E * tc:E * tc + E], hT[:, k, P * tc:P * tc + P], rw[:, l, k, :],
                                               start=(k == 0), stop=(k == KD - 1))
                ins.then_inc(logits_done, 1)
                for i in range(2):
                    arrived(pe, where["shared", l, i])
                    w = tile_in(where["shared", l, i]).rearrange("p k (m b) -> p k b m", b=2)
                    for b in range(2):
                        for k in range(KD):
                            ins = nc.tensor.matmul(banks[i][:, 256 * b:256 * b + 256], w[:, k, b, :], hT[:, k, :],
                                                   start=(k == 0), stop=(k == KD - 1))
                ins.then_inc(sh_up, 1)
                pe.wait_ge(chosen_ready, l + 1)
                nc.tensor.matmul(banks[3][:, 0:E], upper[:, :], mb[:, 0, :], start=True, stop=True)
                nc.tensor.matmul(banks[3][:, E:2 * E], ones[:, :], mb[:, 0, :], start=True, stop=False)
                nc.tensor.matmul(banks[3][:, E:2 * E], upper[:, :], mb[:, 1, :], start=False, stop=True)
                nc.tensor.matmul(banks[3][0:1, 2 * E:3 * E], ones[:, 0:1], mb[:, 0, :], start=True, stop=False)
                nc.tensor.matmul(banks[3][0:1, 2 * E:3 * E], ones[:, 0:1], mb[:, 1, :], start=False, stop=True
                                 ).then_inc(ranks_done, 1)
                pe.wait_ge(sh_ready, l + 1)
                arrived(pe, where["shared", l, 2])
                w = tile_out(where["shared", l, 2])
                for tc in range(TC):
                    for hf in range(NH):
                        for b in range(2):
                            ins = nc.tensor.matmul(banks[4 + NH * tc + hf][:, :], shT[:, b, P * tc:P * tc + P],
                                                   w[:, b, 512 * hf:512 * hf + 512], start=(b == 0), stop=False,
                                                   skip_group_check=True)
                ins.then_inc(sh_down, 1)

                u = U[l]

                def combine(tc, last=False):
                    for hf in range(NH):
                        for r in range(3):
                            ins = nc.tensor.matmul(banks[4 + NH * tc + hf][:, :], S[:, P * tc:P * tc + P],
                                                   y[:, r, 512 * hf:512 * hf + 512], start=False, stop=(last and r == 2),
                                                   skip_group_check=True)
                    return ins

                pe.wait_ge(parts_ready, l + 1)
                pe.wait_ge(route_ready, l + 1)
                unit = pe.alloc_register(f"pe_unit{l}")
                pe.reg_mov(unit, 0)
                with pe.Fori(0, PAIRS // 2) as it:
                    for pair in range(2):
                        t0 = MOE0[l] + 6 * pair
                        s0 = [(t0 + 3 * j) % RING for j in range(2)]
                        w13 = [ring[:, s0[j] * TW:(s0[j] + 2) * TW].rearrange("p (w k n) -> p k w n", w=2, k=KD) for j in range(2)]
                        w2 = [tile_out(t0 + 3 * j + 2) for j in range(2)]

                        def arrived_now(t):
                            pe.wait_ge(landed[(t0 + t) % RING], it * 16 + 16 * loads[t0 + t])

                        n = pe.value_load(npass[0:1, bass.ds(it * 2 + pair, 1)], min_val=1, max_val=4)
                        with pe.Fori(0, n):
                            g = pe.snap(unit, min_val=0, max_val=127)
                            pe.wait_ge(u["onehot_ready"], g + 1)
                            for half in range(2):
                                if half == 1:
                                    pe.wait_ge(u["bank0_read"], g + 1)
                                for kk in range(4):
                                    for tc in range(TC):
                                        for r in range(3):
                                            ins = nc.tensor.matmul(
                                                banks[2 - 2 * half][:, P * kk:P * kk + P],
                                                parts[:, tc, r, :].rearrange("t (p k) -> t k p", k=KD)[:, 4 * half + kk, :],
                                                Pg[:, tc, :], start=(tc == 0 and r == 0), stop=(tc == TC - 1 and r == 2))
                                ins.then_inc(u["gathered"], 1)
                            pe.wait_ge(u["S_ready"], g + 1)
                            for tc in range(TC):
                                nc.tensor.matmul(banks[3][:, P * tc:P * tc + P], Pg[:, tc, :], ident16[:, :],
                                                 start=True, stop=True)
                            for tc in range(TC):
                                ins = nc.tensor.matmul(
                                    banks[3][:, T:T + 6], Pg[:, tc, :],
                                    wparts[:, tc].rearrange("p e r -> p (e r)")[:, bass.ds(it * 12 + 6 * pair, 6)],
                                    start=(tc == 0), stop=(tc == TC - 1))
                            ins.then_inc(u["S_turned"], 1)
                            pe.wait_ge(u["bank1_read"], g + 1)
                            for k in range(KD):
                                if k % 4 == 0:
                                    pe.wait_ge(u["xg_lo" if k == 0 else "xg_hi"], g + 1)
                                for j in range(2):
                                    if k == 0:
                                        arrived_now(3 * j)
                                        arrived_now(3 * j + 1)
                                    ins = nc.tensor.matmul(banks[1][SLOTS * j:SLOTS * (j + 1), :],
                                                           xg[:, k, SLOTS * j:SLOTS * (j + 1)], w13[j][:, k, :, :],
                                                           start=(k == 0), stop=(k == KD - 1))
                            ins.then_inc(u["up_done"], 1)
                            pe.wait_ge(u["y_ready"], g * 2 + 1)
                            combine(0)
                            pe.wait_ge(u["eh_ready"], g + 1)
                            for b in range(2):
                                ins = nc.tensor.transpose(banks[2][:, P * b:P * b + P], eh[:, b, :], ident[:, :])
                            ins.then_inc(u["eh_turned"], 1)
                            combine(1).then_inc(u["combined"], 1)
                            pe.wait_ge(u["ehT_ready"], g + 1)
                            for hf in range(NH):
                                for b in range(2):
                                    for j in range(2):
                                        if hf == 0 and b == 0:
                                            arrived_now(3 * j + 2)
                                        ins = nc.tensor.matmul(banks[hf][SLOTS * j:SLOTS * (j + 1), :],
                                                               ehT[:, b, SLOTS * j:SLOTS * (j + 1)],
                                                               w2[j][:, b, 512 * hf:512 * hf + 512], start=(b == 0), stop=(b == 1))
                                ins.then_inc(u["down0" if hf == 0 else "down1"], 1)
                            pe.reg_add(unit, unit, 1)
                total = pe.snap(unit, min_val=PAIRS, max_val=128)
                pe.wait_ge(u["S_ready"], total + 1)
                pe.wait_ge(u["y_ready"], total * 2 + 1)
                combine(0, last=True).then_inc(routed_done, 1)
                combine(1, last=True).then_inc(routed_done, 1)

            pe.wait_ge(pool_consts, 1)
            turn_h()
            pe.wait_ge(cb_ready, 1)
            for s in range(2):
                ada(0, s, banks[4][:, 256 * s:256 * s + 256])
            pe.wait_ge(row0_ready, 2)
            for s in range(2):
                for k in range(KD):
                    for q in range(4):
                        ins = nc.tensor.matmul(banks[5][32 * q:32 * q + 32, KD * s + k:KD * s + k + 1],
                                               mrow0[:, s, k:256:KD], ident[:, 32 * q:32 * q + 1], start=True, stop=True)
            ins.then_inc(rows0_turned, 1)

            def later(k):
                if k >= 2:
                    pe.wait_ge(bank_rows_read, k - 1)
                ada(*LATER[k], banks[7 * (1 - k % 2)][:, 0:256])

            hT_there()
            for i in range(12):
                project(0, i, token_major=(i >= 8))
                if i in AT_PROJ:
                    later(AT_PROJ.index(i))
            pe.wait_ge(proj_out, 12)

            def scores(n):
                hd, qb = n // 2, n % 2
                if n >= 2:
                    pe.wait_ge(s_ready, n - 1)
                for m in range(2):
                    ins = nc.tensor.matmul(banks[1 + 2 * (n % 2) + m][:, 0:P * (1 + qb)],
                                           qT[64 * m:64 * m + 64, hd, P * qb:P * qb + P],
                                           kT[64 * m:64 * m + 64, hd, 0:P * (1 + qb)], start=True, stop=True)
                ins.then_inc(scored, 1)

            def turn_a(n):
                pe.wait_ge(a_ready, n + 1)
                if n >= 2:
                    pe.wait_ge(o_ready, n - 1)
                for kb in range(1 + n % 2):
                    ins = nc.tensor.transpose(banks[5 + n % 2][:, P * kb:P * kb + P], da_a[:, n % 2, P * kb:P * kb + P], ident[:, :])
                ins.then_inc(a_turned, 1)

            def attend(n):
                hd, qb = n // 2, n % 2
                pe.wait_ge(aT_ready, n + 1)
                for kb in range(1 + qb):
                    ins = nc.tensor.matmul(banks[5 + n % 2][:, T:T + P], da_aT[:, n % 2, kb, :], da_v[:, kb, P * hd:P * hd + P],
                                           start=(kb == 0), stop=(kb == qb))
                ins.then_inc(pv_done, 1)

            scores(0)
            scores(1)
            for n in range(DA_ITEMS):
                if n + 2 < DA_ITEMS:
                    scores(n + 2)
                turn_a(n)
                if n >= 1:
                    attend(n - 1)
                if n == DA_ITEMS - 1:
                    attend(n)
                if n in AT_ITEM:
                    later(4 + AT_ITEM.index(n))
            pe.wait_ge(o_normed, 1)
            pe.wait_ge(bank_rows_read, len(LATER))
            for m in range(4):
                for hh in range(2):
                    for tc in range(TC):
                        ins = nc.tensor.transpose(banks[m][:, T * hh + P * tc:T * hh + P * tc + P], da_o[:, tc, 2 * m + hh, :], ident[:, :])
                ins.then_inc(o_turned, 1)
            pe.wait_ge(oT_ready, 4)
            mix_out(0, 4, da_oT)
            moe(0)

            turn_h()
            hT_there()
            for i in range(24):
                project(1, i, token_major=(8 <= i < 16))
            pe.wait_ge(proj_out, 36)

            def ret_scores(hd):
                if hd >= 2:
                    pe.wait_ge(s_ready, DA_ITEMS + hd - 1)
                bank = banks[hd % 2]
                for kk in range(2):
                    nc.tensor.matmul(bank[:, 0:T], kT[:, 2 * hd + kk, 0:P], qT[:, 2 * hd + kk, :], start=(kk == 0), stop=(kk == 1))
                for kk in range(2):
                    ins = nc.tensor.matmul(bank[:, T:T + P], kT[:, 2 * hd + kk, P:T], qT[:, 2 * hd + kk, P:T],
                                           start=(kk == 0), stop=(kk == 1))
                ins.then_inc(scored, 1)

            def ret_attend(hd):
                pe.wait_ge(s_ready, DA_ITEMS + hd + 1)
                v = [ret_v[:, jb, 512 * hd:512 * hd + 512] for jb in range(2)]
                if hd >= 1:
                    pe.wait_ge(o_ready, DA_ITEMS + 2 * hd - 1)
                nc.tensor.matmul(banks[5][:, :], ret_s[:, 0:P], v[0], start=True, stop=True).then_inc(pv_done, 1)
                if hd >= 1:
                    pe.wait_ge(o_ready, DA_ITEMS + 2 * hd)
                nc.tensor.matmul(banks[6][:, :], ret_s[:, P:T], v[0], start=True, stop=False)
                nc.tensor.matmul(banks[6][:, :], ret_s[:, T:T + P], v[1], start=False, stop=True).then_inc(pv_done, 1)

            ret_scores(0)
            for hd in range(RET_HEADS):
                if hd + 1 < RET_HEADS:
                    ret_scores(hd + 1)
                ret_attend(hd)
            pe.wait_ge(o_normed, 2)
            for ch in range(16):
                if ch >= 8:
                    pe.wait_ge(oT_ready, 4 + 2 * (ch // 2) - 6)
                for tc in range(TC):
                    ins = nc.tensor.transpose(banks[(ch // 2) % 4][:, T * (ch % 2) + P * tc:T * (ch % 2) + P * tc + P],
                                              ret_o[:, tc, ch // 4, P * (ch % 4):P * (ch % 4) + P], ident[:, :])
                if ch % 2:
                    ins.then_inc(o_turned, 1)
            mix_out(1, 8, ret_yT)
            moe(1)

        @block.vector
        def _(dve):
            steps = [0]

            def step(ins):
                ins.then_inc(dve_step, 1)
                steps[0] += 1
                dve.wait_ge(dve_step, steps[0])

            dve.wait_ge(c_silu, 1)
            nc.vector.tensor_copy(cb[:, :, :], cs[:, :].unsqueeze(2).to_broadcast([P, KD, 32])).then_inc(cb_ready, 1)
            dve.wait_ge(consts_in, 16 * 5)
            step(nc.vector.tensor_tensor(lprod, lvec[:, 0:4:2, :], lvec[:, 1:4:2, :], ALU.mult))
            nc.vector.tensor_reduce(lsum[:, :], lprod, AX_X, ALU.add).then_inc(lam_sums, 1)
            nc.vector.tensor_scalar(subs[:, :], subg[:, :], 1.0 - LAM_INIT, None, ALU.mult)

            norms = [0]

            def norm_root(last=False):
                n = norms[0]
                dve.wait_ge(sumsq, TC * (n + 1))
                nc.vector.tensor_scalar(ss[:, 0:TC], ss[:, 0:TC], 1.0 / D, EPS, ALU.mult, ALU.add).then_inc(meansq, 1)
                dve.wait_ge(root, n + 1)
                step(nc.vector.reciprocal(rs[:, 0:TC], rs[:, 0:TC]))

                if not last:
                    for tc in range(TC):
                        nc.vector.tensor_scalar(h[:, tc, :], X[:, tc, :], rs[:, tc:tc + 1], None, ALU.mult).then_inc(h_ready, 1)
                norms[0] += 1

            def evict_hT():
                n = norms[0] - 1
                dve.wait_ge(mod_T_in[n], 1 if n == 0 else 16)
                for m in (1, 3):
                    dve.wait_ge(h_turned, 4 * n + m + 1)
                    for kk in range(2):
                        k = 2 * m + kk
                        ins = nc.vector.tensor_scalar(hT[:, k, :], banks[m][:, T * kk:T * kk + T],
                                                      mod_T[:, n // 2, 3 * (n % 2) + 1, k:k + 1],
                                                      mod_T[:, n // 2, 3 * (n % 2), k:k + 1], ALU.mult, ALU.add)
                    ins.then_inc(hT_dve, 1)

            def update_x(gate, done, at):
                for tc in range(TC):
                    dve.wait_ge(done, at[tc])
                    for hf in range(NH):
                        ins = nc.vector.tensor_tensor(h[:, tc, 512 * hf:512 * hf + 512], banks[4 + NH * tc + hf][:, :],
                                                      mods[:, gate, 512 * hf:512 * hf + 512], ALU.mult)
                    step(ins)
                    ins = nc.vector.tensor_tensor(X[:, tc, :], X[:, tc, :], h[:, tc, :], ALU.add).then_inc(x_new, 1)

            def moe(l):
                norm_root()
                evict_hT()
                dve.wait_ge(h_turned, 4 * norms[0])
                dve.wait_ge(gate_and_moe_mods, 64 if l == 0 else 128)
                for tc in range(TC):
                    ins = nc.vector.tensor_tensor(h[:, tc, :], h[:, tc, :], mods[:, 4, :], ALU.mult)
                step(ins)
                for tc in range(TC):
                    ins = nc.vector.tensor_tensor(h[:, tc, :], h[:, tc, :], mods[:, 3, :], ALU.add)
                ins.then_inc(h_full, 1)
                dve.wait_ge(h_full, l + 1)
                dve.wait_ge(part_hi, l + 1)
                nc.vector.tensor_tensor(h, h, parts[:, :, 0, :], ALU.subtract).then_inc(rest_ready, 1)
                dve.wait_ge(rest_ready, l + 1)
                dve.wait_ge(part_mid, l + 1)
                nc.vector.tensor_tensor(parts[:, :, 2, :], h, parts[:, :, 1, :], ALU.subtract).then_inc(parts_ready, 1)
                dve.wait_ge(scores_ready, l + 1)
                dve.wait_ge(late_consts_in, 16 * 5)
                step(nc.vector.tensor_tensor(choice, score, rb[:, l:l + 1, :].to_broadcast([P, TC, E]), ALU.add))
                for tc in range(TC):
                    for gr in range(GROUPS):
                        ins = nc.vector.max(top[:, tc * GROUPS + gr, :], choice[:, tc, 8 * gr:8 * gr + 8])
                step(ins)
                step(nc.vector.tensor_tensor(gs.rearrange("p c g -> p (c g)").unsqueeze(2), top[:, :, 0:1], top[:, :, 1:2], ALU.add))
                other = gs.unsqueeze(2).to_broadcast([P, TC, GROUPS, GROUPS])
                own = gs.unsqueeze(3).to_broadcast([P, TC, GROUPS, GROUPS])
                nc.vector.tensor_tensor(cmp1, other, own, ALU.is_gt)
                step(nc.vector.tensor_tensor(cmp2, other, own, ALU.is_equal))
                for tc in range(TC):
                    ins = nc.vector.tensor_tensor(cmp2[:, tc, :, :], cmp2[:, tc, :, :], before[:, :, :], ALU.mult)
                step(ins)
                step(nc.vector.tensor_tensor(cmp1, cmp1, cmp2, ALU.add))
                step(nc.vector.tensor_reduce(grank, cmp1, AX_X, ALU.add))
                step(nc.vector.tensor_scalar(grank, grank, TOPG - 0.5, -FAR, ALU.is_gt, ALU.mult))
                step(nc.vector.tensor_tensor(masked.rearrange("p c (g m) -> p (c g) m", m=8),
                                             choice.rearrange("p c (g m) -> p (c g) m", m=8),
                                             grank.rearrange("p c g -> p (c g)").unsqueeze(2).to_broadcast([P, TC * GROUPS, 8]),
                                             ALU.add))
                for tc in range(TC):
                    ins = nc.vector.max(top8[:, tc, :], masked[:, tc, :])
                step(ins)
                for tc in range(TC):
                    ins = nc.vector.match_replace(chosen[:, tc, :], top8[:, tc, :], masked[:, tc, :], -3e38)
                step(ins)
                step(nc.vector.tensor_tensor(chosen, chosen, masked, ALU.not_equal))
                nc.vector.tensor_copy(mb, chosen).then_inc(chosen_ready, 1)
                step(nc.vector.tensor_tensor(masked, score, chosen, ALU.mult))
                step(nc.vector.tensor_reduce(wsum, masked, AX_X, ALU.add))
                step(nc.vector.reciprocal(winv, wsum))
                for tc in range(TC):
                    ins = nc.vector.tensor_scalar(weight[:, tc, :], masked[:, tc, :], winv[:, tc:tc + 1], ROUTED_SCALE,
                                                  ALU.mult, ALU.mult)
                step(ins)
                step(nc.vector.tensor_copy(wparts[:, :, :, 0], weight))
                step(nc.vector.tensor_tensor(wrest, weight, wparts[:, :, :, 0], ALU.subtract))
                step(nc.vector.tensor_copy(wparts[:, :, :, 1], wrest))
                nc.vector.tensor_tensor(wparts[:, :, :, 2], wrest, wparts[:, :, :, 1], ALU.subtract)
                u = U[l]
                nc.vector.memset(S, 0.0).then_inc(u["S_ready"], 1)
                nc.vector.memset(y, 0.0).then_inc(u["y_ready"], 1)
                nc.vector.memset(w_slot, 0.0).then_inc(u["S_turned"], 1)
                nc.vector.memset(y_rest[:, 0, 0:1], 0.0).then_inc(u["bank0_read"], 1)
                nc.vector.memset(y_rest[:, 1, 0:1], 0.0).then_inc(u["bank1_read"], 1)
                dve.wait_ge(sh_silu, l + 1)
                nc.vector.tensor_tensor(shT, sg.rearrange("p (b t) -> p b t", b=2),
                                        banks[1][:, :].rearrange("p (b t) -> p b t", b=2), ALU.mult).then_inc(sh_ready, 1)
                dve.wait_ge(ranks_done, l + 1)
                nc.vector.scalar_tensor_tensor(out=choice, in0=banks[3][:, 0:TC * E].rearrange("p (c e) -> p c e", c=TC),
                                               scalar=1.0, in1=chosen, op0=ALU.add, op1=ALU.mult)
                step(nc.vector.tensor_copy(cnt, banks[3][0:1, 2 * E:3 * E]))
                nc.vector.tensor_scalar(rank.rearrange("p e c -> p c e"), choice, -1.0, None, ALU.add)
                pairs = cnt.rearrange("a (q j) -> a j q", j=2)
                step(nc.vector.tensor_tensor(cmax, pairs[:, 0, :], pairs[:, 1, :], ALU.max))
                step(nc.vector.tensor_scalar(npf, cmax, float(SLOTS), 1.0, ALU.is_gt, ALU.add))
                step(nc.vector.scalar_tensor_tensor(out=npf, in0=cmax, scalar=2.0 * SLOTS, in1=npf, op0=ALU.is_gt, op1=ALU.add))
                nc.vector.scalar_tensor_tensor(out=npass, in0=cmax, scalar=3.0 * SLOTS, in1=npf, op0=ALU.is_gt, op1=ALU.add
                                               ).then_inc(route_ready, 1)
                dve.wait_ge(route_ready, l + 1)
                unit = dve.alloc_register(f"dve_unit{l}")
                dve.reg_mov(unit, 0)
                with dve.Fori(0, PAIRS) as q:
                    n = dve.value_load(npass[0:1, bass.ds(q, 1)], min_val=1, max_val=4)
                    with dve.Fori(0, n):
                        g = dve.snap(unit, min_val=0, max_val=127)
                        dve.wait_ge(u["gathered"], g * 2 + 2)
                        nc.vector.tensor_copy(xg[:, 4:8, :], banks[0][:, :].rearrange("p (k n) -> p k n", k=4)
                                              ).then_inc(u["xg_hi"], 1)
                        dve.wait_ge(u["S_turned"], g + 2)
                        for j in range(2):
                            nc.vector.tensor_reduce(w_slot[SLOTS * j:SLOTS * (j + 1), :],
                                                    banks[3][SLOTS * j:SLOTS * (j + 1), T + 3 * j:T + 3 * j + 3], AX_X, ALU.add
                                                    ).then_inc(u["w_ready"], 1)
                        dve.wait_ge(u["w_ready"], g * 2 + 2)
                        dve.wait_ge(u["silu_done"], g + 1)
                        nc.vector.scalar_tensor_tensor(out=eh.rearrange("p b n -> p n b"),
                                                       in0=banks[1][:, 256:512].rearrange("p (n b) -> p n b", b=2),
                                                       scalar=w_slot, in1=sg[:, 0:256].rearrange("p (n b) -> p n b", b=2),
                                                       op0=ALU.mult, op1=ALU.mult).then_inc(u["eh_ready"], 1)
                        dve.wait_ge(u["combined"], g + 1)
                        nc.vector.tensor_copy(S, banks[3][:, 0:T]).then_inc(u["S_ready"], 1)
                        for hf in range(NH):
                            dve.wait_ge(u["y_hi"], g * 2 + hf + 1)
                            nc.vector.tensor_tensor(y_rest[:, hf, :], banks[hf][:, :], y[:, 0, 512 * hf:512 * hf + 512],
                                                    ALU.subtract).then_inc(u[f"bank{hf}_read"], 1)
                        for hf in range(NH):
                            dve.wait_ge(u["y_mid"], g * 2 + hf + 1)
                            nc.vector.tensor_tensor(y[:, 2, 512 * hf:512 * hf + 512], y_rest[:, hf, :],
                                                    y[:, 1, 512 * hf:512 * hf + 512], ALU.subtract).then_inc(u["y_ready"], 1)
                        dve.reg_add(unit, unit, 1)
                    dve.sem_inc(tiles_used, 6)
                update_x(5, routed_done, (2 * l + 1, 2 * l + 2))

            norm_root()
            dve.wait_ge(lam_exp, 1)
            step(nc.vector.tensor_tensor(nlam[:, :], lexp[:, 1:2], lexp[:, 0:1], ALU.subtract))
            step(nc.vector.tensor_scalar(nlam[:, :], nlam[:, :], -LAM_INIT, None, ALU.add))
            dve.wait_ge(rows0_in, 16 * 8)
            dve.wait_ge(ada_done, 2)
            step(nc.vector.tensor_tensor(mrow0[:, 1, :], banks[4][:, 256:512], brow0[:, 1, :], ALU.add))
            nc.vector.scalar_tensor_tensor(out=mrow0[:, 1, :], in0=mrow0[:, 1, :], scalar=1.0, in1=nrow0[:, 0, :],
                                           op0=ALU.add, op1=ALU.mult).then_inc(row0_ready, 1)
            nc.vector.tensor_tensor(mrow0[:, 0, :], banks[4][:, 0:256], brow0[:, 0, :], ALU.add).then_inc(row0_ready, 1)
            dve.wait_ge(rows0_turned, 1)
            nc.vector.tensor_copy(mod_T[:, 0, 0:2, :], banks[5][:, 0:2 * KD].rearrange("p (s k) -> p s k", s=2)
                                  ).then_inc(mod_T_in[0], 1)
            evict_hT()

            def later_rows(k):
                l, sec = LATER[k]
                if k == 0:
                    dve.wait_ge(rowsB_in, 16 * 12)
                if k == 4:
                    dve.wait_ge(rowsA_in, 16 * 8)
                bias = browA[:, sec - 2, :] if l == 0 else browB[:, sec, :]
                dve.wait_ge(ada_done, 2 + k + 1)
                ins = nc.vector.tensor_tensor(mrow[:, k, :], banks[7 * (1 - k % 2)][:, 0:256], bias, ALU.add)
                ins.then_inc(bank_rows_read, 1)
                dve.wait_ge(bank_rows_read, k + 1)
                if sec % 3 == 1:
                    gain = nrowA[:, 0, :] if l == 0 else nrowB[:, sec // 3, :]
                    nc.vector.scalar_tensor_tensor(out=mrow[:, k, :], in0=mrow[:, k, :], scalar=1.0, in1=gain,
                                                   op0=ALU.add, op1=ALU.mult).then_inc(rows_ready, 1)
                else:
                    dve.sem_inc(rows_ready, 1)

            for k in range(4):
                later_rows(k)

            def finish_a(n):
                W = P * (1 + n % 2)
                dve.wait_ge(exp_done, 2 * n + 2)
                step(nc.vector.reciprocal(soft[:, 2, n, :], soft[:, 1, n, :]))
                step(nc.vector.tensor_tensor(soft[:, 2, n, 1:2], soft[:, 2, n, 1:2], nlam[:, :], ALU.mult))
                if n >= 2:
                    dve.wait_ge(a_turned, n - 1)
                step(nc.vector.tensor_scalar(da_a[:, n % 2, 0:W], da_s[:, n % 2, 0, 0:W], soft[:, 2, n, 0:1], None, ALU.mult))
                nc.vector.scalar_tensor_tensor(out=da_a[:, n % 2, 0:W], in0=da_s[:, n % 2, 1, 0:W], scalar=soft[:, 2, n, 1:2],
                                               in1=da_a[:, n % 2, 0:W], op0=ALU.mult, op1=ALU.add).then_inc(a_ready, 1)

            def keep_o(n):
                dve.wait_ge(pv_done, n + 1)
                nc.vector.tensor_copy(da_o[:, n % 2, n // 2, :], banks[5 + n % 2][:, T:T + P]).then_inc(o_ready, 1)

            for n in range(DA_ITEMS):
                hd, qb = n // 2, n % 2
                W = P * (1 + qb)
                slope = 2.0 ** (-8.0 * (hd + 1) / DA_HEADS)
                sn = da_s[:, n % 2, :, 0:W]
                dve.wait_ge(scored, n + 1)
                if n >= 2:
                    dve.wait_ge(a_ready, n - 1)
                for m in range(2):
                    ins = nc.vector.scalar_tensor_tensor(out=sn[:, m, :], in0=dist[:, T - W:T], scalar=-8.0 * slope,
                                                         in1=banks[1 + 2 * (n % 2) + m][:, 0:W], op0=ALU.mult, op1=ALU.add)
                step(ins)
                step(nc.vector.tensor_reduce(soft[:, 0, n, :], sn, AX_X, ALU.max))
                nc.vector.tensor_scalar(soft[:, 0, n, :], soft[:, 0, n, :], -0.125, None, ALU.mult).then_inc(s_ready, 1)
                if n >= 3:
                    keep_o(n - 3)
                if n >= 1:
                    finish_a(n - 1)
                if n >= 2 and n - 2 in AT_ITEM:
                    later_rows(4 + AT_ITEM.index(n - 2))
            finish_a(DA_ITEMS - 1)
            for n in range(DA_ITEMS - 3, DA_ITEMS):
                keep_o(n)
            for k, at in enumerate(AT_ITEM):
                if at >= DA_ITEMS - 2:
                    later_rows(4 + k)
            dve.wait_ge(o_ready, DA_ITEMS)
            for tc in range(TC):
                ins = nc.vector.tensor_tensor(da_sq[:, tc], da_o[:, tc], da_o[:, tc], ALU.mult)
            step(ins)
            step(nc.vector.tensor_reduce(ss[:, :], da_sq.rearrange("p c h d -> p (c h) d"), AX_X, ALU.add))
            nc.vector.tensor_scalar(ss[:, :], ss[:, :], 1.0 / P, EPS, ALU.mult, ALU.add).then_inc(o_meansq, 1)
            dve.wait_ge(o_root, 1)
            step(nc.vector.reciprocal(rs[:, :], rs[:, :]))
            o2 = da_o.rearrange("p c h d -> p (c h) d")
            nc.vector.tensor_tensor(o2, o2, rs[:, :].unsqueeze(2).to_broadcast([P, 2 * DA_HEADS, P]), ALU.mult
                                    ).then_inc(o_normed, 1)
            dve.wait_ge(rows_stored, 192)
            dve.wait_ge(gate_and_moe_mods, 64)
            update_x(2, out_done, (4, 4))
            moe(0)

            norm_root()
            evict_hT()
            dve.wait_ge(decay_ready, 1)
            for hd in range(RET_HEADS):
                dve.wait_ge(scored, DA_ITEMS + hd + 1)
                if hd >= 1:
                    dve.wait_ge(pv_done, DA_ITEMS + 2 * hd)
                nc.vector.scalar_tensor_tensor(out=ret_s[:, 0:T], in0=banks[hd % 2][:, 0:T], scalar=RET_DK ** -0.5,
                                               in1=decay[:, hd, :], op0=ALU.mult, op1=ALU.mult)
                nc.vector.scalar_tensor_tensor(out=ret_s[:, T:T + P], in0=banks[hd % 2][:, T:T + P], scalar=RET_DK ** -0.5,
                                               in1=decay[:, hd, 0:P], op0=ALU.mult, op1=ALU.mult).then_inc(s_ready, 1)
            dve.wait_ge(o_sumsq, 2 * RET_HEADS)
            nc.vector.tensor_scalar(ss[:, 0:8], ss[:, 0:8], 1.0 / 512, EPS, ALU.mult, ALU.add).then_inc(o_meansq, 1)
            dve.wait_ge(o_root, 2)
            step(nc.vector.reciprocal(rs[:, 0:8], rs[:, 0:8]))
            dve.wait_ge(o_ready, DA_ITEMS + 2 * RET_HEADS)
            for n in range(2 * RET_HEADS):
                ins = nc.vector.tensor_scalar(ret_o[:, n % 2, n // 2, :], ret_o[:, n % 2, n // 2, :], rs[:, n:n + 1], None, ALU.mult)
            ins.then_inc(o_normed, 1)
            for ch in range(16):
                dve.wait_ge(o_turned, 4 + ch // 2 + 1)
                nc.vector.scalar_tensor_tensor(out=ret_yT[:, ch, :], in0=banks[(ch // 2) % 4][:, T * (ch % 2):T * (ch % 2) + T],
                                               scalar=gn[:, ch:ch + 1], in1=ret_sg[:, ch, :], op0=ALU.mult, op1=ALU.mult
                                               ).then_inc(oT_ready, 1)
            dve.wait_ge(gate_and_moe_mods, 128)
            update_x(2, out_done, (12, 12))
            moe(1)
            norm_root(last=True)
            dve.wait_ge(last_gain, 16)
            for tc in range(TC):
                nc.vector.scalar_tensor_tensor(out=h[:, tc, :], in0=X[:, tc, :], scalar=rs[:, tc:tc + 1], in1=mods[:, 0, :],
                                               op0=ALU.mult, op1=ALU.mult).then_inc(h_ready, 1)


_INS = ["x", "c", "norm_mix", "norm_ffn", "ada_w", "ada_b", "da_w_in", "da_w_out", "da_lq1", "da_lk1", "da_lq2",
        "da_lk2", "da_subln", "ret_w_in", "ret_w_out", "ret_gn", "router_w", "router_b", "exp_w1", "exp_w3",
        "exp_w2", "sh_w1", "sh_w3", "sh_w2", "final_norm"]
_OUTS = [((1, 256, 1024), "float32")]


def kernel(**inputs):
    import numpy as _np
    import concourse.bacc as _bacc
    from concourse import mybir as _mybir
    from concourse.bass_utils import run_bass_kernel_spmd as _run

    nc = _bacc.Bacc("TRN2", target_bir_lowering=False, num_devices=1)
    arrays, args = {}, []
    for name in _INS:
        a = _np.ascontiguousarray(inputs[name])
        arrays[f"in_{name}_dram"] = a
        args.append(nc.dram_tensor(f"in_{name}_dram", a.shape, _mybir.dt.from_np(a.dtype), kind="ExternalInput").ap())
    for i, (shape, dtype) in enumerate(_OUTS):
        dt = _mybir.dt.from_np(_np.dtype(dtype))
        args.append(nc.dram_tensor(f"out_{i}_dram", shape, dt, kind="ExternalOutput").ap())
    trunk(nc, *args)
    r = _run(nc, [arrays], core_ids=[0])
    got = tuple(r.results[0][f"out_{i}_dram"] for i in range(len(_OUTS)))
    return got[0]
```

```python
import math
from contextlib import ExitStack

import concourse.bass as bass
from concourse import mybir

F32 = mybir.dt.float32
BF16 = mybir.dt.bfloat16
F32R = mybir.dt.float32r
I32 = mybir.dt.int32
ALU = mybir.AluOpType
ACT = mybir.ActivationFunctionType
AX_X = mybir.AxisListType.X

P = 128
EPS = 1e-6
RING = 12
TW = 2048
SLOTS = 64
DA_HEADS, DA_DH = 8, 64
RET_HEADS, RET_DK = 4, 256
GROUPS, TOPG, TOPK = 8, 4, 8
ROUTED_SCALE = 2.5
FAR = 1e30


LATER = [(1, s) for s in range(4)] + [(0, s) for s in range(2, 6)] + [(1, 4), (1, 5)]
AT_PROJ = [2, 5, 8, 11]
AT_ITEM = [1, 3, 6, 9, 12, 15]


def plan_stream():
    later = [[("ada", l, 4 * s + q) for q in range(4)] for l, s in LATER]
    order = [("ada", 0, i) for i in range(8)]
    for i in range(12):
        order.append(("mix_in", 0, i))
        if i in AT_PROJ:
            order += later[AT_PROJ.index(i)]
    order += sum(later[4:], [])
    order += [("mix_out", 0, i) for i in range(4)]
    order += [("shared", 0, i) for i in range(3)] + [("pad",)]
    moe = {0: len(order)}
    order += [("expert", 0, i) for i in range(192)]
    order += [("mix_in", 1, i) for i in range(24)] + [("mix_out", 1, i) for i in range(8)]
    order += [("shared", 1, i) for i in range(3)] + [("pad",)]
    moe[1] = len(order)
    order += [("expert", 1, i) for i in range(192)]
    return order, moe


def trunk(nc, x, c, norm_mix, norm_ffn, ada_w, ada_b, da_w_in, da_w_out, da_lq1, da_lk1, da_lq2, da_lk2,
          da_subln, ret_w_in, ret_w_out, ret_gn, router_w, router_b, exp_w1, exp_w3, exp_w2,
          sh_w1, sh_w3, sh_w2, final_norm, out):
    _, T, D = x.shape
    TC, KD = T // P, D // P
    E = router_w.shape[2]
    PAIRS = E // 2
    NH = D // 512
    LAM_INIT = 0.8 - 0.6 * math.exp(-0.3 * 0)
    DEPTH = 2
    DA_ITEMS = 2 * DA_HEADS

    order, MOE0 = plan_stream()
    where = {key: n for n, key in enumerate(order) if key[0] != "pad"}
    loads = [sum(1 for m in range(n % RING, n + 1, RING) if order[m][0] != "pad") for n in range(len(order))]
    assert all(MOE0[l] % 2 == 0 for l in range(DEPTH))

    with ExitStack() as ctx:
        def sb(name, shape, dt=F32):
            return ctx.enter_context(nc.sbuf_tensor(name, shape, dt))

        def sb2(name, width):
            with nc.sbuf_tensor(name + "_r", [P, width], F32R) as as_f32r:
                pass
            return sb(name, [P, width]), as_f32r

        def sem(name):
            return ctx.enter_context(nc.semaphore(name))

        ring, ring_r = zip(*(sb2(f"ring{i}", 2 * TW) for i in range(RING // 2)))
        X = sb("X", [P, TC, D])
        HH, HH_r = sb2("HH", 2 * TC * D)
        h = HH[:, 0:TC * D].rearrange("p (c d) -> p c d", c=TC)
        hT_hi = HH_r[:, TC * D:].rearrange("p (k t) -> p k t", k=KD)
        mods, mods_r = sb2("mods", 6 * D)
        gains = mods[:, :].rearrange("p (s d) -> p s d", s=6)
        hT_full = mods[:, 0:2 * D].rearrange("p (k t) -> p k t", k=KD)
        hT_lo = mods_r[:, 0:2 * D].rearrange("p (k t) -> p k t", k=KD)
        arena, arena_r = sb2("arena", 12288)

        ident = sb("ident", [P, P])
        upper = sb("upper", [P, P], BF16)
        ones = sb("ones", [P, P], BF16)
        ident16 = sb("ident16", [P, P], BF16)
        dist = sb("dist", [P, T])
        slot_no = sb("slot_no", [P, SLOTS])
        pass_base = sb("pass_base", [P, 4, 4])
        before = sb("before", [P, GROUPS, GROUPS])
        mod_T = sb("mod_T", [P, DEPTH, 6, KD])
        cT = sb("cT", [P, KD])
        cs = sb("cs", [P, KD])
        cb = sb("cb", [P, KD, 32])
        lsum = sb("lsum", [P, 2])
        lexp = sb("lexp", [P, 2])
        nlam = sb("nlam", [P, 1])
        subg = sb("subg", [P, 1])
        subs = sb("subs", [P, 1])
        gn = sb("gn", [P, 16])
        rw = sb("rw", [P, KD, DEPTH * E])
        rb = sb("rb", [P, DEPTH, E])
        soft = sb("soft", [P, 3, 2 * DA_HEADS, 2])
        decay = sb("decay", [P, RET_HEADS, T])
        ret_s = sb("ret_s", [P, T + P])
        ss = sb("ss", [P, 16])
        rs = sb("rs", [P, 16])

        banks = [ctx.enter_context(nc.psum_tensor(f"bank{i}", [P, 512], F32)) for i in range(8)]
        mod_dram = nc.dram_tensor("mod_dram", [DEPTH, 6, D], F32, kind="Internal").ap()

        mrow0 = arena[:, 6144:6656].rearrange("p (s n) -> p s n", s=2)
        brow0 = arena[:, 6912:7424].rearrange("p (s n) -> p s n", s=2)
        nrow0 = arena[:, 7424:7680].rearrange("p (s n) -> p s n", s=1)
        mrow = HH[:, 0:2560].rearrange("p (s n) -> p s n", s=10)
        browA = HH[:, 2560:3584].rearrange("p (s n) -> p s n", s=4)
        nrowA = HH[:, 3584:3840].rearrange("p (s n) -> p s n", s=1)
        browB = arena[:, 8192:9728].rearrange("p (s n) -> p s n", s=6)
        nrowB = arena[:, 9728:10240].rearrange("p (s n) -> p s n", s=2)
        lvec = arena[:, 11264:11520].rearrange("p (i n) -> p i n", i=4)
        lprod = arena[:, 11520:11648].rearrange("p (i n) -> p i n", i=2)
        qT = arena[:, 0:2048].rearrange("p (k t) -> p k t", k=8)
        kT = arena[:, 2048:4096].rearrange("p (k t) -> p k t", k=8)
        da_v = arena[:, 4096:6144].rearrange("p (c d) -> p c d", c=TC)
        da_o = arena[:, 6144:8192].rearrange("p (c h d) -> p c h d", c=TC, h=DA_HEADS)
        da_oT = arena_r[:, 0:2048]
        da_s = arena[:, 10240:11264].rearrange("p (b m k) -> p b m k", b=2, m=2)
        da_a = arena[:, 11264:11776].rearrange("p (b k) -> p b k", b=2)
        da_aT = arena[:, 11776:12288].rearrange("p (b k q) -> p b k q", b=2, k=2)
        ret_v = arena[:, 4096:8192].rearrange("p (c d) -> p c d", c=TC)
        ret_sg = arena[:, 8192:12288].rearrange("p (c t) -> p c t", c=16)
        ret_yT = arena_r[:, 0:4096]
        ret_o = HH[:, :].rearrange("p (c h d) -> p c h d", c=TC, h=RET_HEADS)
        oT_full_at = {0: arena[:, 2048:4096], 1: arena[:, 4096:8192]}
        oT_lo = {0: arena_r[:, 2048:4096], 1: arena_r[:, 4096:8192]}
        high = {("mix_in", 0): (arena_r[:, 10240:12288], arena_r[:, 6144:8192]),
                ("mix_in", 1): (mods_r[:, 3 * D:5 * D], HH_r[:, 0:2 * D]),
                ("mix_out", 0): (arena_r[:, 4096:6144], arena_r[:, 10240:12288]),
                ("mix_out", 1): (mods_r[:, 3 * D:5 * D], arena_r[:, 8192:10240]),
                ("shared", 0): (arena_r[:, 10240:12288], arena_r[:, 3072:5120]),
                ("shared", 1): (arena_r[:, 10240:12288], arena_r[:, 3072:5120])}
        rw_hi = arena_r[:, 8192:9216].rearrange("p (k m) -> p k m", k=KD)
        rw_lo = arena_r[:, 9216:10240].rearrange("p (k m) -> p k m", k=KD)
        da_junk = HH[:, 3840:4096].rearrange("p (b d) -> p b d", b=2)
        ret_junk = cb.rearrange("p k m -> p (k m)").bitcast(BF16)
        parts = arena[:, 0:3072].bitcast(BF16).rearrange("p (c r d) -> p c r d", c=TC, r=3)
        xg = arena[:, 8736:9760].rearrange("p (k n) -> p k n", k=KD)
        y = arena_r[:, 3072:5120].rearrange("p (r d) -> p r d", r=2)
        S = arena_r[:, 5120:5376]
        Pg = arena[:, 5376:5504].bitcast(BF16).rearrange("p (c n) -> p c n", c=TC)
        sg = arena[:, 5760:6272]
        eh = arena[:, 6272:6528].rearrange("p (b n) -> p b n", b=2)
        ehT = arena[:, 6528:6784].rearrange("p (b n) -> p b n", b=2)
        marks = arena[:, 10210:10212]
        wparts = arena[:, 9760:9952].bitcast(BF16).rearrange("p (c e r) -> p c e r", c=TC, r=3)
        wrest = arena[:, 9952:10080].rearrange("p (c e) -> p c e", c=TC)
        scoreT = arena[:, 6784:7040]
        w_slot = arena[:, 10208:10209]
        shT = arena[:, 6784:7296].rearrange("p (b t) -> p b t", b=2)
        score = arena[:, 7296:7424].rearrange("p (c e) -> p c e", c=TC)
        choice = arena[:, 7424:7552].rearrange("p (c e) -> p c e", c=TC)
        masked = arena[:, 7552:7680].rearrange("p (c e) -> p c e", c=TC)
        chosen = arena[:, 7680:7808].rearrange("p (c e) -> p c e", c=TC)
        top = arena[:, 7808:7936].rearrange("p (g m) -> p g m", m=8)
        gs = arena[:, 7936:7952].rearrange("p (c g) -> p c g", c=TC)
        cmp1 = arena[:, 7952:8080].rearrange("p (c g m) -> p c g m", c=TC, g=GROUPS)
        cmp2 = arena[:, 8080:8208].rearrange("p (c g m) -> p c g m", c=TC, g=GROUPS)
        grank = arena[:, 8208:8224].rearrange("p (c g) -> p c g", c=TC)
        top8 = arena[:, 8224:8240].rearrange("p (c m) -> p c m", c=TC)
        wsum = arena[:, 8240:8242]
        winv = arena[:, 8242:8244]
        mb = arena[:, 8244:8308].bitcast(BF16).rearrange("p (c e) -> p c e", c=TC)
        rank = arena[:, 8308:8436].rearrange("p (e c) -> p e c", c=TC)
        weight = arena[:, 8436:8564].rearrange("p (c e) -> p c e", c=TC)
        cnt = arena[0:1, 8564:8628]
        cmax = arena[0:1, 8628:8660]
        npf = arena[0:1, 8660:8692]
        npass = arena[0:1, 8692:8724].bitcast(I32)
        rk = arena[:, 8724:8728]

        landed = [sem(f"landed{i}") for i in range(RING)]
        tiles_used = sem("tiles_used")
        c_in, consts_in, late_consts_in, x_in = sem("c_in"), sem("consts_in"), sem("late_consts_in"), sem("x_in")
        rows0_in, rowsA_in, rowsB_in = sem("rows0_in"), sem("rowsA_in"), sem("rowsB_in")
        pool_consts, pool_step = sem("pool_consts"), sem("pool_step")
        rows_zero = sem("rows_zero")
        c_silu, cb_ready = sem("c_silu"), sem("cb_ready")
        ada_done, bank_rows_read, rows_ready, row0_ready = (
            sem(n) for n in ("ada_done", "bank_rows_read", "rows_ready", "row0_ready"))
        mod_T_in = [sem(f"mod_T_in{n}") for n in range(4)]
        h_full = sem("h_full")
        w_hi, w_lo, w_lo_pool, rw_split, oT_full, oT_hi, oT_split = (
            sem(n) for n in ("w_hi", "w_lo", "w_lo_pool", "rw_split", "oT_full", "oT_hi", "oT_split"))
        rows0_turned, rows_stored = sem("rows0_turned"), sem("rows_stored")
        gate_and_moe_mods, gate1_in, last_gain = sem("gate_and_moe_mods"), sem("gate1_in"), sem("last_gain")
        sumsq, meansq, root, h_ready, h_turned, hT_act, hT_dve, hT_rounded, hT_split = (
            sem(n) for n in ("sumsq", "meansq", "root", "h_ready", "h_turned", "hT_act", "hT_dve", "hT_rounded", "hT_split"))
        proj_done, proj_out = sem("proj_done"), sem("proj_out")
        scored, s_ready, exp_done, a_ready, a_turned, aT_ready, pv_done, o_ready = (
            sem(n) for n in ("scored", "s_ready", "exp_done", "a_ready", "a_turned", "aT_ready", "pv_done", "o_ready"))
        o_meansq, o_root, o_normed, o_turned = (
            sem(n) for n in ("o_meansq", "o_root", "o_normed", "o_turned"))
        o_sumsq = sem("o_sumsq")
        lam_sums, lam_exp = sem("lam_sums"), sem("lam_exp")
        decay_arg, decay_exp, decay_ready = sem("decay_arg"), sem("decay_exp"), sem("decay_ready")
        out_done, x_new = sem("out_done"), sem("x_new")
        part_hi, rest_ready, part_mid, parts_ready = (sem(n) for n in ("part_hi", "rest_ready", "part_mid", "parts_ready"))
        scoresT_ready = sem("scoresT_ready")
        logits_done, scores_ready, chosen_ready, ranks_done, route_ready = (
            sem(n) for n in ("logits_done", "scores_ready", "chosen_ready", "ranks_done", "route_ready"))
        sh_up, sh_silu, sh_ready, sh_down = (sem(n) for n in ("sh_up", "sh_silu", "sh_ready", "sh_down"))
        U = [{n: sem(f"{n}{l}") for n in (
            "cols_ready", "onehot_ready", "gathered", "xg_lo", "xg_hi", "S_turned", "w_ready", "up_done", "silu_done",
            "eh_ready", "eh_turned", "ehT_ready", "combined", "S_ready", "down0", "down1", "y_hi", "bank0_read",
            "bank1_read")}
            for l in range(DEPTH)]
        routed_done = sem("routed_done")
        dve_step = sem("dve_step")
        written = sem("written")

        def tile_src(key):
            kind, l, i = key
            if kind == "ada":
                s, q = i // 4, i % 4
                return ada_w[l].rearrange("(p k) n -> p k n", k=KD)[:, :, s * D + q * 256:s * D + q * 256 + 256]
            if kind == "mix_in":
                w = (da_w_in if l == 0 else ret_w_in)[0]
                return w.rearrange("(p k) n -> p k n", k=KD)[:, :, i * 256:(i + 1) * 256]
            if kind == "mix_out":
                w = (da_w_out if l == 0 else ret_w_out)[0]
                return w[i * 256:(i + 1) * 256, :].rearrange("(b p) n -> p b n", p=P)
            w = (sh_w1, sh_w3, sh_w2)[i][l]
            return w.rearrange("(p k) n -> p k n", k=KD) if i < 2 else w.rearrange("(p b) n -> p b n", b=2)

        def slot(n):
            return ring[n % RING // 2][:, (n % 2) * TW:(n % 2 + 1) * TW]

        def slot_r(n):
            return ring_r[n % RING // 2][:, (n % 2) * TW:(n % 2 + 1) * TW]

        def tile_in(n):
            return slot(n).rearrange("p (k n) -> p k n", k=KD)

        def tile_out(n):
            return slot(n).rearrange("p (b n) -> p b n", b=2)

        def arrived(eng, n):
            eng.wait_ge(landed[n % RING], 16 * loads[n])

        split = [("mix_in", 0, i) for i in range(12)] + [("mix_out", 0, i) for i in range(4)] + [("shared", 0, i) for i in range(2)]
        split += [("mix_in", 1, i) for i in range(24)] + [("mix_out", 1, i) for i in range(8)] + [("shared", 1, i) for i in range(2)]
        by_pool = [("shared", l, 1) for l in range(DEPTH)]
        by_dve = [key for key in split if key not in by_pool]

        def parts_of(key):
            kind, l, i = key
            hi, lo = high[kind, l][i % 2], slot_r(where[key])
            if kind == "mix_out":
                return [a.rearrange("p (b n) -> p b n", b=2) for a in (hi, lo)]
            return [a.rearrange("p (k n) -> p k n", k=KD) for a in (hi, lo)]

        block = ctx.enter_context(nc.Block())

        @block.sync
        def _(sp):
            def load(n, src):
                out_rows = order[n][0] == "mix_out" or order[n][0:3:2] == ("shared", 2)
                sp.dma_start(tile_out(n) if out_rows else tile_in(n), src).then_inc(landed[n % RING], 16)

            def load_expert(l, t, e):
                n = MOE0[l] + t
                w = (exp_w1, exp_w3, exp_w1, exp_w3, exp_w2, exp_w2)[t % 6][l][bass.ds(e + (0, 0, 1, 1, 0, 1)[t % 6], 1), :, :]
                if t % 6 < 4:
                    sp.dma_start(tile_in(n), w.rearrange("o (p k) n -> p (o k) n", k=KD)).then_inc(landed[n % RING], 16)
                else:
                    sp.dma_start(tile_out(n), w.rearrange("o (p b) n -> p (o b) n", b=2)).then_inc(landed[n % RING], 16)

            units = [sp.alloc_register(f"sp_units{l}") for l in range(DEPTH)]

            def pair_used(l, t, q):
                if t == 0:
                    sp.reg_add(units[l], units[l], sp.value_load(npass[0:1, bass.ds(q, 1)], min_val=1, max_val=4))
                if t in (0, 4):
                    sp.wait_ge(U[l]["up_done" if t == 0 else "down1"], sp.snap(units[l], min_val=1, max_val=128))

            at = 0
            for l in range(DEPTH):
                for n in range(at, MOE0[l] + RING):
                    m = n - RING
                    if m >= 0 and order[m][0] == "expert":
                        pair_used(l - 1, (n - at) % 6, PAIRS - 2 + (n - at) // 6)
                    if order[n][0] == "pad":
                        continue
                    if m >= 0 and order[m][0] != "expert":
                        sp.wait_ge(tiles_used, sum(order[i][0] != "expert" for i in range(m + 1)))
                    if n < MOE0[l]:
                        load(n, tile_src(order[n]))
                    else:
                        load_expert(l, n - MOE0[l], 2 * ((n - MOE0[l]) // 6))
                sp.wait_ge(route_ready, l + 1)
                sp.reg_mov(units[l], 0)
                with sp.Fori(0, PAIRS // 2 - 1) as it:
                    for t in range(RING):
                        pair_used(l, t % 6, it * 2 + t // 6)
                        load_expert(l, t, it * 4 + 4 + 2 * (t // 6))
                at = MOE0[l] + 3 * E

        @block.gpsimd
        def _(pool):
            steps = [0]

            def step(ins):
                ins.then_inc(pool_step, 1)
                steps[0] += 1
                pool.wait_ge(pool_step, steps[0])

            nc.gpsimd.memset(arena[:, 6912:7680], 0.0).then_inc(rows_zero, 1)
            nc.gpsimd.memset(arena[:, 8192:10240], 0.0).then_inc(rows_zero, 1)
            pool.wait_ge(rows_zero, 2)
            for q in range(4):
                pool.dma_start(brow0[32 * q:32 * q + 1, :, :],
                               ada_b[0:1].rearrange("a (s q n) -> q a s n", s=6, q=4)[q, :, 0:2]).then_inc(rows0_in, 16)
                pool.dma_start(nrow0[32 * q:32 * q + 1, 0, :], norm_mix[0:1, 256 * q:256 * (q + 1)]).then_inc(rows0_in, 16)
            step(nc.gpsimd.memset(ident[:, :], 0.0))
            step(nc.gpsimd.affine_select(out=ident[:, :], in_=ident[:, :], compare_op=ALU.not_equal, fill=1.0, base=0,
                                         pattern=[[-1, P]], channel_multiplier=1))
            step(nc.gpsimd.memset(upper[:, :], 1.0))
            step(nc.gpsimd.affine_select(out=upper[:, :], in_=upper[:, :], compare_op=ALU.is_gt, fill=0.0, base=0,
                                         pattern=[[1, P]], channel_multiplier=-1))
            nc.gpsimd.memset(ones[:, :], 1.0)
            nc.gpsimd.tensor_copy(ident16[:, :], ident[:, :])
            step(nc.gpsimd.iota(dist[:, :], pattern=[[-1, T]], base=T - P, channel_multiplier=1,
                                allow_small_or_imprecise_dtypes=True))
            step(nc.gpsimd.affine_select(out=dist[:, :], in_=dist[:, :], compare_op=ALU.is_ge, fill=FAR, base=T - P,
                                         pattern=[[-1, T]], channel_multiplier=1))
            nc.gpsimd.iota(slot_no[:, :], pattern=[[1, SLOTS]], base=0, channel_multiplier=0,
                           allow_small_or_imprecise_dtypes=True)
            nc.gpsimd.iota(pass_base[:, :, :], pattern=[[-SLOTS, 4], [0, 4]], base=0, channel_multiplier=0,
                           allow_small_or_imprecise_dtypes=True)
            step(nc.gpsimd.memset(before[:, :, :], 1.0))
            step(nc.gpsimd.affine_select(out=before[:, :, :], in_=before[:, :, :], compare_op=ALU.is_gt, fill=0.0, base=0,
                                         pattern=[[1, GROUPS], [-1, GROUPS]], channel_multiplier=0))
            nc.gpsimd.memset(ret_s[:, :], 0.0).then_inc(pool_consts, 1)

            def store_rows(l, first, at, count):
                pool.wait_ge(rows_ready, at + count)
                for q in range(4):
                    pool.dma_start(mod_dram[l, first:first + count].rearrange("s (q n) -> q s n", q=4)[q:q + 1],
                                   mrow[32 * q:32 * q + 1, at:at + count, :]).then_inc(rows_stored, 16)

            def spread(l, first, count, done):
                for s in range(first, first + count):
                    pool.dma_start(gains[:, s, :], mod_dram[l, s:s + 1, :].broadcast_to([P, D])).then_inc(done, 16)

            def turn_mods(l, first):
                pool.dma_start(mod_T[:, l, first:first + 2, :],
                               mod_dram[l, first:first + 2].rearrange("s (p k) -> p s k", k=KD)
                               ).then_inc(mod_T_in[2 * l + first // 3], 16)

            for hd in range(RET_HEADS):
                nc.gpsimd.iota(decay[:, hd, :], pattern=[[1, T]], base=0, channel_multiplier=-1,
                               allow_small_or_imprecise_dtypes=True).then_inc(decay_arg, 1)
            pool.wait_ge(decay_exp, RET_HEADS)
            for hd in range(RET_HEADS):
                ins = nc.gpsimd.affine_select(out=decay[:, hd, :], in_=decay[:, hd, :], compare_op=ALU.is_ge, fill=0.0,
                                              base=0, pattern=[[1, T]], channel_multiplier=-1)
            ins.then_inc(decay_ready, 1)
            pool.wait_ge(proj_done, 12)
            nc.gpsimd.memset(HH[:, 2560:3840], 0.0).then_inc(rows_zero, 1)
            store_rows(1, 0, 0, 4)
            store_rows(0, 2, 4, 4)
            pool.wait_ge(rows_stored, 128)
            turn_mods(1, 0)
            turn_mods(0, 3)
            spread(0, 2, 4, gate_and_moe_mods)
            store_rows(1, 4, 8, 2)
            pool.wait_ge(rows_stored, 192)
            turn_mods(1, 3)
            pool.wait_ge(x_new, 2)
            spread(1, 2, 1, gate1_in)

            for l in range(DEPTH):
                u = U[l]
                pool.wait_ge(out_done, (4, 12)[l])
                pool.wait_ge(late_consts_in, 16 * 5)
                step(nc.gpsimd.tensor_copy(rw_hi, rw[:, :, :]))
                nc.gpsimd.tensor_tensor(rw_lo, rw[:, :, :], rw_hi, ALU.subtract).then_inc(rw_split, 1)
                key = by_pool[l]
                pool.wait_ge(w_hi, split.index(key) + 1)
                nc.gpsimd.tensor_tensor(slot_r(where[key]), slot(where[key]), high["shared", l][1], ALU.subtract).then_inc(w_lo_pool, 1)
                pool.wait_ge(part_hi, l + 1)
                nc.gpsimd.tensor_tensor(h, h, parts[:, :, 0, :], ALU.subtract).then_inc(rest_ready, 1)
                pool.wait_ge(rest_ready, l + 1)
                pool.wait_ge(part_mid, l + 1)
                nc.gpsimd.tensor_tensor(parts[:, :, 2, :], h, parts[:, :, 1, :], ALU.subtract).then_inc(parts_ready, 1)
                pool.wait_ge(sh_up, l + 1)
                nc.gpsimd.memset(y.bitcast(F32), 0.0).then_inc(u["bank0_read"], 1)
                if l == 1:
                    pool.wait_ge(x_new, 6)
                    pool.dma_start(gains[:, 2, :], final_norm.rearrange("(a d) -> a d", a=1).broadcast_to([P, D])
                                   ).then_inc(last_gain, 16)
                pool.wait_ge(route_ready, l + 1)
                unit = pool.alloc_register(f"pool_unit{l}")
                pool.reg_mov(unit, 0)
                with pool.Fori(0, PAIRS) as q:
                    n = pool.value_load(npass[0:1, bass.ds(q, 1)], min_val=1, max_val=4)
                    with pool.Fori(0, n) as i:
                        g = pool.snap(unit, min_val=0, max_val=127)
                        pool.wait_ge(u["S_turned"], g + 1)
                        nc.gpsimd.tensor_tensor(rk, rank.rearrange("p e c -> p (e c)")[:, bass.ds(q * 4, 4)],
                                                pass_base.rearrange("p a b -> p (a b)")[:, bass.ds(i * 4, 4)], ALU.add
                                                ).then_inc(u["cols_ready"], 1)
                        pool.wait_ge(u["cols_ready"], g + 1)
                        pool.reg_add(unit, unit, 1)
                        for j in range(2):
                            for tc in range(TC):
                                m = TC * j + tc
                                ins = nc.gpsimd.tensor_scalar(Pg[:, tc, SLOTS * j:SLOTS * (j + 1)], slot_no[:, :],
                                                              rk[:, m:m + 1], None, ALU.is_equal)
                        ins.then_inc(u["onehot_ready"], 1)
                if l == 0:
                    pool.wait_ge(out_done, 12)
                    spread(1, 3, 3, gate_and_moe_mods)

        @block.scalar
        def _(act):
            act.dma_start(cT[:, :], c.rearrange("o (p k) -> p (o k)", k=KD)).then_inc(c_in, 16)
            act.dma_start(X[:, :, :], x[0].rearrange("(c p) d -> p c d", p=P)).then_inc(x_in, 16)
            for i, v in enumerate((da_lq1, da_lk1, da_lq2, da_lk2)):
                act.dma_start(lvec[:, i, :], v.broadcast_to([P, DA_DH])).then_inc(consts_in, 16)
            act.dma_start(subg[:, :], da_subln.rearrange("a p -> p a"), allow_slow_non_contiguous=True).then_inc(consts_in, 16)
            act.wait_ge(c_in, 16)
            nc.scalar.activation(cs[:, :], cT[:, :], ACT.Silu).then_inc(c_silu, 1)

            def release(k):
                act.sem_inc(tiles_used, k)

            norms = [0]

            def norm_stats():
                n = norms[0]
                for tc in range(TC):
                    if n == 0:
                        act.wait_ge(x_in, 16)
                    else:
                        act.wait_ge(x_new, TC * (n - 1) + tc + 1)
                    nc.scalar.activation(h[:, tc, :], X[:, tc, :], ACT.Square, accum_out=ss[:, tc:tc + 1]
                                         ).then_inc(sumsq, 1)
                act.wait_ge(meansq, n + 1)
                nc.scalar.activation(rs[:, 0:TC], ss[:, 0:TC], ACT.Sqrt).then_inc(root, 1)
                norms[0] += 1

            def evict_hT():
                n = norms[0] - 1
                act.wait_ge(mod_T_in[n], 1 if n == 0 else 16)
                for m in (0, 2):
                    act.wait_ge(h_turned, 4 * n + m + 1)
                    for kk in range(2):
                        k = 2 * m + kk
                        ins = nc.scalar.activation(hT_full[:, k, :], banks[m][:, T * kk:T * kk + T], ACT.Identity,
                                                   scale=mod_T[:, n // 2, 3 * (n % 2) + 1, k:k + 1],
                                                   bias=mod_T[:, n // 2, 3 * (n % 2), k:k + 1])
                    ins.then_inc(hT_act, 1)
                for m in range(4):
                    if m % 2 == 0:
                        act.wait_ge(hT_act, 2 * n + m // 2 + 1)
                    else:
                        act.wait_ge(hT_dve, 2 * n + m // 2 + 1)
                    nc.scalar.copy(hT_hi[:, 2 * m:2 * m + 2, :], hT_full[:, 2 * m:2 * m + 2, :]).then_inc(hT_rounded, 1)

            def round_w(*key):
                if key in split:
                    arrived(act, where[key])
                    nc.scalar.copy(high[key[0:2]][key[2] % 2], slot(where[key])).then_inc(w_hi, 1)

            norm_stats()
            for hd in range(RET_HEADS):
                log_g = math.log1p(-(2.0 ** (-5.0 - hd)))
                act.wait_ge(decay_arg, hd + 1)
                nc.scalar.activation(decay[:, hd, :], decay[:, hd, :], ACT.Exp, scale=log_g).then_inc(decay_exp, 1)
            act.wait_ge(lam_sums, 1)
            nc.scalar.activation(lexp[:, :], lsum[:, :], ACT.Exp).then_inc(lam_exp, 1)
            for s in range(2):
                act.wait_ge(ada_done, s + 1)
                release(4)
            proj = [0]

            def evict_proj(dst, func=None):
                act.wait_ge(proj_done, proj[0] + 1)
                src = banks[3 + proj[0] % 4][:, :].rearrange("p (m t) -> p m t", m=2)
                if func is None:
                    nc.scalar.copy(dst, src).then_inc(proj_out, 1)
                else:
                    nc.scalar.activation(dst, src, func).then_inc(proj_out, 1)
                proj[0] += 1
                release(1)

            def mixer_out(l, tiles):
                for i in range(tiles):
                    act.wait_ge(out_done, (0 if l == 0 else 4) + i + 1)
                    release(1)
                    round_w("mix_out", l, i + 2)

            def moe(l):
                round_w("shared", l, 0)
                norm_stats()
                evict_hT()
                round_w("shared", l, 1)
                act.wait_ge(logits_done, l + 1)
                nc.scalar.activation(scoreT, banks[2][:, 0:T], ACT.Sigmoid).then_inc(scoresT_ready, 1)
                act.wait_ge(h_full, l + 1)
                nc.scalar.copy(parts[:, :, 0, :], h).then_inc(part_hi, 1)
                act.wait_ge(rest_ready, l + 1)
                nc.scalar.copy(parts[:, :, 1, :], h).then_inc(part_mid, 1)
                act.wait_ge(sh_up, l + 1)
                nc.scalar.activation(sg, banks[0][:, :], ACT.Silu).then_inc(sh_silu, 1)
                release(2)
                act.wait_ge(sh_down, l + 1)
                release(MOE0[l] - where["shared", l, 2])
                act.wait_ge(route_ready, l + 1)
                u = U[l]
                unit = act.alloc_register(f"act_unit{l}")
                act.reg_mov(unit, 0)
                with act.Fori(0, PAIRS) as q:
                    n = act.value_load(npass[0:1, bass.ds(q, 1)], min_val=1, max_val=4)
                    with act.Fori(0, n) as i:
                        g = act.snap(unit, min_val=0, max_val=127)
                        act.wait_ge(u["gathered"], g * 2 + 1)
                        nc.scalar.copy(xg[:, 0:4, :], banks[2][:, :].rearrange("p (k n) -> p k n", k=4)).then_inc(u["xg_lo"], 1)
                        act.wait_ge(u["up_done"], g + 1)
                        nc.scalar.activation(sg[:, 0:256], banks[1][:, 0:256], ACT.Silu).then_inc(u["silu_done"], 1)
                        act.wait_ge(u["eh_turned"], g + 1)
                        nc.scalar.copy(ehT, banks[2][:, 0:256].rearrange("p (b n) -> p b n", b=2)).then_inc(u["ehT_ready"], 1)
                        for hf in range(NH):
                            act.wait_ge(u[f"down{hf}"], g + 1)
                            nc.scalar.copy(y[:, 0, 512 * hf:512 * hf + 512], banks[hf][:, :]).then_inc(u["y_hi"], 1)
                        act.reg_add(unit, unit, 1)

            def evict_aT(n):
                act.wait_ge(a_turned, n + 1)
                W = P * (1 + n % 2)
                nc.scalar.copy(da_aT[:, n % 2, 0:1 + n % 2, :], banks[5 + n % 2][:, 0:W].rearrange("p (b q) -> p b q", q=P)
                               ).then_inc(aT_ready, 1)

            def square_o(n):
                act.wait_ge(o_ready, n + 1)
                if n >= 2:
                    act.wait_ge(o_sumsq, n - 1)
                nc.scalar.activation(da_junk[:, n % 2, :], da_o[:, n % 2, n // 2, :], ACT.Square,
                                     accum_out=ss[:, DA_HEADS * (n % 2) + n // 2:DA_HEADS * (n % 2) + n // 2 + 1]
                                     ).then_inc(o_sumsq, 1)

            evict_hT()
            round_w("mix_in", 0, 0)
            act.dma_start(gn[:, :], ret_gn.rearrange("a (c p) -> p (a c)", p=P), allow_slow_non_contiguous=True
                          ).then_inc(late_consts_in, 16)
            for l in range(DEPTH):
                act.dma_start(rw[:, :, E * l:E * (l + 1)], router_w[l].rearrange("(p k) e -> p k e", k=KD)).then_inc(late_consts_in, 16)
                act.dma_start(rb[:, l, :], router_b[l:l + 1, :].broadcast_to([P, E])).then_inc(late_consts_in, 16)
            act.wait_ge(rows_zero, 2)
            for q in range(4):
                act.dma_start(browB[32 * q:32 * q + 1, :, :],
                              ada_b[1:2].rearrange("a (s q n) -> q a s n", s=6, q=4)[q]).then_inc(rowsB_in, 16)
                for i, g in enumerate((norm_mix, norm_ffn)):
                    act.dma_start(nrowB[32 * q:32 * q + 1, i, :], g[1:2, 256 * q:256 * (q + 1)]).then_inc(rowsB_in, 16)
            round_w("mix_in", 0, 1)
            for i in range(12):
                if i < 4:
                    evict_proj(qT[:, 2 * i:2 * i + 2, :])
                elif i < 8:
                    evict_proj(kT[:, 2 * (i - 4):2 * (i - 4) + 2, :])
                else:
                    evict_proj(da_v[:, :, 256 * (i - 8):256 * (i - 7)])
                round_w("mix_in", 0, i + 2)
                if i in AT_PROJ:
                    act.wait_ge(ada_done, 2 + AT_PROJ.index(i) + 1)
                    release(4)
            act.wait_ge(rows_zero, 3)
            for q in range(4):
                act.dma_start(browA[32 * q:32 * q + 1, :, :],
                              ada_b[0:1].rearrange("a (s q n) -> q a s n", s=6, q=4)[q, :, 2:6]).then_inc(rowsA_in, 16)
                act.dma_start(nrowA[32 * q:32 * q + 1, 0, :], norm_ffn[0:1, 256 * q:256 * (q + 1)]).then_inc(rowsA_in, 16)
            for n in range(2 * DA_HEADS):
                W = P * (1 + n % 2)
                if n >= 2 and n - 2 in AT_ITEM:
                    act.wait_ge(ada_done, 6 + AT_ITEM.index(n - 2) + 1)
                    release(4)
                act.wait_ge(s_ready, n + 1)
                for m in range(2):
                    nc.scalar.activation(da_s[:, n % 2, m, 0:W], da_s[:, n % 2, m, 0:W], ACT.Exp, scale=0.125,
                                         bias=soft[:, 0, n, m:m + 1], accum_out=soft[:, 1, n, m:m + 1]).then_inc(exp_done, 1)
                if n >= 1:
                    evict_aT(n - 1)
                if n >= 4:
                    square_o(n - 4)
            evict_aT(2 * DA_HEADS - 1)
            for n in range(DA_ITEMS - 4, DA_ITEMS):
                square_o(n)
            act.wait_ge(pv_done, DA_ITEMS)
            round_w("mix_out", 0, 0)
            act.wait_ge(o_meansq, 1)
            nc.scalar.activation(rs[:, :], ss[:, :], ACT.Sqrt).then_inc(o_root, 1)
            round_w("mix_out", 0, 1)
            act.wait_ge(ada_done, 2 + len(LATER))
            release(4)
            for m in range(4):
                act.wait_ge(o_turned, m + 1)
                nc.scalar.activation(oT_full_at[0][:, 512 * m:512 * m + 512], banks[m][:, :], ACT.Copy, scale=subs[:, 0:1]
                                     ).then_inc(oT_full, 1)
            for m in range(4):
                act.wait_ge(oT_full, m + 1)
                nc.scalar.copy(da_oT[:, 512 * m:512 * m + 512], oT_full_at[0][:, 512 * m:512 * m + 512]).then_inc(oT_hi, 1)
            mixer_out(0, 4)
            moe(0)

            round_w("mix_in", 1, 0)
            norm_stats()
            evict_hT()
            round_w("mix_in", 1, 1)
            for i in range(24):
                if i < 4:
                    evict_proj(qT[:, 2 * i:2 * i + 2, :])
                elif i < 8:
                    evict_proj(kT[:, 2 * (i - 4):2 * (i - 4) + 2, :])
                elif i < 16:
                    evict_proj(ret_v[:, :, 256 * (i - 8):256 * (i - 7)])
                else:
                    evict_proj(ret_sg[:, 2 * (i - 16):2 * (i - 16) + 2, :], ACT.Silu)
                round_w("mix_in", 1, i + 2)
            for n in range(2 * RET_HEADS):
                hd, qb = n // 2, n % 2
                act.wait_ge(pv_done, DA_ITEMS + n + 1)
                if n >= 1:
                    act.wait_ge(o_sumsq, DA_ITEMS + n)
                nc.scalar.activation(ret_junk, banks[5 + n % 2][:, :], ACT.Square, accum_out=ss[:, n:n + 1]
                                     ).then_inc(o_sumsq, 1)
                nc.scalar.copy(ret_o[:, qb, hd, :], banks[5 + n % 2][:, :]).then_inc(o_ready, 1)
            act.wait_ge(o_meansq, 2)
            nc.scalar.activation(rs[:, 0:8], ss[:, 0:8], ACT.Sqrt).then_inc(o_root, 1)
            round_w("mix_out", 1, 0)
            for g in range(4):
                act.wait_ge(oT_full, 4 + 4 * (g + 1))
                nc.scalar.copy(ret_yT[:, 1024 * g:1024 * g + 1024], oT_full_at[1][:, 1024 * g:1024 * g + 1024]).then_inc(oT_hi, 1)
                if g == 1:
                    round_w("mix_out", 1, 1)
            mixer_out(1, 8)
            moe(1)
            norm_stats()
            for tc in range(TC):
                act.wait_ge(h_ready, 2 * 4 + tc + 1)
                act.dma_start(out[0, P * tc:P * (tc + 1), :], h[:, tc, :]).then_inc(written, 16)
            act.wait_ge(written, 16 * TC)

        @block.tensor
        def _(pe):
            def ada(l, s, bank):
                tiles = [where["ada", l, 4 * s + q] for q in range(4)]
                for n in tiles:
                    arrived(pe, n)
                for k in range(KD):
                    for q in range(4):
                        ins = nc.tensor.matmul(bank[32 * q:32 * q + 32, :],
                                               cb[:, k, :], tile_in(tiles[q])[:, k, :], start=(k == 0), stop=(k == KD - 1))
                ins.then_inc(ada_done, 1)

            norms = [0]

            def turn_h():
                pe.wait_ge(h_ready, TC * (norms[0] + 1))
                for m in range(4):
                    for kk in range(2):
                        for tc in range(TC):
                            ins = nc.tensor.transpose(
                                banks[m][:, T * kk + P * tc:T * kk + P * tc + P],
                                h[:, tc, :].rearrange("t (p k) -> t k p", k=KD)[:, 2 * m + kk, :], ident[:, :])
                    ins.then_inc(h_turned, 1)
                norms[0] += 1

            def hT_there():
                pe.wait_ge(hT_split, 4 * norms[0])

            def product(out, a, b, first, last):
                for i, (x1, x2) in enumerate(((0, 0), (0, 1), (1, 0))):
                    ins = nc.tensor.matmul(out, a[x1], b[x2], start=(first and i == 0), stop=(last and i == 2),
                                           skip_group_check=True)
                return ins

            def w_there(*key):
                if key in by_dve:
                    pe.wait_ge(w_lo, by_dve.index(key) + 1)
                else:
                    pe.wait_ge(w_lo_pool, by_pool.index(key) + 1)

            hTs = (hT_hi, hT_lo)

            proj = [0]

            def project(l, i, token_major):
                w_there("mix_in", l, i)
                if proj[0] >= 4:
                    pe.wait_ge(proj_out, proj[0] - 3)
                bank, ws = banks[3 + proj[0] % 4], parts_of(("mix_in", l, i))
                for m in range(2):
                    for k in range(KD):
                        if token_major:
                            a, b = [x[:, k, P * m:P * m + P] for x in hTs], [w[:, k, :] for w in ws]
                        else:
                            a, b = [w[:, k, P * m:P * m + P] for w in ws], [x[:, k, :] for x in hTs]
                        ins = product(bank[:, 256 * m:256 * m + 256], a, b, k == 0, k == KD - 1)
                ins.then_inc(proj_done, 1)
                proj[0] += 1

            def mix_out(l, tiles, src):
                for i in range(tiles):
                    w_there("mix_out", l, i)
                    ws = parts_of(("mix_out", l, i))
                    pe.wait_ge(oT_split, (i + 1 if l == 0 else 4 + i // 2 + 1))
                    for b in range(2):
                        for tc in range(TC):
                            for hf in range(NH):
                                at = T * (2 * i + b) + P * tc
                                ins = product(banks[4 + NH * tc + hf][:, :], [x[:, at:at + P] for x in src],
                                              [w[:, b, 512 * hf:512 * hf + 512] for w in ws], i == 0 and b == 0,
                                              i == tiles - 1 and b == 1)
                    ins.then_inc(out_done, 1)

            def moe(l):
                turn_h()
                hT_there()
                pe.wait_ge(rw_split, l + 1)
                for k in range(KD):
                    ins = product(banks[2][:, 0:T], (rw_hi[:, k, :], rw_lo[:, k, :]), [x[:, k, :] for x in hTs],
                                  k == 0, k == KD - 1)
                ins.then_inc(logits_done, 1)
                for i in range(2):
                    if i == 0:
                        pe.wait_ge(scoresT_ready, l + 1)
                        for tc in range(TC):
                            ins = nc.tensor.transpose(banks[2][:, T + P * tc:T + P * tc + P], scoreT[:, P * tc:P * tc + P],
                                                      ident[:, :])
                        ins.then_inc(scores_ready, 1)
                    w_there("shared", l, i)
                    ws = [w.rearrange("p k (m b) -> p k b m", b=2) for w in parts_of(("shared", l, i))]
                    for b in range(2):
                        for k in range(KD):
                            ins = product(banks[i][:, 256 * b:256 * b + 256], [w[:, k, b, :] for w in ws],
                                          [x[:, k, :] for x in hTs], k == 0, k == KD - 1)
                ins.then_inc(sh_up, 1)
                pe.wait_ge(chosen_ready, l + 1)
                nc.tensor.matmul(banks[3][:, 0:E], upper[:, :], mb[:, 0, :], start=True, stop=True)
                nc.tensor.matmul(banks[3][:, E:2 * E], ones[:, :], mb[:, 0, :], start=True, stop=False)
                nc.tensor.matmul(banks[3][:, E:2 * E], upper[:, :], mb[:, 1, :], start=False, stop=True)
                nc.tensor.matmul(banks[3][0:1, 2 * E:3 * E], ones[:, 0:1], mb[:, 0, :], start=True, stop=False)
                nc.tensor.matmul(banks[3][0:1, 2 * E:3 * E], ones[:, 0:1], mb[:, 1, :], start=False, stop=True
                                 ).then_inc(ranks_done, 1)
                pe.wait_ge(sh_ready, l + 1)
                arrived(pe, where["shared", l, 2])
                w = tile_out(where["shared", l, 2])
                for tc in range(TC):
                    for hf in range(NH):
                        for b in range(2):
                            ins = nc.tensor.matmul(banks[4 + NH * tc + hf][:, :], shT[:, b, P * tc:P * tc + P],
                                                   w[:, b, 512 * hf:512 * hf + 512], start=(b == 0), stop=False,
                                                   skip_group_check=True)
                ins.then_inc(sh_down, 1)

                u = U[l]

                def combine(tc, last=False):
                    for hf in range(NH):
                        for r in range(2):
                            ins = nc.tensor.matmul(banks[4 + NH * tc + hf][:, :], S[:, P * tc:P * tc + P],
                                                   y[:, r, 512 * hf:512 * hf + 512], start=False, stop=(last and r == 1),
                                                   skip_group_check=True)
                    return ins

                pe.wait_ge(parts_ready, l + 1)
                pe.wait_ge(route_ready, l + 1)
                unit = pe.alloc_register(f"pe_unit{l}")
                pe.reg_mov(unit, 0)
                with pe.Fori(0, PAIRS // 2) as it:
                    for pair in range(2):
                        t0 = MOE0[l] + 6 * pair
                        w13 = [ring[(t0 + 2 * j) % RING // 2][:, :].rearrange("p (w k n) -> p k w n", w=2, k=KD) for j in range(2)]
                        w2 = [tile_out(t0 + 4 + j) for j in range(2)]

                        def arrived_now(t):
                            pe.wait_ge(landed[(t0 + t) % RING], it * 16 + 16 * loads[t0 + t])

                        n = pe.value_load(npass[0:1, bass.ds(it * 2 + pair, 1)], min_val=1, max_val=4)
                        with pe.Fori(0, n):
                            g = pe.snap(unit, min_val=0, max_val=127)
                            pe.wait_ge(u["onehot_ready"], g + 1)
                            for half in range(2):
                                if half == 1:
                                    pe.wait_ge(u["bank0_read"], g + 1)
                                for kk in range(4):
                                    for tc in range(TC):
                                        for r in range(3):
                                            ins = nc.tensor.matmul(
                                                banks[2 - 2 * half][:, P * kk:P * kk + P],
                                                parts[:, tc, r, :].rearrange("t (p k) -> t k p", k=KD)[:, 4 * half + kk, :],
                                                Pg[:, tc, :], start=(tc == 0 and r == 0), stop=(tc == TC - 1 and r == 2))
                                ins.then_inc(u["gathered"], 1)
                            pe.wait_ge(u["S_ready"], g + 1)
                            for tc in range(TC):
                                nc.tensor.matmul(banks[3][:, P * tc:P * tc + P], Pg[:, tc, :], ident16[:, :],
                                                 start=True, stop=True)
                            for tc in range(TC):
                                ins = nc.tensor.matmul(
                                    banks[3][:, T:T + 6], Pg[:, tc, :],
                                    wparts[:, tc].rearrange("p e r -> p (e r)")[:, bass.ds(it * 12 + 6 * pair, 6)],
                                    start=(tc == 0), stop=(tc == TC - 1))
                            ins.then_inc(u["S_turned"], 1)
                            pe.wait_ge(u["bank1_read"], g + 1)
                            for k in range(KD):
                                if k % 4 == 0:
                                    pe.wait_ge(u["xg_lo" if k == 0 else "xg_hi"], g + 1)
                                for j in range(2):
                                    if k == 0:
                                        arrived_now(2 * j)
                                        arrived_now(2 * j + 1)
                                    ins = nc.tensor.matmul(banks[1][SLOTS * j:SLOTS * (j + 1), :],
                                                           xg[:, k, SLOTS * j:SLOTS * (j + 1)], w13[j][:, k, :, :],
                                                           start=(k == 0), stop=(k == KD - 1))
                            ins.then_inc(u["up_done"], 1)
                            combine(0)
                            pe.wait_ge(u["eh_ready"], g + 1)
                            for b in range(2):
                                ins = nc.tensor.transpose(banks[2][:, P * b:P * b + P], eh[:, b, :], ident[:, :])
                            ins.then_inc(u["eh_turned"], 1)
                            combine(1).then_inc(u["combined"], 1)
                            pe.wait_ge(u["ehT_ready"], g + 1)
                            for hf in range(NH):
                                for b in range(2):
                                    for j in range(2):
                                        if hf == 0 and b == 0:
                                            arrived_now(4 + j)
                                        ins = nc.tensor.matmul(banks[hf][SLOTS * j:SLOTS * (j + 1), :],
                                                               ehT[:, b, SLOTS * j:SLOTS * (j + 1)],
                                                               w2[j][:, b, 512 * hf:512 * hf + 512], start=(b == 0), stop=(b == 1))
                                ins.then_inc(u["down0" if hf == 0 else "down1"], 1)
                            pe.reg_add(unit, unit, 1)
                total = pe.snap(unit, min_val=PAIRS, max_val=128)
                pe.wait_ge(u["S_ready"], total + 1)
                pe.wait_ge(u["bank0_read"], total + 1)
                pe.wait_ge(u["bank1_read"], total + 1)
                combine(0, last=True).then_inc(routed_done, 1)
                combine(1, last=True).then_inc(routed_done, 1)

            pe.wait_ge(pool_consts, 1)
            turn_h()
            pe.wait_ge(cb_ready, 1)
            for s in range(2):
                ada(0, s, banks[4][:, 256 * s:256 * s + 256])
            pe.wait_ge(row0_ready, 2)
            for s in range(2):
                for k in range(KD):
                    for q in range(4):
                        ins = nc.tensor.matmul(banks[5][32 * q:32 * q + 32, KD * s + k:KD * s + k + 1],
                                               mrow0[:, s, k:256:KD], ident[:, 32 * q:32 * q + 1], start=True, stop=True)
            ins.then_inc(rows0_turned, 1)

            def later(k):
                if k >= 2:
                    pe.wait_ge(bank_rows_read, k - 1)
                ada(*LATER[k], banks[7 * (1 - k % 2)][:, 0:256])

            hT_there()
            for i in range(12):
                project(0, i, token_major=(i >= 8))
                if i in AT_PROJ:
                    later(AT_PROJ.index(i))
            pe.wait_ge(proj_out, 12)

            def scores(n):
                hd, qb = n // 2, n % 2
                if n >= 2:
                    pe.wait_ge(s_ready, n - 1)
                for m in range(2):
                    ins = nc.tensor.matmul(banks[1 + 2 * (n % 2) + m][:, 0:P * (1 + qb)],
                                           qT[64 * m:64 * m + 64, hd, P * qb:P * qb + P],
                                           kT[64 * m:64 * m + 64, hd, 0:P * (1 + qb)], start=True, stop=True)
                ins.then_inc(scored, 1)

            def turn_a(n):
                pe.wait_ge(a_ready, n + 1)
                if n >= 2:
                    pe.wait_ge(o_ready, n - 1)
                for kb in range(1 + n % 2):
                    ins = nc.tensor.transpose(banks[5 + n % 2][:, P * kb:P * kb + P], da_a[:, n % 2, P * kb:P * kb + P], ident[:, :])
                ins.then_inc(a_turned, 1)

            def attend(n):
                hd, qb = n // 2, n % 2
                pe.wait_ge(aT_ready, n + 1)
                for kb in range(1 + qb):
                    ins = nc.tensor.matmul(banks[5 + n % 2][:, T:T + P], da_aT[:, n % 2, kb, :], da_v[:, kb, P * hd:P * hd + P],
                                           start=(kb == 0), stop=(kb == qb))
                ins.then_inc(pv_done, 1)

            scores(0)
            scores(1)
            for n in range(DA_ITEMS):
                if n + 2 < DA_ITEMS:
                    scores(n + 2)
                turn_a(n)
                if n >= 1:
                    attend(n - 1)
                if n == DA_ITEMS - 1:
                    attend(n)
                if n in AT_ITEM:
                    later(4 + AT_ITEM.index(n))
            pe.wait_ge(o_normed, 1)
            pe.wait_ge(bank_rows_read, len(LATER))
            for m in range(4):
                for hh in range(2):
                    for tc in range(TC):
                        ins = nc.tensor.transpose(banks[m][:, T * hh + P * tc:T * hh + P * tc + P], da_o[:, tc, 2 * m + hh, :], ident[:, :])
                ins.then_inc(o_turned, 1)
            mix_out(0, 4, (da_oT, oT_lo[0]))
            moe(0)

            turn_h()
            hT_there()
            for i in range(24):
                project(1, i, token_major=(8 <= i < 16))
            pe.wait_ge(proj_out, 36)

            def ret_scores(hd):
                if hd >= 2:
                    pe.wait_ge(s_ready, DA_ITEMS + hd - 1)
                bank = banks[hd % 2]
                for kk in range(2):
                    nc.tensor.matmul(bank[:, 0:T], kT[:, 2 * hd + kk, 0:P], qT[:, 2 * hd + kk, :], start=(kk == 0), stop=(kk == 1))
                for kk in range(2):
                    ins = nc.tensor.matmul(bank[:, T:T + P], kT[:, 2 * hd + kk, P:T], qT[:, 2 * hd + kk, P:T],
                                           start=(kk == 0), stop=(kk == 1))
                ins.then_inc(scored, 1)

            def ret_attend(hd):
                pe.wait_ge(s_ready, DA_ITEMS + hd + 1)
                v = [ret_v[:, jb, 512 * hd:512 * hd + 512] for jb in range(2)]
                if hd >= 1:
                    pe.wait_ge(o_ready, DA_ITEMS + 2 * hd - 1)
                nc.tensor.matmul(banks[5][:, :], ret_s[:, 0:P], v[0], start=True, stop=True).then_inc(pv_done, 1)
                if hd >= 1:
                    pe.wait_ge(o_ready, DA_ITEMS + 2 * hd)
                nc.tensor.matmul(banks[6][:, :], ret_s[:, P:T], v[0], start=True, stop=False)
                nc.tensor.matmul(banks[6][:, :], ret_s[:, T:T + P], v[1], start=False, stop=True).then_inc(pv_done, 1)

            ret_scores(0)
            for hd in range(RET_HEADS):
                if hd + 1 < RET_HEADS:
                    ret_scores(hd + 1)
                ret_attend(hd)
            pe.wait_ge(o_normed, 2)
            for ch in range(16):
                if ch >= 8:
                    pe.wait_ge(oT_full, 4 + 2 * (ch // 2) - 6)
                for tc in range(TC):
                    ins = nc.tensor.transpose(banks[(ch // 2) % 4][:, T * (ch % 2) + P * tc:T * (ch % 2) + P * tc + P],
                                              ret_o[:, tc, ch // 4, P * (ch % 4):P * (ch % 4) + P], ident[:, :])
                if ch % 2:
                    ins.then_inc(o_turned, 1)
            mix_out(1, 8, (ret_yT, oT_lo[1]))
            moe(1)

        @block.vector
        def _(dve):
            steps = [0]

            def step(ins):
                ins.then_inc(dve_step, 1)
                steps[0] += 1
                dve.wait_ge(dve_step, steps[0])

            dve.wait_ge(c_silu, 1)
            nc.vector.tensor_copy(cb[:, :, :], cs[:, :].unsqueeze(2).to_broadcast([P, KD, 32])).then_inc(cb_ready, 1)
            dve.wait_ge(consts_in, 16 * 5)
            step(nc.vector.tensor_tensor(lprod, lvec[:, 0:4:2, :], lvec[:, 1:4:2, :], ALU.mult))
            nc.vector.tensor_reduce(lsum[:, :], lprod, AX_X, ALU.add).then_inc(lam_sums, 1)
            nc.vector.tensor_scalar(subs[:, :], subg[:, :], 1.0 - LAM_INIT, None, ALU.mult)

            norms = [0]

            def norm_root(last=False):
                n = norms[0]
                dve.wait_ge(sumsq, TC * (n + 1))
                nc.vector.tensor_scalar(ss[:, 0:TC], ss[:, 0:TC], 1.0 / D, EPS, ALU.mult, ALU.add).then_inc(meansq, 1)
                dve.wait_ge(root, n + 1)
                step(nc.vector.reciprocal(rs[:, 0:TC], rs[:, 0:TC]))

                if not last:
                    for tc in range(TC):
                        nc.vector.tensor_scalar(h[:, tc, :], X[:, tc, :], rs[:, tc:tc + 1], None, ALU.mult).then_inc(h_ready, 1)
                norms[0] += 1

            def evict_hT():
                n = norms[0] - 1
                dve.wait_ge(mod_T_in[n], 1 if n == 0 else 16)
                for m in (1, 3):
                    dve.wait_ge(h_turned, 4 * n + m + 1)
                    for kk in range(2):
                        k = 2 * m + kk
                        ins = nc.vector.tensor_scalar(hT_full[:, k, :], banks[m][:, T * kk:T * kk + T],
                                                      mod_T[:, n // 2, 3 * (n % 2) + 1, k:k + 1],
                                                      mod_T[:, n // 2, 3 * (n % 2), k:k + 1], ALU.mult, ALU.add)
                    ins.then_inc(hT_dve, 1)
                for m in range(4):
                    dve.wait_ge(hT_rounded, 4 * n + m + 1)
                    nc.vector.tensor_tensor(hT_lo[:, 2 * m:2 * m + 2, :], hT_full[:, 2 * m:2 * m + 2, :],
                                            hT_hi[:, 2 * m:2 * m + 2, :], ALU.subtract).then_inc(hT_split, 1)

            def low_part(*key):
                dve.wait_ge(w_hi, split.index(key) + 1)
                nc.vector.tensor_tensor(slot_r(where[key]), slot(where[key]),
                                        high[key[0:2]][key[2] % 2], ALU.subtract).then_inc(w_lo, 1)

            def update_x(gate, done, at):
                for tc in range(TC):
                    dve.wait_ge(done, at[tc])
                    for hf in range(NH):
                        ins = nc.vector.tensor_tensor(h[:, tc, 512 * hf:512 * hf + 512], banks[4 + NH * tc + hf][:, :],
                                                      gains[:, gate, 512 * hf:512 * hf + 512], ALU.mult)
                    step(ins)
                    ins = nc.vector.tensor_tensor(X[:, tc, :], X[:, tc, :], h[:, tc, :], ALU.add).then_inc(x_new, 1)

            def moe(l):
                norm_root()
                evict_hT()
                low_part("shared", l, 0)
                dve.wait_ge(h_turned, 4 * norms[0])
                dve.wait_ge(gate_and_moe_mods, 64 if l == 0 else 112)
                for tc in range(TC):
                    ins = nc.vector.tensor_tensor(h[:, tc, :], h[:, tc, :], gains[:, 4, :], ALU.mult)
                step(ins)
                for tc in range(TC):
                    ins = nc.vector.tensor_tensor(h[:, tc, :], h[:, tc, :], gains[:, 3, :], ALU.add)
                ins.then_inc(h_full, 1)
                dve.wait_ge(scores_ready, l + 1)
                dve.wait_ge(late_consts_in, 16 * 5)
                step(nc.vector.tensor_copy(score, banks[2][:, T:2 * T].rearrange("p (c l e) -> p c l e", c=TC, l=DEPTH)[:, :, l, :]))
                step(nc.vector.tensor_tensor(choice, score, rb[:, l:l + 1, :].to_broadcast([P, TC, E]), ALU.add))
                for tc in range(TC):
                    for gr in range(GROUPS):
                        ins = nc.vector.max(top[:, tc * GROUPS + gr, :], choice[:, tc, 8 * gr:8 * gr + 8])
                step(ins)
                step(nc.vector.tensor_tensor(gs.rearrange("p c g -> p (c g)").unsqueeze(2), top[:, :, 0:1], top[:, :, 1:2], ALU.add))
                other = gs.unsqueeze(2).to_broadcast([P, TC, GROUPS, GROUPS])
                own = gs.unsqueeze(3).to_broadcast([P, TC, GROUPS, GROUPS])
                nc.vector.tensor_tensor(cmp1, other, own, ALU.is_gt)
                step(nc.vector.tensor_tensor(cmp2, other, own, ALU.is_equal))
                for tc in range(TC):
                    ins = nc.vector.tensor_tensor(cmp2[:, tc, :, :], cmp2[:, tc, :, :], before[:, :, :], ALU.mult)
                step(ins)
                step(nc.vector.tensor_tensor(cmp1, cmp1, cmp2, ALU.add))
                step(nc.vector.tensor_reduce(grank, cmp1, AX_X, ALU.add))
                step(nc.vector.tensor_scalar(grank, grank, TOPG - 0.5, -FAR, ALU.is_gt, ALU.mult))
                step(nc.vector.tensor_tensor(masked.rearrange("p c (g m) -> p (c g) m", m=8),
                                             choice.rearrange("p c (g m) -> p (c g) m", m=8),
                                             grank.rearrange("p c g -> p (c g)").unsqueeze(2).to_broadcast([P, TC * GROUPS, 8]),
                                             ALU.add))
                for tc in range(TC):
                    ins = nc.vector.max(top8[:, tc, :], masked[:, tc, :])
                step(ins)
                for tc in range(TC):
                    ins = nc.vector.match_replace(chosen[:, tc, :], top8[:, tc, :], masked[:, tc, :], -3e38)
                step(ins)
                step(nc.vector.tensor_tensor(chosen, chosen, masked, ALU.not_equal))
                nc.vector.tensor_copy(mb, chosen).then_inc(chosen_ready, 1)
                step(nc.vector.tensor_tensor(masked, score, chosen, ALU.mult))
                step(nc.vector.tensor_reduce(wsum, masked, AX_X, ALU.add))
                step(nc.vector.reciprocal(winv, wsum))
                for tc in range(TC):
                    ins = nc.vector.tensor_scalar(weight[:, tc, :], masked[:, tc, :], winv[:, tc:tc + 1], ROUTED_SCALE,
                                                  ALU.mult, ALU.mult)
                step(ins)
                step(nc.vector.tensor_copy(wparts[:, :, :, 0], weight))
                step(nc.vector.tensor_tensor(wrest, weight, wparts[:, :, :, 0], ALU.subtract))
                step(nc.vector.tensor_copy(wparts[:, :, :, 1], wrest))
                nc.vector.tensor_tensor(wparts[:, :, :, 2], wrest, wparts[:, :, :, 1], ALU.subtract)
                u = U[l]
                nc.vector.memset(S.bitcast(F32), 0.0).then_inc(u["S_ready"], 1)
                nc.vector.memset(w_slot, 0.0).then_inc(u["S_turned"], 1)
                nc.vector.memset(marks, 0.0).then_inc(u["bank1_read"], 1)
                dve.wait_ge(sh_silu, l + 1)
                nc.vector.tensor_tensor(shT, sg.rearrange("p (b t) -> p b t", b=2),
                                        banks[1][:, :].rearrange("p (b t) -> p b t", b=2), ALU.mult).then_inc(sh_ready, 1)
                dve.wait_ge(ranks_done, l + 1)
                nc.vector.scalar_tensor_tensor(out=choice, in0=banks[3][:, 0:TC * E].rearrange("p (c e) -> p c e", c=TC),
                                               scalar=1.0, in1=chosen, op0=ALU.add, op1=ALU.mult)
                step(nc.vector.tensor_copy(cnt, banks[3][0:1, 2 * E:3 * E]))
                nc.vector.tensor_scalar(rank.rearrange("p e c -> p c e"), choice, -1.0, None, ALU.add)
                pairs = cnt.rearrange("a (q j) -> a j q", j=2)
                step(nc.vector.tensor_tensor(cmax, pairs[:, 0, :], pairs[:, 1, :], ALU.max))
                step(nc.vector.tensor_scalar(npf, cmax, float(SLOTS), 1.0, ALU.is_gt, ALU.add))
                step(nc.vector.scalar_tensor_tensor(out=npf, in0=cmax, scalar=2.0 * SLOTS, in1=npf, op0=ALU.is_gt, op1=ALU.add))
                nc.vector.scalar_tensor_tensor(out=npass, in0=cmax, scalar=3.0 * SLOTS, in1=npf, op0=ALU.is_gt, op1=ALU.add
                                               ).then_inc(route_ready, 1)
                dve.wait_ge(route_ready, l + 1)
                unit = dve.alloc_register(f"dve_unit{l}")
                dve.reg_mov(unit, 0)
                with dve.Fori(0, PAIRS) as q:
                    n = dve.value_load(npass[0:1, bass.ds(q, 1)], min_val=1, max_val=4)
                    with dve.Fori(0, n):
                        g = dve.snap(unit, min_val=0, max_val=127)
                        dve.wait_ge(u["gathered"], g * 2 + 2)
                        nc.vector.tensor_copy(xg[:, 4:8, :], banks[0][:, :].rearrange("p (k n) -> p k n", k=4)
                                              ).then_inc(u["xg_hi"], 1)
                        dve.wait_ge(u["S_turned"], g + 2)
                        for j in range(2):
                            nc.vector.tensor_reduce(w_slot[SLOTS * j:SLOTS * (j + 1), :],
                                                    banks[3][SLOTS * j:SLOTS * (j + 1), T + 3 * j:T + 3 * j + 3], AX_X, ALU.add
                                                    ).then_inc(u["w_ready"], 1)
                        dve.wait_ge(u["w_ready"], g * 2 + 2)
                        dve.wait_ge(u["silu_done"], g + 1)
                        nc.vector.scalar_tensor_tensor(out=eh.rearrange("p b n -> p n b"),
                                                       in0=banks[1][:, 256:512].rearrange("p (n b) -> p n b", b=2),
                                                       scalar=w_slot, in1=sg[:, 0:256].rearrange("p (n b) -> p n b", b=2),
                                                       op0=ALU.mult, op1=ALU.mult).then_inc(u["eh_ready"], 1)
                        dve.wait_ge(u["combined"], g + 1)
                        nc.vector.tensor_copy(S, banks[3][:, 0:T]).then_inc(u["S_ready"], 1)
                        for hf in range(NH):
                            dve.wait_ge(u["y_hi"], g * 2 + hf + 1)
                            nc.vector.tensor_tensor(y[:, 1, 512 * hf:512 * hf + 512], banks[hf][:, :],
                                                    y[:, 0, 512 * hf:512 * hf + 512], ALU.subtract
                                                    ).then_inc(u[f"bank{hf}_read"], 1)
                        dve.reg_add(unit, unit, 1)
                update_x(5, routed_done, (2 * l + 1, 2 * l + 2))

            norm_root()
            dve.wait_ge(lam_exp, 1)
            step(nc.vector.tensor_tensor(nlam[:, :], lexp[:, 1:2], lexp[:, 0:1], ALU.subtract))
            step(nc.vector.tensor_scalar(nlam[:, :], nlam[:, :], -LAM_INIT, None, ALU.add))
            dve.wait_ge(rows0_in, 16 * 8)
            dve.wait_ge(ada_done, 2)
            step(nc.vector.tensor_tensor(mrow0[:, 1, :], banks[4][:, 256:512], brow0[:, 1, :], ALU.add))
            nc.vector.scalar_tensor_tensor(out=mrow0[:, 1, :], in0=mrow0[:, 1, :], scalar=1.0, in1=nrow0[:, 0, :],
                                           op0=ALU.add, op1=ALU.mult).then_inc(row0_ready, 1)
            nc.vector.tensor_tensor(mrow0[:, 0, :], banks[4][:, 0:256], brow0[:, 0, :], ALU.add).then_inc(row0_ready, 1)
            dve.wait_ge(rows0_turned, 1)
            nc.vector.tensor_copy(mod_T[:, 0, 0:2, :], banks[5][:, 0:2 * KD].rearrange("p (s k) -> p s k", s=2)
                                  ).then_inc(mod_T_in[0], 1)
            evict_hT()

            def later_rows(k):
                l, sec = LATER[k]
                if k == 0:
                    dve.wait_ge(rowsB_in, 16 * 12)
                if k == 4:
                    dve.wait_ge(rowsA_in, 16 * 8)
                bias = browA[:, sec - 2, :] if l == 0 else browB[:, sec, :]
                dve.wait_ge(ada_done, 2 + k + 1)
                ins = nc.vector.tensor_tensor(mrow[:, k, :], banks[7 * (1 - k % 2)][:, 0:256], bias, ALU.add)
                ins.then_inc(bank_rows_read, 1)
                dve.wait_ge(bank_rows_read, k + 1)
                if sec % 3 == 1:
                    gain = nrowA[:, 0, :] if l == 0 else nrowB[:, sec // 3, :]
                    nc.vector.scalar_tensor_tensor(out=mrow[:, k, :], in0=mrow[:, k, :], scalar=1.0, in1=gain,
                                                   op0=ALU.add, op1=ALU.mult).then_inc(rows_ready, 1)
                else:
                    dve.sem_inc(rows_ready, 1)

            for i in range(12):
                low_part("mix_in", 0, i)
                if i - 1 in AT_PROJ:
                    later_rows(AT_PROJ.index(i - 1))
            later_rows(3)

            def finish_a(n):
                W = P * (1 + n % 2)
                dve.wait_ge(exp_done, 2 * n + 2)
                step(nc.vector.reciprocal(soft[:, 2, n, :], soft[:, 1, n, :]))
                step(nc.vector.tensor_tensor(soft[:, 2, n, 1:2], soft[:, 2, n, 1:2], nlam[:, :], ALU.mult))
                if n >= 2:
                    dve.wait_ge(a_turned, n - 1)
                step(nc.vector.tensor_scalar(da_a[:, n % 2, 0:W], da_s[:, n % 2, 0, 0:W], soft[:, 2, n, 0:1], None, ALU.mult))
                nc.vector.scalar_tensor_tensor(out=da_a[:, n % 2, 0:W], in0=da_s[:, n % 2, 1, 0:W], scalar=soft[:, 2, n, 1:2],
                                               in1=da_a[:, n % 2, 0:W], op0=ALU.mult, op1=ALU.add).then_inc(a_ready, 1)

            def keep_o(n):
                dve.wait_ge(pv_done, n + 1)
                nc.vector.tensor_copy(da_o[:, n % 2, n // 2, :], banks[5 + n % 2][:, T:T + P]).then_inc(o_ready, 1)

            for n in range(DA_ITEMS):
                hd, qb = n // 2, n % 2
                W = P * (1 + qb)
                slope = 2.0 ** (-8.0 * (hd + 1) / DA_HEADS)
                sn = da_s[:, n % 2, :, 0:W]
                dve.wait_ge(scored, n + 1)
                if n >= 2:
                    dve.wait_ge(a_ready, n - 1)
                for m in range(2):
                    ins = nc.vector.scalar_tensor_tensor(out=sn[:, m, :], in0=dist[:, T - W:T], scalar=-8.0 * slope,
                                                         in1=banks[1 + 2 * (n % 2) + m][:, 0:W], op0=ALU.mult, op1=ALU.add)
                step(ins)
                step(nc.vector.tensor_reduce(soft[:, 0, n, :], sn, AX_X, ALU.max))
                nc.vector.tensor_scalar(soft[:, 0, n, :], soft[:, 0, n, :], -0.125, None, ALU.mult).then_inc(s_ready, 1)
                if n >= 3:
                    keep_o(n - 3)
                if n >= 1:
                    finish_a(n - 1)
                if n >= 2 and n - 2 in AT_ITEM:
                    later_rows(4 + AT_ITEM.index(n - 2))
            finish_a(DA_ITEMS - 1)
            for n in range(DA_ITEMS - 3, DA_ITEMS):
                keep_o(n)
            dve.wait_ge(o_ready, DA_ITEMS)
            dve.wait_ge(o_sumsq, DA_ITEMS)
            nc.vector.tensor_scalar(ss[:, :], ss[:, :], 1.0 / P, EPS, ALU.mult, ALU.add).then_inc(o_meansq, 1)
            dve.wait_ge(o_root, 1)
            step(nc.vector.reciprocal(rs[:, :], rs[:, :]))
            o2 = da_o.rearrange("p c h d -> p (c h) d")
            nc.vector.tensor_tensor(o2, o2, rs[:, :].unsqueeze(2).to_broadcast([P, 2 * DA_HEADS, P]), ALU.mult
                                    ).then_inc(o_normed, 1)
            later_rows(len(LATER) - 1)
            low_part("mix_out", 0, 0)
            low_part("mix_out", 0, 1)
            for m in range(4):
                dve.wait_ge(oT_hi, m + 1)
                nc.vector.tensor_tensor(oT_lo[0][:, 512 * m:512 * m + 512], oT_full_at[0][:, 512 * m:512 * m + 512],
                                        da_oT[:, 512 * m:512 * m + 512], ALU.subtract).then_inc(oT_split, 1)
            low_part("mix_out", 0, 2)
            low_part("mix_out", 0, 3)
            dve.wait_ge(rows_stored, 192)
            dve.wait_ge(gate_and_moe_mods, 64)
            update_x(2, out_done, (4, 4))
            moe(0)

            norm_root()
            evict_hT()
            for i in range(24):
                low_part("mix_in", 1, i)
            dve.wait_ge(decay_ready, 1)
            for hd in range(RET_HEADS):
                dve.wait_ge(scored, DA_ITEMS + hd + 1)
                if hd >= 1:
                    dve.wait_ge(pv_done, DA_ITEMS + 2 * hd)
                nc.vector.scalar_tensor_tensor(out=ret_s[:, 0:T], in0=banks[hd % 2][:, 0:T], scalar=RET_DK ** -0.5,
                                               in1=decay[:, hd, :], op0=ALU.mult, op1=ALU.mult)
                nc.vector.scalar_tensor_tensor(out=ret_s[:, T:T + P], in0=banks[hd % 2][:, T:T + P], scalar=RET_DK ** -0.5,
                                               in1=decay[:, hd, 0:P], op0=ALU.mult, op1=ALU.mult).then_inc(s_ready, 1)
            dve.wait_ge(o_sumsq, DA_ITEMS + 2 * RET_HEADS)
            nc.vector.tensor_scalar(ss[:, 0:8], ss[:, 0:8], 1.0 / 512, EPS, ALU.mult, ALU.add).then_inc(o_meansq, 1)
            dve.wait_ge(o_root, 2)
            step(nc.vector.reciprocal(rs[:, 0:8], rs[:, 0:8]))
            dve.wait_ge(o_ready, DA_ITEMS + 2 * RET_HEADS)
            for n in range(2 * RET_HEADS):
                ins = nc.vector.tensor_scalar(ret_o[:, n % 2, n // 2, :], ret_o[:, n % 2, n // 2, :], rs[:, n:n + 1], None, ALU.mult)
            ins.then_inc(o_normed, 1)
            for ch in range(16):
                dve.wait_ge(o_turned, 4 + ch // 2 + 1)
                nc.vector.scalar_tensor_tensor(out=oT_full_at[1][:, T * ch:T * ch + T],
                                               in0=banks[(ch // 2) % 4][:, T * (ch % 2):T * (ch % 2) + T],
                                               scalar=gn[:, ch:ch + 1], in1=ret_sg[:, ch, :], op0=ALU.mult, op1=ALU.mult
                                               ).then_inc(oT_full, 1)
                if ch % 4 == 3:
                    g = ch // 4
                    if g == 0:
                        low_part("mix_out", 1, 0)
                    dve.wait_ge(oT_hi, 4 + g + 1)
                    nc.vector.tensor_tensor(oT_lo[1][:, 1024 * g:1024 * g + 1024],
                                            oT_full_at[1][:, 1024 * g:1024 * g + 1024], ret_yT[:, 1024 * g:1024 * g + 1024],
                                            ALU.subtract).then_inc(oT_split, 1)
            for i in range(1, 8):
                low_part("mix_out", 1, i)
            dve.wait_ge(gate1_in, 16)
            update_x(2, out_done, (12, 12))
            moe(1)
            norm_root(last=True)
            dve.wait_ge(last_gain, 16)
            for tc in range(TC):
                nc.vector.scalar_tensor_tensor(out=h[:, tc, :], in0=X[:, tc, :], scalar=rs[:, tc:tc + 1], in1=gains[:, 2, :],
                                               op0=ALU.mult, op1=ALU.mult).then_inc(h_ready, 1)


_INS = ["x", "c", "norm_mix", "norm_ffn", "ada_w", "ada_b", "da_w_in", "da_w_out", "da_lq1", "da_lk1", "da_lq2",
        "da_lk2", "da_subln", "ret_w_in", "ret_w_out", "ret_gn", "router_w", "router_b", "exp_w1", "exp_w3",
        "exp_w2", "sh_w1", "sh_w3", "sh_w2", "final_norm"]
_OUTS = [((1, 256, 1024), "float32")]


def kernel(**inputs):
    import numpy as _np
    import concourse.bacc as _bacc
    from concourse import mybir as _mybir
    from concourse.bass_utils import run_bass_kernel_spmd as _run

    nc = _bacc.Bacc("TRN2", target_bir_lowering=False, num_devices=1)
    arrays, args = {}, []
    for name in _INS:
        a = _np.ascontiguousarray(inputs[name])
        arrays[f"in_{name}_dram"] = a
        args.append(nc.dram_tensor(f"in_{name}_dram", a.shape, _mybir.dt.from_np(a.dtype), kind="ExternalInput").ap())
    for i, (shape, dtype) in enumerate(_OUTS):
        dt = _mybir.dt.from_np(_np.dtype(dtype))
        args.append(nc.dram_tensor(f"out_{i}_dram", shape, dt, kind="ExternalOutput").ap())
    trunk(nc, *args)
    r = _run(nc, [arrays], core_ids=[0])
    got = tuple(r.results[0][f"out_{i}_dram"] for i in range(len(_OUTS)))
    return got[0]
```
